# Optimizing a Trainium2 kernel written in Bass

```python
import math
import jax, jax.numpy as jnp
from jax import lax
import numpy as np

D_MODEL = 1024
BATCH = 1
SEQ = 256
DEPTH = 2

CHUNK = 64
QBLOCK = 128
N_BRANCH = 4
HEAD_DIM = 64
BRANCH_WIDTH = 4 * HEAD_DIM

A_HEADS = 4
A_KV_HEADS = 2
A_GROUP = A_HEADS // A_KV_HEADS
WINDOW = 128
WINDOW_CHUNKS = WINDOW // CHUNK
B_HEADS = 4
B_DK = 64
B_DV = 64
C_HEADS = 4
C_Q_LORA = 256
C_KV_LORA = 128
C_NOPE = 64
C_ROPE = 32
C_V = 64
ROPE_THETA = 10000.0
D_HEADS = 4
D_FF = ((-(-8 * D_MODEL // 3)) + 255) // 256 * 256
EPS = 1e-6

SPLITS = (
    A_HEADS * HEAD_DIM, A_KV_HEADS * HEAD_DIM, A_KV_HEADS * HEAD_DIM,
    B_HEADS * B_DK, B_HEADS * B_DK, B_HEADS * B_DV, B_HEADS * B_DV,
    C_Q_LORA, C_KV_LORA, C_ROPE,
    D_HEADS * HEAD_DIM, D_HEADS * HEAD_DIM, D_HEADS * HEAD_DIM, D_HEADS,
    N_BRANCH * D_MODEL,
)
N_IN = sum(SPLITS)

kernel_name = "hybrid_parallel_gated_streaming_trunk"

def rms_norm(x, g):
    xf = x.astype(jnp.float32)
    y = xf * lax.rsqrt(jnp.mean(xf * xf, axis=-1, keepdims=True) + EPS)
    return (y * g.astype(jnp.float32)).astype(x.dtype)

def rope(x, pos):
    half = x.shape[-1] // 2
    inv = jnp.exp(-math.log(ROPE_THETA) * jnp.arange(half, dtype=jnp.float32) / half)
    ang = pos.astype(jnp.float32)[:, None] * inv[None, :]
    cos = jnp.cos(ang)[None, :, None, :]
    sin = jnp.sin(ang)[None, :, None, :]
    xf = x.astype(jnp.float32)
    x1, x2 = xf[..., :half], xf[..., half:]
    return jnp.concatenate([x1 * cos - x2 * sin, x2 * cos + x1 * sin], axis=-1).astype(x.dtype)

def window_sink_attention(q, k, v, sinks):
    b, s, _, dh = q.shape
    nc = s // CHUNK
    qc = q.reshape(b, nc, CHUNK, A_KV_HEADS, A_GROUP, dh)

    def window(t):
        tc = t.reshape(b, nc, CHUNK, A_KV_HEADS, dh)
        parts = [jnp.pad(tc, ((0, 0), (j, 0), (0, 0), (0, 0), (0, 0)))[:, :nc]
                 for j in range(WINDOW_CHUNKS - 1, -1, -1)]
        return jnp.concatenate(parts, axis=2)

    kw, vw = window(k), window(v)
    scores = jnp.einsum('bcqkgd,bcskd->bckgqs', qc, kw,
                        preferred_element_type=jnp.float32) * (dh ** -0.5)
    key_chunk_offset = jnp.arange(WINDOW) // CHUNK - (WINDOW_CHUNKS - 1)
    valid = (jnp.arange(nc)[:, None] + key_chunk_offset[None, :]) >= 0
    scores = jnp.where(valid[None, :, None, None, None, :], scores, -jnp.inf)
    sink = sinks.astype(jnp.float32).reshape(1, 1, A_KV_HEADS, A_GROUP, 1, 1)
    m = jnp.maximum(jnp.max(scores, axis=-1, keepdims=True), sink)
    p = jnp.exp(scores - m)
    denom = jnp.sum(p, axis=-1, keepdims=True) + jnp.exp(sink - m)
    out = jnp.einsum('bckgqs,bcskd->bcqkgd', (p / denom).astype(v.dtype), vw)
    return out.reshape(b, s, A_HEADS * dh)

def hgrn2_recurrence(q, f_logit, i, lb):
    b, s, _ = q.shape
    nc = s // CHUNK
    lb = lb.astype(jnp.float32)
    f = lb + (1.0 - lb) * jax.nn.sigmoid(f_logit.astype(jnp.float32))
    log_f = jnp.log(f)
    k = 1.0 - f
    qf = jax.nn.silu(q.astype(jnp.float32))
    vf = i.astype(jnp.float32)

    def to_chunks(t, d):
        return t.reshape(b, nc, CHUNK, B_HEADS, d).transpose(1, 0, 3, 2, 4)

    xs = (to_chunks(qf, B_DK), to_chunks(k, B_DK), to_chunks(vf, B_DV), to_chunks(log_f, B_DK))
    causal = jnp.tril(jnp.ones((CHUNK, CHUNK), dtype=bool))

    def step(state, inp):
        qc, kc, vc, lc = inp
        bcum = jnp.cumsum(lc, axis=2)
        diff = bcum[:, :, :, None, :] - bcum[:, :, None, :, :]
        decay = jnp.exp(jnp.where(causal[:, :, None], diff, -jnp.inf))
        attn = jnp.einsum('bhtsk,bhsk->bhts', decay * qc[:, :, :, None, :], kc)
        o = (jnp.einsum('bhts,bhsv->bhtv', attn, vc)
             + jnp.einsum('bhtk,bhkv->bhtv', qc * jnp.exp(bcum), state))
        blast = bcum[:, :, -1:, :]
        state = (jnp.exp(blast[:, :, 0, :])[..., None] * state
                 + jnp.einsum('bhsk,bhsv->bhkv', kc * jnp.exp(blast - bcum), vc))
        return state, o

    s0 = jnp.zeros((b, B_HEADS, B_DK, B_DV), jnp.float32)
    _, o = lax.scan(step, s0, xs)
    return o.transpose(1, 0, 3, 2, 4).reshape(b, s, B_HEADS, B_DV)

def sweep_attention(q, k, v, bias_fn):
    b, s, h, dq = q.shape
    nb = s // QBLOCK
    scale = dq ** -0.5
    kpos = jnp.arange(s)
    qb = q.reshape(b, nb, QBLOCK, h, dq).swapaxes(0, 1)

    def body(args):
        q_blk, blk = args
        qpos = blk * QBLOCK + jnp.arange(QBLOCK)
        scores = jnp.einsum('bqhd,bshd->bhqs', q_blk, k,
                            preferred_element_type=jnp.float32) * scale
        p = jax.nn.softmax(bias_fn(scores, qpos, kpos), axis=-1)
        return jnp.einsum('bhqs,bshd->bqhd', p.astype(v.dtype), v)

    out = lax.map(body, (qb, jnp.arange(nb)))
    return out.swapaxes(0, 1).reshape(b, s, h * v.shape[-1])

def chunk_causal_bias(scores, qpos, kpos):
    ok = (kpos // CHUNK)[None, :] <= (qpos // CHUNK)[:, None]
    return jnp.where(ok, scores, -jnp.inf)

def mla_attention(cq, ckv, kr, cq_g, ckv_g, w_uq, w_ukv, qn_g, kn_g, pos):
    b, s, _ = cq.shape
    q = (rms_norm(cq, cq_g) @ w_uq).reshape(b, s, C_HEADS, C_NOPE + C_ROPE)
    kv = (rms_norm(ckv, ckv_g) @ w_ukv).reshape(b, s, C_HEADS, C_NOPE + C_V)
    k = jnp.concatenate([kv[..., :C_NOPE],
                         jnp.broadcast_to(kr[:, :, None, :], (b, s, C_HEADS, C_ROPE))], axis=-1)
    v = kv[..., C_NOPE:]
    q = rms_norm(q, qn_g)
    k = rms_norm(k, kn_g)
    q = jnp.concatenate([q[..., :C_NOPE], rope(q[..., C_NOPE:], pos)], axis=-1)
    k = jnp.concatenate([k[..., :C_NOPE], rope(k[..., C_NOPE:], pos)], axis=-1)
    return sweep_attention(q, k, v, chunk_causal_bias)

def forgetting_attention(q, k, v, f_logit, f_bias):
    log_f = jax.nn.log_sigmoid(f_logit.astype(jnp.float32) + f_bias.astype(jnp.float32))
    fcum = jnp.cumsum(log_f, axis=1).transpose(0, 2, 1)

    def fox_bias(scores, qpos, kpos):
        fq = lax.dynamic_slice_in_dim(fcum, qpos[0], QBLOCK, axis=2)
        logits = scores + fq[..., :, None] - fcum[:, :, None, :]
        return jnp.where(kpos[None, :] <= qpos[:, None], logits, -jnp.inf)

    return sweep_attention(q, k, v, fox_bias)

def setup_inputs(seed: int = 0) -> dict:
    key = jax.random.key(seed)
    ks = jax.random.split(key, 24)
    L = DEPTH

    def w(k, shape, fan_in):
        return jax.random.normal(k, shape, jnp.float32) * (fan_in ** -0.5)

    def gain(k, shape):
        return 1.0 + 0.02 * jax.random.normal(k, shape, jnp.float32)

    return {
        "x": jax.random.normal(ks[0], (BATCH, SEQ, D_MODEL), jnp.float32),
        "norm_mix_g": gain(ks[1], (L, D_MODEL)),
        "norm_ffn_g": gain(ks[2], (L, D_MODEL)),
        "w_in": w(ks[3], (L, D_MODEL, N_IN), D_MODEL),
        "a_q_norm_g": gain(ks[4], (L, HEAD_DIM)),
        "a_k_norm_g": gain(ks[5], (L, HEAD_DIM)),
        "a_sinks": 0.5 * jax.random.normal(ks[6], (L, A_HEADS), jnp.float32),
        "hgrn_lb_logits": 0.1 * jax.random.normal(ks[7], (L, B_HEADS * B_DK), jnp.float32),
        "b_o_norm_g": gain(ks[8], (L, B_DV)),
        "c_cq_norm_g": gain(ks[9], (L, C_Q_LORA)),
        "c_ckv_norm_g": gain(ks[10], (L, C_KV_LORA)),
        "c_w_uq": w(ks[11], (L, C_Q_LORA, C_HEADS * (C_NOPE + C_ROPE)), C_Q_LORA),
        "c_w_ukv": w(ks[12], (L, C_KV_LORA, C_HEADS * (C_NOPE + C_V)), C_KV_LORA),
        "c_q_norm_g": gain(ks[13], (L, C_NOPE + C_ROPE)),
        "c_k_norm_g": gain(ks[14], (L, C_NOPE + C_ROPE)),
        "d_q_norm_g": gain(ks[15], (L, HEAD_DIM)),
        "d_k_norm_g": gain(ks[16], (L, HEAD_DIM)),
        "d_f_bias": 0.1 * jax.random.normal(ks[17], (L, D_HEADS), jnp.float32),
        "w_branch": w(ks[18], (L, N_BRANCH, BRANCH_WIDTH, D_MODEL), BRANCH_WIDTH),
        "w_out": w(ks[19], (L, D_MODEL, D_MODEL), D_MODEL),
        "w_ffn_in": w(ks[20], (L, D_MODEL, 2 * D_FF), D_MODEL),
        "w_ffn_out": w(ks[21], (L, D_FF, D_MODEL), D_FF),
    }

def reference(x, norm_mix_g, norm_ffn_g, w_in, a_q_norm_g, a_k_norm_g, a_sinks,
              hgrn_lb_logits, b_o_norm_g, c_cq_norm_g, c_ckv_norm_g, c_w_uq, c_w_ukv,
              c_q_norm_g, c_k_norm_g, d_q_norm_g, d_k_norm_g, d_f_bias,
              w_branch, w_out, w_ffn_in, w_ffn_out):
    b, s, _ = x.shape
    pos = jnp.arange(s)
    split_points = np.cumsum(SPLITS)[:-1].tolist()
    lb_soft = jax.nn.softmax(hgrn_lb_logits.astype(jnp.float32), axis=0)
    lower_bounds = jnp.cumsum(lb_soft, axis=0) - lb_soft[0:1]

    for l in range(DEPTH):
        h = rms_norm(x, norm_mix_g[l])
        (a_q, a_k, a_v, b_q, b_f, b_i, b_g, c_cq, c_ckv, c_kr,
         d_q, d_k, d_v, d_f, gate_logits) = jnp.split(h @ w_in[l], split_points, axis=-1)

        qa = rms_norm(a_q.reshape(b, s, A_HEADS, HEAD_DIM), a_q_norm_g[l])
        ka = rms_norm(a_k.reshape(b, s, A_KV_HEADS, HEAD_DIM), a_k_norm_g[l])
        va = a_v.reshape(b, s, A_KV_HEADS, HEAD_DIM)
        y_a = window_sink_attention(qa, ka, va, a_sinks[l])

        o_b = hgrn2_recurrence(b_q, b_f, b_i, lower_bounds[l])
        y_b = (rms_norm(o_b, b_o_norm_g[l]).reshape(b, s, B_HEADS * B_DV)
               * jax.nn.silu(b_g.astype(jnp.float32))).astype(x.dtype)

        y_c = mla_attention(c_cq, c_ckv, c_kr, c_cq_norm_g[l], c_ckv_norm_g[l],
                            c_w_uq[l], c_w_ukv[l], c_q_norm_g[l], c_k_norm_g[l], pos)

        qd = rms_norm(d_q.reshape(b, s, D_HEADS, HEAD_DIM), d_q_norm_g[l])
        kd = rms_norm(d_k.reshape(b, s, D_HEADS, HEAD_DIM), d_k_norm_g[l])
        vd = d_v.reshape(b, s, D_HEADS, HEAD_DIM)
        y_d = forgetting_attention(qd, kd, vd, d_f, d_f_bias[l])

        gates = jax.nn.sigmoid(gate_logits.astype(jnp.float32)).astype(x.dtype)
        gates = gates.reshape(b, s, N_BRANCH, D_MODEL)
        merged = jnp.zeros_like(x)
        for n, y in enumerate((y_a, y_b, y_c, y_d)):
            merged = merged + gates[:, :, n] * (y @ w_branch[l, n])
        x = x + merged @ w_out[l]

        h = rms_norm(x, norm_ffn_g[l])
        g, u = jnp.split(h @ w_ffn_in[l], 2, axis=-1)
        x = x + (jax.nn.silu(g) * u) @ w_ffn_out[l]
    return x


_drawn_inputs = setup_inputs


def setup_inputs(seed=0):
    import zlib

    import numpy as np

    out = dict(_drawn_inputs(seed))
    spreads = {}
    factors = {'norm_mix_g': 2.718,
     'norm_ffn_g': 2.85,
     'a_q_norm_g': 8.0,
     'a_k_norm_g': 8.0,
     'a_sinks': 8.0,
     'hgrn_lb_logits': 8.0,
     'b_o_norm_g': 5.891,
     'c_cq_norm_g': 8.0,
     'c_ckv_norm_g': 8.0,
     'c_q_norm_g': 8.0,
     'c_k_norm_g': 8.0,
     'd_q_norm_g': 8.0,
     'd_k_norm_g': 8.0,
     'd_f_bias': 7.725}
    for name, (base, spread) in spreads.items():
        noise = np.random.default_rng([zlib.crc32(name.encode()), seed]).standard_normal(out[name].shape)
        drawn = base * np.exp(spread * noise) if base else spread * noise
        out[name] = __import__('jax').numpy.asarray(drawn.astype(out[name].dtype))
    for name, factor in factors.items():
        out[name] = (out[name] * factor).astype(out[name].dtype)
    return out
```

```python
from contextlib import ExitStack

import concourse.bass as bass
from concourse import mybir

F32 = mybir.dt.float32
F32R = mybir.dt.float32r
BF16 = mybir.dt.bfloat16
U8 = mybir.dt.uint8
ALU = mybir.AluOpType
ACT = mybir.ActivationFunctionType
AX = mybir.AxisListType

P = 128
SEQ = 256
T = SEQ // P
D = 1024
DK = D // P
DEPTH = 2
CHUNK = 64
H = 4
HD = 64
A_KV = 2
C_Q, C_KV, C_ROPE, C_DQ = 256, 128, 32, 96
D_FF = 2816
FFN_BLOCKS = D_FF // 256
FF_TILES = D_FF // P
BW = H * HD
EPS = 1e-6
NEG = -1e30

OFF_A, OFF_B, OFF_C, OFF_D, OFF_G = 0, 512, 1536, 1952, 2724
Z_BLOCKS = [
    (OFF_B, 512),
    (OFF_D + 512, 260),
    (OFF_B + 512, 512),
    (OFF_D, 512),
    (OFF_A, 512),
    (OFF_C, 416),
]
BR_A, BR_B, BR_C, BR_D = 0, 1, 2, 3
MERGE_ORDER = [BR_B, BR_D, BR_A, BR_C]

CW = 2048
Z0 = 0
GATE0 = [12, 16, 23, 28]
UQ, UKV = 20, 21
PROJ = [22, 27, 32, 33]
OUT0 = 34
FFN0 = 38
DOWN0 = FFN0 + 2 * FFN_BLOCKS
DOWN_CHUNKS = -(-FF_TILES // 4)
CHUNKS = DOWN0 + 2 * DOWN_CHUNKS
RAW, RING = 2, 4
assert CHUNKS % RING == 0 and FFN_BLOCKS % 2 == 1 and (FFN0 + 2) % RING == 0

PAR_COLS = [("mix", DK), ("ffn", DK), ("cq", 2), ("ckv", 1), ("aq", 1), ("ak", 1), ("dq", 1), ("dk", 1),
            ("lb", 2), ("bo", HD), ("cqn", C_DQ), ("ckn", C_DQ), ("sink", H), ("fb", H)]
DERIVED = [("low", 2), ("oml", 2), ("ga", 1), ("gd", 1)]


def columns(spec):
    first, out = 0, {}
    for name, n in spec:
        out[name] = (first, n)
        first += n
    return out, first


PAR, PAR_IN = columns(PAR_COLS)
PARX, PAR_N = columns(PAR_COLS + DERIVED)

CONST, CONST_N = columns([("ident", P), ("tri", P), ("stri", P), ("ones", P), ("cos", T * C_ROPE), ("sin", T * C_ROPE),
                          ("half", 16)])
MASKS, MASK_N = columns([("ident", P), ("causal", P), ("chunk", P), ("window", P)])
LEVELS = 7

NORM1, NORM_D, NORM_A, NORM_C1, NORM_B, NORM_C2, NORM2 = range(7)
NORM_WIDTH = [T, 16, 12, 2 * T, 8, 16, T]
NORM_AT = [sum(NORM_WIDTH[:i]) for i in range(7)]
NORM_N = sum(NORM_WIDTH)


PT_DONE = [1, 3, 4, 6, 7, 9]
LINKS = 50


def width(c):
    if c < 2 * len(Z_BLOCKS):
        return 4 * Z_BLOCKS[c // 2][1]
    if c == UQ:
        return 2 * H * C_DQ
    if c == UKV:
        return H * 2 * HD
    if c >= DOWN0 and (c - DOWN0) % DOWN_CHUNKS == DOWN_CHUNKS - 1:
        return (FF_TILES - 4 * (DOWN_CHUNKS - 1)) * 512
    return CW


SIGNALS = dict(
    hi=CHUNKS, lo=CHUNKS, mm=CHUNKS, par=1, dve=LINKS,
    sumsq=2 * T, mean=7, rstd=7, xn=2 * T,
    xT=12, xT_hi=12, xT_lo=12,
    z=T * len(Z_BLOCKS), gate=4 * 2 * T, u=2 * T, merge=4 * 2 * T, xmid=2 * T, xout=2 * T,
    b_in=2, b_e=1, b_tq=1, b_f=1, b_q=1, b_ln=1, b_scan=1, b_d=LEVELS, b_abs=LEVELS, b_E=LEVELS,
    b_QK=LEVELS + 1, b_lev=2 * (LEVELS + 1), b_at=2 * (LEVELS + 1), b_Ex=1, b_cross=2, b_atx=2, b_o=1, b_sq=1, b_tg=1,
    b_y=1,
    d_zf=1, d_abs=1, d_e=1, d_ln=1, d_lf=1, d_x=1, ad_sq=2, ad_n=2, ad_T=4, ad_sb=4,
    c_sq=1, c_n=1, c_T=2, c_hi=1, c_lo=1, c_sq2=1, c_n2=1, c_T2=4, c_sb2=4,
    score=6, top=6, prob=6, pT=9, pT_sb=9, pv=6, y=6, yT=4, yT_hi=4, yT_lo=4,
    tanh=2 * FFN_BLOCKS, act=2 * FFN_BLOCKS, sw=FFN_BLOCKS, aT=FFN_BLOCKS, aT_hi=FFN_BLOCKS, aT_lo=FFN_BLOCKS,
)


HEADS = dict(mm=RING, xout=1, act=1, aT=1, aT_lo=1)


def at(name, layer, k):
    return layer * SIGNALS[name] + ((HEADS[name] if name in HEADS else 0) + k)


def trunk(nc, x_in, stream, par_in, const_in, mask_in, level_in, out):
    ctx = ExitStack()
    with ctx:
        def sb(name, shape, dt=F32):
            return ctx.enter_context(nc.sbuf_tensor(name, shape, dt))

        def new_sem(name):
            return ctx.enter_context(nc.semaphore(name))

        x = sb("x", [P, T, D])
        xT_hi = sb("xT_hi", [P, T, DK, P], F32R)
        xT_lo = sb("xT_lo", [P, T, DK, P], F32R)
        raw = sb("raw", [P, RAW, CW])
        w_hi = sb("w_hi", [P, RING, CW], F32R)
        w_lo = sb("w_lo", [P, RING, CW], F32R)
        par = sb("par", [P, DEPTH, PAR_N])
        now = sb("now", [P, PAR_N])
        const = sb("const", [P, CONST_N])
        mask = sb("mask", [P, MASK_N], BF16)
        level = sb("level", [P, LEVELS, P], U8)
        stat = sb("stat", [P, 3, NORM_N])
        small = sb("small", [P, 128])
        dsm = sb("dsm", [P, 5, 2 * H])

        with ExitStack() as attention:
            gates = attention.enter_context(nc.sbuf_tensor("gates", [P, 2, T, D], F32))
            yT_hi = attention.enter_context(nc.sbuf_tensor("yT_hi", [P, 2, 2, T, P], F32R))
            yT_lo = attention.enter_context(nc.sbuf_tensor("yT_lo", [P, 2, 2, T, P], F32R))
            cT_hi = attention.enter_context(nc.sbuf_tensor("cT_hi", [P, 3, T, P], F32R))
            cT_lo = attention.enter_context(nc.sbuf_tensor("cT_lo", [P, 3, T, P], F32R))
            AREA = [("wide", 2 * D), ("zqf", 1024), ("zdv", T * 260), ("zc", T * 416), ("qkT", 2048), ("prob", 1024),
                    ("pT", 1024), ("y", 1024), ("kdup", 512), ("X", 1024), ("b", 4608)]
            area, area_n = columns(AREA)
            arena = attention.enter_context(nc.sbuf_tensor("arena", [P, area_n], F32))
        with ExitStack() as ffn:
            keep_x_normed = ffn.enter_context(nc.sbuf_tensor("keep_gates", [P, 2, T, D], F32))
            aT_hi = ffn.enter_context(nc.sbuf_tensor("aT_hi", [P, FF_TILES * SEQ], F32R))
            aT_lo = ffn.enter_context(nc.sbuf_tensor("aT_lo", [P, FF_TILES * SEQ], F32R))
        del keep_x_normed

        def region(name, first=0, n=None):
            col, size = area[name]
            return arena[:, col + first:col + (size if n is None else first + n)]

        wide = region("wide")
        xn = wide.rearrange("p (t d) -> p t d", t=T)
        merged = xn
        z_ig = region("wide", 0, 1024).rearrange("p (t c) -> p t c", t=T)
        z_dqk = region("wide", 1024, 1024).rearrange("p (t c) -> p t c", t=T)
        z_qf = region("zqf").rearrange("p (t c) -> p t c", t=T)
        z_a = z_qf
        z_dv = region("zdv").rearrange("p (t c) -> p t c", t=T)
        z_c = region("zc").rearrange("p (t c) -> p t c", t=T)
        z_of = [z_qf, z_dv, z_ig, z_dqk, z_a, z_c]
        prob = region("prob").rearrange("p (h k s) -> p h k s", k=T, h=H)
        pT = region("pT").rearrange("p (k h s) -> p k h s", k=T, h=H)
        y = region("y").rearrange("p (b t c) -> p b t c", b=2, t=T)
        kdup = region("kdup").rearrange("p (t c) -> p t c", t=T)
        X = region("X").rearrange("p (t h s) -> p t h s", t=T, h=H)
        bq, bk, bT, bE, bQ, bK = (region("b", 512 * i, 512) for i in range(6))
        AT = [region("b", 3072 + 512 * i, 512).rearrange("p (h s) -> p h s", h=H) for i in range(3)]
        c_q = region("b", 0, 768).rearrange("p (g c) -> p g c", c=C_DQ)
        c_k = region("b", 768, 768).rearrange("p (g c) -> p g c", c=C_DQ)
        c_kv = region("b", 1536, 1024).rearrange("p (g c) -> p g c", c=2 * HD)
        c_s = region("b", 2560, 768)
        c_s2 = region("b", 3328, 512)
        c_r = region("b", 3840, 512)
        square = region("prob")
        junk = region("y", 0, 768)

        act = gates[:, 0, :, :].rearrange("p a b -> p (a b)")[:, 0:1024].rearrange("p (b t c) -> p b t c", b=2, t=T)
        sw = gates[:, 1, :, :].rearrange("p a b -> p (a b)")[:, 0:1024].rearrange("p (b t c) -> p b t c", b=2, t=T)

        acc = ctx.enter_context(nc.psum_tensor("acc", [P, 4, 512], F32))
        wk = ctx.enter_context(nc.psum_tensor("wk", [P, 4, 512], F32))

        raw_loaded = [new_sem(f"raw_loaded{i}") for i in range(RAW)]
        loaded = {n: new_sem(f"loaded_{n}") for n in ("x", "par", "const", "mask", "level")}
        stored = new_sem("stored")
        setup = new_sem("setup")
        sem = {n: new_sem(f"s_{n}") for n in SIGNALS}

        def p_(name):
            col, n = PARX[name]
            return now[:, col:col + n]

        def c_(name, rows=P):
            col, n = CONST[name]
            return const[0:rows, col:col + n]

        def m_(name):
            col, n = MASKS[name]
            return mask[:, col:col + n]

        def norm(which, row):
            return stat[:, row, NORM_AT[which]:NORM_AT[which] + NORM_WIDTH[which]]

        mx, negm, rowsum, rden, esink = (small[:, 24 * i:24 * i + 24] for i in range(5))
        lf = dsm[:, 0, :]

        block = ctx.enter_context(nc.Block())

        @block.sync
        def _(sp):
            for slot in range(RAW):
                sp.dma_start(raw[:, slot, :], stream[slot]).then_inc(raw_loaded[slot], 16)
                if slot == 0:
                    sp.dma_start(x[:, :, :], x_in).then_inc(loaded["x"], 16)
            with sp.Fori(0, DEPTH * CHUNKS // RAW - 1) as i:
                for slot in range(RAW):
                    sp.wait_ge(sem["lo"], i * RAW + (slot + 1))
                    sp.dma_start(raw[:, slot, :],
                                 stream[bass.ds(i * RAW + (RAW + slot), 1), :, :].rearrange("a p n -> (a p) n"))\
                        .then_inc(raw_loaded[slot], 16)
            sp.wait_ge(sem["xout"], at("xout", DEPTH - 1, 2 * T))
            sp.dma_start(out, x[:, :, :]).then_inc(stored, 16)
            sp.wait_ge(stored, 16)

        @block.gpsimd
        def _(pool):
            pool.wait_ge(loaded["const"], 16)
            with pool.Fori(0, DEPTH) as l:
                for which in range(7):
                    pool.wait_ge(sem["mean"], at("mean", l, which + 1))
                    nc.gpsimd.tensor_tensor(norm(which, 2), norm(which, 1), c_("half")[:, 0:NORM_WIDTH[which]],
                                            ALU.pow).then_inc(sem["rstd"], 1)

        @block.scalar
        def _(act_e):
            e = act_e
            e.dma_start(const[:, :], const_in).then_inc(loaded["const"], 16)
            e.dma_start(par[:, :, 0:PAR_IN], par_in).then_inc(loaded["par"], 16)
            e.dma_start(arena[:, 0:MASK_N], mask_in).then_inc(loaded["mask"], 16)
            e.dma_start(arena[:, MASK_N:MASK_N + LEVELS * P], level_in).then_inc(loaded["level"], 16)
            e.wait_ge(setup, 2)
            nc.scalar.activation(small[:, 8:12], small[:, 4:8], ACT.Exp).then_inc(setup, 1)

            with e.Fori(0, DEPTH) as l:
                split = [0]

                def split_chunk(c):
                    e.wait_ge(sem["mm"], at("mm", l, c - (RING - 1)))
                    e.wait_ge(raw_loaded[c % RAW], (l * (CHUNKS // RAW) + (c // RAW + 1)) * 16)
                    n = width(c)
                    nc.scalar.activation(w_hi[:, c % RING, 0:n], raw[:, c % RAW, 0:n], ACT.Copy).then_inc(sem["hi"], 1)

                def split_to(p):
                    while split[0] < min(p + RING, CHUNKS):
                        split_chunk(split[0])
                        split[0] += 1

                def transpose_hi(first, gain):
                    for n in range(4):
                        e.wait_ge(sem["xT"], at("xT", l, first + n + 1))
                        t, h = n // 2, n % 2
                        if gain is None:
                            nc.scalar.activation(xT_hi[:, t, 4 * h:4 * h + 4, :].rearrange("p k s -> p (k s)"),
                                                 wk[:, n, :], ACT.Copy, scale=0.5).then_inc(sem["xT_hi"], 1)
                            continue
                        for k in range(4):
                            i = nc.scalar.activation(xT_hi[:, t, 4 * h + k, :], wk[:, n, k * P:(k + 1) * P], ACT.Copy,
                                                     scale=p_(gain)[:, 4 * h + k:4 * h + k + 1])
                        i.then_inc(sem["xT_hi"], 1)

                def evacuate_z(b):
                    e.wait_ge(sem["mm"], at("mm", l, 2 * b + 2))
                    for t in range(T):
                        n = Z_BLOCKS[b][1]
                        nc.scalar.activation(z_of[b][:, t, 0:n], acc[:, 2 * (b % 2) + t, 0:n], ACT.Copy)\
                            .then_inc(sem["z"], 1)

                def gate_tanh(g):
                    branch, half = g // 2, g % 2
                    e.wait_ge(sem["mm"], at("mm", l, GATE0[branch] + 2 * half + 2))
                    if branch >= 2:
                        e.wait_ge(sem["merge"], at("merge", l, 4 * (branch - 1)))
                    for t in range(T):
                        nc.scalar.activation(gates[:, branch % 2, t, half * 512:half * 512 + 512],
                                             acc[:, 2 * half + t, :], ACT.Tanh, scale=0.5).then_inc(sem["gate"], 1)

                def exps(u, scale):
                    t = u % 2
                    e.wait_ge(sem["top"], at("top", l, u + 1))
                    if u:
                        e.wait_ge(sem["pT"], at("pT", l, PT_DONE[u - 1]))
                    if u // 2 == 1:
                        c = slice(4 * u, 4 * u + 4)
                        nc.scalar.activation(esink[:, c], esink[:, c], ACT.Exp)
                    for h in range(H):
                        col = (h // 2) * SEQ
                        i = nc.scalar.activation(prob[:, h, 0:t + 1, :].rearrange("p k s -> p (k s)"),
                                                 wk[:, h % 2, col:col + (t + 1) * P], ACT.Exp,
                                                 bias=negm[:, 4 * u + h:4 * u + h + 1], scale=scale,
                                                 accum_out=rowsum[:, 4 * u + h:4 * u + h + 1])
                    i.then_inc(sem["prob"], 1)

                def pT_copy(u):
                    if u:
                        e.wait_ge(sem["pv"], at("pv", l, u))
                    for k in range(u % 2 + 1):
                        n = (PT_DONE[u - 1] if u else 0) + k + 1
                        e.wait_ge(sem["pT"], at("pT", l, n))
                        nc.scalar.activation(pT[:, k, :, :].rearrange("p h s -> p (h s)"), wk[:, 2 + k, :], ACT.Copy)\
                            .then_inc(sem["pT_sb"], 1)

                def yT_hi_copy(n):
                    e.wait_ge(sem["yT"], at("yT", l, n + 1))
                    if n >= 2:
                        e.wait_ge(sem["mm"], at("mm", l, PROJ[n - 2] + 1))
                    nc.scalar.activation(yT_hi[:, n % 2].rearrange("p c t s -> p (c t s)"), wk[:, 2, :], ACT.Copy)\
                        .then_inc(sem["yT_hi"], 1)

                def squares(first):
                    for t in range(T):
                        nc.scalar.activation(xn[:, t, :], x[:, t, :], ACT.Square,
                                             accum_out=norm(first, 0)[:, t:t + 1]).then_inc(sem["sumsq"], 1)

                e.wait_ge(loaded["x"], 16)
                e.wait_ge(setup, 7)
                e.wait_ge(sem["xout"], at("xout", l, 0))
                squares(NORM1)
                split_chunk(0)
                split_chunk(1)
                split[0] = 2
                e.wait_ge(sem["par"], at("par", l, 1))
                transpose_hi(0, "mix")
                split_to(1)
                evacuate_z(0)
                split_to(2)
                e.wait_ge(sem["b_in"], at("b_in", l, 2))
                nc.scalar.activation(bE, wk[:, 1, :], ACT.Exp, scale=-1.0).then_inc(sem["b_e"], 1)
                nc.scalar.activation(bQ, wk[:, 0, :], ACT.Tanh, scale=0.5).then_inc(sem["b_tq"], 1)
                split_to(3)
                evacuate_z(1)
                e.wait_ge(sem["d_zf"], at("d_zf", l, 1))
                nc.scalar.activation(dsm[:, 1, :], lf, ACT.Abs).then_inc(sem["d_abs"], 1)
                e.wait_ge(sem["d_abs"], at("d_abs", l, 1))
                nc.scalar.activation(dsm[:, 2, :], dsm[:, 1, :], ACT.Exp, scale=-1.0).then_inc(sem["d_e"], 1)
                e.wait_ge(sem["d_e"], at("d_e", l, 1))
                nc.scalar.activation(dsm[:, 3, :], dsm[:, 2, :], ACT.Ln, bias=1.0).then_inc(sem["d_ln"], 1)
                e.wait_ge(sem["b_f"], at("b_f", l, 1))
                nc.scalar.activation(bK, bK, ACT.Ln).then_inc(sem["b_ln"], 1)

                def level_exp(j):
                    e.wait_ge(sem["b_d"], at("b_d", l, j))
                    nc.scalar.activation(bE, bE, ACT.Abs).then_inc(sem["b_abs"], 1)
                    e.wait_ge(sem["b_abs"], at("b_abs", l, j))
                    nc.scalar.activation(bE, bE, ACT.Exp, scale=-1.0).then_inc(sem["b_E"], 1)

                split_to(4)
                level_exp(1)
                split_to(5)
                evacuate_z(2)
                level_exp(2)
                split_to(6)
                level_exp(3)
                split_to(7)
                evacuate_z(3)
                e.wait_ge(sem["z"], at("z", l, 8))
                nc.scalar.activation(square[:, 0:1024], region("wide", 1024, 1024), ACT.Square)\
                    .then_inc(sem["ad_sq"], 1)
                level_exp(4)
                split_to(8)
                level_exp(5)
                split_to(9)
                evacuate_z(4)
                e.wait_ge(sem["z"], at("z", l, 10))
                e.wait_ge(sem["mean"], at("mean", l, NORM_D + 1))
                nc.scalar.activation(square[:, 0:768].rearrange("p (t c) -> p t c", t=T), z_a[:, :, 0:384], ACT.Square)\
                    .then_inc(sem["ad_sq"], 1)
                level_exp(6)
                split_to(10)
                level_exp(7)
                e.wait_ge(sem["ad_T"], at("ad_T", l, 1))
                nc.scalar.activation(region("qkT", 0, 512), wk[:, 2, :], ACT.Copy).then_inc(sem["ad_sb"], 1)
                e.wait_ge(sem["ad_T"], at("ad_T", l, 2))
                nc.scalar.activation(region("qkT", 512, 512), wk[:, 3, :], ACT.Copy, scale=p_("gd"))\
                    .then_inc(sem["ad_sb"], 1)
                split_to(11)
                evacuate_z(5)
                e.wait_ge(sem["z"], at("z", l, 12))
                for t in range(T):
                    nc.scalar.activation(junk[:, t * C_Q:(t + 1) * C_Q], z_c[:, t, 0:C_Q], ACT.Square,
                                         accum_out=norm(NORM_C1, 0)[:, t:t + 1])
                for t in range(T):
                    i = nc.scalar.activation(junk[:, (4 + t) * C_KV:(5 + t) * C_KV], z_c[:, t, C_Q:C_Q + C_KV], ACT.Square,
                                             accum_out=norm(NORM_C1, 0)[:, T + t:T + t + 1])
                i.then_inc(sem["c_sq"], 1)
                e.wait_ge(sem["b_QK"], at("b_QK", l, LEVELS))
                for hp in range(2):
                    nc.scalar.activation(bE[:, hp * SEQ:hp * SEQ + P], bT[:, hp * SEQ:hp * SEQ + P], ACT.Exp,
                                         scale=-1.0, bias=bT[:, hp * SEQ + P - 1:hp * SEQ + P])
                    i = nc.scalar.activation(bE[:, hp * SEQ + P:(hp + 1) * SEQ], bT[:, hp * SEQ + P:(hp + 1) * SEQ],
                                             ACT.Exp)
                i.then_inc(sem["b_Ex"], 1)
                split_to(12)
                e.wait_ge(sem["ad_T"], at("ad_T", l, 3))
                nc.scalar.activation(region("qkT", 1024, 512), wk[:, 2, :], ACT.Copy).then_inc(sem["ad_sb"], 1)
                e.wait_ge(sem["ad_T"], at("ad_T", l, 4))
                nc.scalar.activation(region("qkT", 1536, 512), wk[:, 3, :], ACT.Copy, scale=p_("ga"))\
                    .then_inc(sem["ad_sb"], 1)
                split_to(13)
                for odd in range(2):
                    e.wait_ge(sem["b_cross"], at("b_cross", l, odd + 1))
                    nc.scalar.activation(AT[2][:, 2 * odd:2 * odd + 2, :].rearrange("p h s -> p (h s)"),
                                         wk[:, 2 + odd, 0:2 * P], ACT.Copy).then_inc(sem["b_atx"], 1)
                gate_tanh(0)
                exps(0, 1.0)
                split_to(14)
                e.wait_ge(sem["c_T"], at("c_T", l, 2))
                for k in range(2):
                    nc.scalar.activation(cT_hi[:, k].rearrange("p t s -> p (t s)"), wk[:, 1, k * SEQ:(k + 1) * SEQ],
                                         ACT.Copy, scale=p_("cq")[:, k:k + 1])
                nc.scalar.activation(cT_hi[:, 2].rearrange("p t s -> p (t s)"), wk[:, 2, 0:SEQ], ACT.Copy,
                                     scale=p_("ckv")).then_inc(sem["c_hi"], 1)
                e.wait_ge(sem["b_o"], at("b_o", l, 1))
                e.wait_ge(sem["b_QK"], at("b_QK", l, LEVELS + 1))
                nc.scalar.activation(bE, wk[:, 3, :], ACT.Square).then_inc(sem["b_sq"], 1)
                nc.scalar.activation(bQ.rearrange("p (t c) -> p t c", t=T), z_ig[:, :, BW:2 * BW], ACT.Tanh, scale=0.5)\
                    .then_inc(sem["b_tg"], 1)
                split_to(15)
                gate_tanh(1)
                pT_copy(0)
                exps(1, 1.0)
                split_to(16)
                split_to(17)
                gate_tanh(2)
                pT_copy(1)
                exps(2, 1.0)
                split_to(18)
                yT_hi_copy(0)
                split_to(19)
                gate_tanh(3)
                pT_copy(2)
                exps(3, 1.0)
                split_to(20)
                yT_hi_copy(1)
                e.wait_ge(sem["mm"], at("mm", l, UQ + 1))
                e.wait_ge(sem["b_y"], at("b_y", l, 1))
                for t in range(T):
                    nc.scalar.activation(c_q[:, 4 * t:4 * t + 4, :].rearrange("p g c -> p (g c)"),
                                         acc[:, t, 0:H * C_DQ], ACT.Copy).then_inc(sem["u"], 1)
                split_to(21)
                e.wait_ge(sem["mm"], at("mm", l, UKV + 1))
                for t in range(T):
                    nc.scalar.activation(c_kv[:, 4 * t:4 * t + 4, :].rearrange("p g c -> p (g c)"), acc[:, 2 + t, :],
                                         ACT.Copy).then_inc(sem["u"], 1)
                pT_copy(3)
                e.wait_ge(sem["u"], at("u", l, 4))
                nc.scalar.activation(c_s.rearrange("p (g c) -> p g c", c=C_DQ), c_q, ACT.Square)
                nc.scalar.activation(c_s2.rearrange("p (g c) -> p g c", c=HD), c_kv[:, :, 0:HD], ACT.Square)
                for t in range(T):
                    i = nc.scalar.activation(c_r[:, 32 * t:32 * t + 32], z_c[:, t, 384:416], ACT.Square,
                                             accum_out=dsm[:, 4, t:t + 1])
                i.then_inc(sem["c_sq2"], 1)
                split_to(24)
                gate_tanh(4)
                yT_hi_copy(2)
                split_to(25)
                for n in range(4):
                    e.wait_ge(sem["c_T2"], at("c_T2", l, n + 1))
                    nc.scalar.activation(arena[0:C_DQ, area["qkT"][0] + 512 * n:area["qkT"][0] + 512 * n + 512],
                                         wk[0:C_DQ, n, :], ACT.Copy).then_inc(sem["c_sb2"], 1)
                split_to(26)
                gate_tanh(5)
                exps(4, C_DQ ** -0.5)
                split_to(27)
                pT_copy(4)
                exps(5, C_DQ ** -0.5)
                split_to(29)
                gate_tanh(6)
                pT_copy(5)
                split_to(31)
                gate_tanh(7)
                yT_hi_copy(3)
                split_to(33)
                transpose_hi(4, None)
                split_to(37)
                e.wait_ge(sem["xmid"], at("xmid", l, 4))
                squares(NORM2)
                transpose_hi(8, "ffn")

                def ffn_split(c, i):
                    e.wait_ge(sem["mm"], at("mm", l, i * 4 + (c - (RING - 1))))
                    e.wait_ge(raw_loaded[c % RAW], (l * (CHUNKS // RAW) + i * 2 + (c // RAW + 1)) * 16)
                    nc.scalar.activation(w_hi[:, c % RING, :], raw[:, c % RAW, :], ACT.Copy).then_inc(sem["hi"], 1)

                def ffn_tanh(b, i):
                    e.wait_ge(sem["mm"], at("mm", l, i * 4 + (FFN0 + 2 * b + 2)))
                    for t in range(T):
                        nc.scalar.activation(sw[:, b % 2, t, :], acc[:, 2 * (b % 2) + t, 0:256], ACT.Tanh, scale=0.5)\
                            .then_inc(sem["tanh"], 1)

                def ffn_hi(b, i):
                    e.wait_ge(sem["aT"], at("aT", l, i * 2 + (b + 1)))
                    to = aT_hi[:, b * 512:b * 512 + 512] if isinstance(i, int) else aT_hi[:, bass.ds(i * 1024 + b * 512, 512)]
                    nc.scalar.activation(to, wk[:, b % 2, :], ACT.Copy, scale=0.5).then_inc(sem["aT_hi"], 1)

                split_to(39)
                ffn_tanh(0, 0)
                with e.Fori(0, FFN_BLOCKS // 2) as i:
                    for b in (1, 2):
                        ffn_split(FFN0 + 2 * b + 3, i)
                        ffn_split(FFN0 + 2 * b + 4, i)
                        ffn_tanh(b, i)
                        ffn_hi(b - 1, i)
                split[0] = DOWN0 + 3
                split_to(DOWN0)
                ffn_hi(FFN_BLOCKS - 1, 0)
                split_to(CHUNKS)

        @block.vector
        def _(v):
            V = nc.vector
            v.wait_ge(loaded["par"], 16)
            lb = PARX["lb"][0]
            lo_, om_ = PARX["low"][0], PARX["oml"][0]
            V.tensor_tensor(small[:, 0:2], par[:, 0, lb:lb + 2], par[:, 1, lb:lb + 2], ALU.max).then_inc(setup, 1)
            v.wait_ge(setup, 1)
            V.tensor_tensor(small[:, 4:8].rearrange("p (l c) -> p l c", l=2), par[:, :, lb:lb + 2],
                            small[:, 0:2][:, None, :].to_broadcast([P, 2, 2]), ALU.subtract).then_inc(setup, 1)
            v.wait_ge(setup, 3)
            V.tensor_tensor(small[:, 12:14], small[:, 8:10], small[:, 10:12], ALU.add).then_inc(setup, 1)
            v.wait_ge(setup, 4)
            V.reciprocal(small[:, 14:16], small[:, 12:14]).then_inc(setup, 1)
            v.wait_ge(setup, 5)
            V.tensor_tensor(par[:, 1, lo_:lo_ + 2], small[:, 10:12], small[:, 14:16], ALU.mult).then_inc(setup, 1)
            V.memset(par[:, 0, lo_:lo_ + 2], 0.0)
            v.wait_ge(loaded["mask"], 16)
            v.wait_ge(loaded["level"], 16)
            V.tensor_copy(level[:, :, :].rearrange("p l s -> p (l s)"), arena[:, MASK_N:MASK_N + LEVELS * P])
            V.tensor_copy(mask[:, :], arena[:, 0:MASK_N]).then_inc(setup, 1)
            v.wait_ge(setup, 7)
            V.tensor_scalar(par[:, :, om_:om_ + 2], par[:, :, lo_:lo_ + 2], -1.0, 1.0, ALU.mult, ALU.add)\
                .then_inc(setup, 1)
            for name, q, k in (("ga", "aq", "ak"), ("gd", "dq", "dk")):
                col = PARX[name][0]
                V.scalar_tensor_tensor(par[:, :, col:col + 1], par[:, :, PARX[q][0]:PARX[q][0] + 1], HD ** -0.5,
                                       par[:, :, PARX[k][0]:PARX[k][0] + 1], ALU.mult, ALU.mult).then_inc(setup, 1)
            v.sem_inc(sem["xout"], HEADS["xout"])
            v.sem_inc(sem["act"], HEADS["act"])
            v.sem_inc(sem["aT_lo"], HEADS["aT_lo"])
            v.wait_ge(setup, 10)
            v.wait_ge(loaded["const"], 16)
            v.wait_ge(loaded["x"], 16)

            with v.Fori(0, DEPTH) as l:
                split = [0]
                links = [0]

                def link(i):
                    i.then_inc(sem["dve"], 1)
                    links[0] += 1
                    v.wait_ge(sem["dve"], at("dve", l, links[0]))

                def split_chunk(c):
                    n = width(c)
                    v.wait_ge(sem["hi"], at("hi", l, c + 1))
                    V.tensor_tensor(w_lo[:, c % RING, 0:n], raw[:, c % RAW, 0:n], w_hi[:, c % RING, 0:n].bitcast(F32),
                                    ALU.subtract).then_inc(sem["lo"], 1)

                def split_to(p):
                    while split[0] < min(p + RING, CHUNKS):
                        split_chunk(split[0])
                        split[0] += 1

                def mean(which, cols, scale):
                    i = V.tensor_scalar(norm(which, 1)[:, cols], norm(which, 0)[:, cols], scale, EPS, ALU.mult, ALU.add)
                    return i

                def transpose_lo(first, gain):
                    for n in range(4):
                        v.wait_ge(sem["xT_hi"], at("xT_hi", l, first + n + 1))
                        t, h = n // 2, n % 2
                        if gain is None:
                            V.scalar_tensor_tensor(xT_lo[:, t, 4 * h:4 * h + 4, :].rearrange("p k s -> p (k s)"),
                                                   wk[:, n, :], 0.5,
                                                   xT_hi[:, t, 4 * h:4 * h + 4, :].rearrange("p k s -> p (k s)").bitcast(F32),
                                                   ALU.mult, ALU.subtract).then_inc(sem["xT_lo"], 1)
                            continue
                        for k in range(4):
                            i = V.scalar_tensor_tensor(xT_lo[:, t, 4 * h + k, :], wk[:, n, k * P:(k + 1) * P],
                                                       p_(gain)[:, 4 * h + k:4 * h + k + 1],
                                                       xT_hi[:, t, 4 * h + k, :].bitcast(F32), ALU.mult, ALU.subtract)
                        i.then_inc(sem["xT_lo"], 1)

                def norm_x(which, first):
                    v.wait_ge(sem["sumsq"], at("sumsq", l, first + T))
                    mean(which, slice(0, T), 1.0 / D).then_inc(sem["mean"], 1)
                    v.wait_ge(sem["rstd"], at("rstd", l, which + 1))
                    for t in range(T):
                        V.tensor_scalar(xn[:, t, :], x[:, t, :], norm(which, 2)[:, t:t + 1], None, ALU.mult)\
                            .then_inc(sem["xn"], 1)

                def tops(u, scale, sinks=False):
                    t = u % 2
                    c = slice(4 * u, 4 * u + 4)
                    v.wait_ge(sem["score"], at("score", l, u + 1))
                    link(V.reduce_max(mx[:, c].rearrange("p (h o) -> p h o", h=2),
                                      wk[:, 0:2, :].rearrange("p o (h m) -> p h o m", h=2)[:, :, :, 0:(t + 1) * P], axis=AX.X))
                    if sinks:
                        link(V.tensor_tensor(mx[:, c], mx[:, c], p_("sink"), ALU.max))
                        link(V.tensor_tensor(esink[:, c], p_("sink"), mx[:, c], ALU.subtract))
                    V.tensor_scalar(negm[:, c], mx[:, c], -scale, None, ALU.mult).then_inc(sem["top"], 1)

                def attended(u, b, sinks=False):
                    t = u % 2
                    c = slice(4 * u, 4 * u + 4)
                    v.wait_ge(sem["pv"], at("pv", l, u + 1))
                    if sinks:
                        link(V.tensor_tensor(rowsum[:, c], rowsum[:, c], esink[:, c], ALU.add))
                    link(V.reciprocal(rden[:, c], rowsum[:, c]))
                    V.tensor_tensor(y[:, b, t, :].rearrange("p (h c) -> p h c", h=H),
                                    wk[:, 3, 0:BW].rearrange("p (h c) -> p h c", h=H),
                                    rden[:, c][:, :, None].to_broadcast([P, H, HD]), ALU.mult).then_inc(sem["y"], 1)

                def yT_lo_copy(n):
                    v.wait_ge(sem["yT_hi"], at("yT_hi", l, n + 1))
                    V.tensor_tensor(yT_lo[:, n % 2].rearrange("p c t s -> p (c t s)"), wk[:, 2, :],
                                    yT_hi[:, n % 2].rearrange("p c t s -> p (c t s)").bitcast(F32), ALU.subtract)\
                        .then_inc(sem["yT_lo"], 1)

                def merge(n):
                    v.wait_ge(sem["mm"], at("mm", l, PROJ[n] + 1))
                    v.wait_ge(sem["gate"], at("gate", l, 4 * n + 4))
                    for half in range(2):
                        for t in range(T):
                            cols = slice(half * 512, half * 512 + 512)
                            g = gates[:, n % 2, t, cols]
                            to = merged[:, t, cols]
                            bank = acc[:, 2 * half + t, :]
                            if n == 0:
                                V.scalar_tensor_tensor(to, g, 1.0, bank, ALU.add, ALU.mult).then_inc(sem["merge"], 1)
                                continue
                            link(V.scalar_tensor_tensor(g, g, 1.0, bank, ALU.add, ALU.mult))
                            V.tensor_tensor(to, to, g, ALU.add).then_inc(sem["merge"], 1)

                V.tensor_copy(now[:, :], par[:, bass.ds(l, 1), :].rearrange("p a n -> p (a n)")).then_inc(sem["par"], 1)
                v.wait_ge(sem["par"], at("par", l, 1))
                norm_x(NORM1, 0)
                split_chunk(0)
                split_chunk(1)
                split[0] = 2
                transpose_lo(0, "mix")
                split_to(2)
                v.wait_ge(sem["b_tq"], at("b_tq", l, 1))
                V.scalar_tensor_tensor(bq, bQ, 1.0, wk[:, 0, :], ALU.add, ALU.mult).then_inc(sem["b_q"], 1)
                link(V.tensor_scalar(bE, bE, 1.0, None, ALU.add))
                link(V.reciprocal(bT, bE))
                for hp in range(2):
                    c = slice(hp * SEQ, (hp + 1) * SEQ)
                    i = V.tensor_scalar(bT[:, c], bT[:, c], p_("oml")[:, hp:hp + 1], p_("low")[:, hp:hp + 1], ALU.mult,
                                        ALU.add)
                link(i)
                V.tensor_scalar(bk, bT, -0.5, 0.5, ALU.mult, ALU.add)
                V.tensor_scalar(bK, bT, 1e-19, None, ALU.max).then_inc(sem["b_f"], 1)
                split_to(3)
                v.wait_ge(sem["z"], at("z", l, 4))
                V.tensor_tensor(lf.rearrange("p (t h) -> p t h", t=T), z_dv[:, :, BW:BW + H],
                                p_("fb")[:, None, :].to_broadcast([P, T, H]), ALU.add).then_inc(sem["d_zf"], 1)
                split_to(4)
                v.wait_ge(sem["b_ln"], at("b_ln", l, 1))
                for n in range(4):
                    c = slice(n * P, (n + 1) * P)
                    i = V.tensor_tensor_scan(bT[:, c], c_("ones"), bK[:, c], 0.0, ALU.mult, ALU.add)
                i.then_inc(sem["b_scan"], 1)
                v.wait_ge(sem["b_scan"], at("b_scan", l, 1))

                def level_diff(j):
                    m = 2 ** j // 2
                    if j > 1:
                        v.wait_ge(sem["b_QK"], at("b_QK", l, j - 1))
                    blocks = bT.rearrange("p (n m) -> p n m", m=2 * m)
                    V.tensor_tensor(bE.rearrange("p (n m) -> p n m", m=2 * m), blocks,
                                    blocks[:, :, m - 1:m].to_broadcast([P, 512 // (2 * m), 2 * m]), ALU.subtract)\
                        .then_inc(sem["b_d"], 1)

                def level_qk(j):
                    v.wait_ge(sem["b_E"], at("b_E", l, j))
                    if j > 1:
                        v.wait_ge(sem["b_lev"], at("b_lev", l, 2 * j))
                    V.tensor_tensor(bQ, bq, bE, ALU.mult)
                    V.tensor_tensor(bK, bk, bE, ALU.mult).then_inc(sem["b_QK"], 1)

                def level_take(j):
                    for odd in range(2):
                        bank = wk[:, odd, :].rearrange("p (h s) -> p h s", h=H)
                        if j == 0:
                            v.wait_ge(sem["b_lev"], at("b_lev", l, odd + 1))
                            V.tensor_tensor(AT[odd], bank, c_("ident")[:, None, :].to_broadcast([P, H, P]), ALU.mult)\
                                .then_inc(sem["b_at"], 1)
                        else:
                            V.copy_predicated(AT[odd], level[:, j - 1, :][:, None, :].to_broadcast([P, H, P]), bank)\
                                .then_inc(sem["b_at"], 1)

                level_diff(1)
                v.wait_ge(sem["d_ln"], at("d_ln", l, 1))
                link(V.tensor_scalar(dsm[:, 4, :], lf, 0.0, None, ALU.min))
                V.tensor_tensor(lf, dsm[:, 4, :], dsm[:, 3, :], ALU.subtract).then_inc(sem["d_lf"], 1)
                v.wait_ge(sem["d_lf"], at("d_lf", l, 1))
                for t in range(T):
                    i = V.tensor_tensor(X[:, t], c_("stri")[:, None, :].to_broadcast([P, H, P]),
                                        lf[:, H * t:H * t + H][:, :, None].to_broadcast([P, H, P]), ALU.mult)
                i.then_inc(sem["d_x"], 1)
                for j in range(1, LEVELS + 1):
                    split_to(4 + j)
                    level_qk(j)
                    level_take(j - 1)
                    if j < LEVELS:
                        level_diff(j + 1)
                    if j == 4:
                        v.wait_ge(sem["ad_sq"], at("ad_sq", l, 1))
                        link(V.reduce_sum(norm(NORM_D, 0), square[:, 0:1024].rearrange("p (g c) -> p g c", c=HD),
                                          axis=AX.X))
                        mean(NORM_D, slice(0, 16), 1.0 / HD).then_inc(sem["mean"], 1)
                    if j == 5:
                        v.wait_ge(sem["rstd"], at("rstd", l, NORM_D + 1))
                        zq = region("wide", 1024, 1024).rearrange("p (g c) -> p g c", c=HD)
                        V.tensor_tensor(zq, zq, norm(NORM_D, 2)[:, :, None].to_broadcast([P, 16, HD]), ALU.mult)\
                            .then_inc(sem["ad_n"], 1)
                    if j == 6:
                        v.wait_ge(sem["ad_sq"], at("ad_sq", l, 2))
                        link(V.reduce_sum(norm(NORM_A, 0), square[:, 0:768].rearrange("p (g c) -> p g c", c=HD),
                                          axis=AX.X))
                        mean(NORM_A, slice(0, 12), 1.0 / HD).then_inc(sem["mean"], 1)
                    if j == 7:
                        v.wait_ge(sem["rstd"], at("rstd", l, NORM_A + 1))
                        for t in range(T):
                            r = norm(NORM_A, 2)[:, 6 * t:6 * t + 6]
                            q = z_a[:, t, 0:BW].rearrange("p (h c) -> p h c", h=H)
                            V.tensor_tensor(q, q, r[:, 0:H][:, :, None].to_broadcast([P, H, HD]), ALU.mult)
                            k = z_a[:, t, BW:BW + P].rearrange("p (h c) -> p h c", h=A_KV)
                            for dup in range(2):
                                i = V.tensor_tensor(kdup[:, t, :].rearrange("p (h d c) -> p h d c", h=A_KV, d=2)[:, :, dup],
                                                    k, r[:, H:H + A_KV][:, :, None].to_broadcast([P, A_KV, HD]), ALU.mult)
                        i.then_inc(sem["ad_n"], 1)
                split_to(12)
                v.wait_ge(sem["b_Ex"], at("b_Ex", l, 1))
                v.wait_ge(sem["b_lev"], at("b_lev", l, 2 * (LEVELS + 1)))
                halves = [a.rearrange("p (h t s) -> p h t s", h=2, t=T) for a in (bq, bk, bE, bQ, bK)]
                V.tensor_tensor(halves[3][:, :, 1], halves[0][:, :, 1], halves[2][:, :, 1], ALU.mult)
                V.tensor_tensor(halves[4][:, :, 0], halves[1][:, :, 0], halves[2][:, :, 0], ALU.mult)\
                    .then_inc(sem["b_QK"], 1)
                level_take(LEVELS)
                v.wait_ge(sem["c_sq"], at("c_sq", l, 1))
                mean(NORM_C1, slice(0, T), 1.0 / C_Q)
                mean(NORM_C1, slice(T, 2 * T), 1.0 / C_KV).then_inc(sem["mean"], 1)
                split_to(13)
                tops(0, 1.0)
                v.wait_ge(sem["rstd"], at("rstd", l, NORM_C1 + 1))
                for t in range(T):
                    r = norm(NORM_C1, 2)
                    V.tensor_scalar(z_c[:, t, 0:C_Q], z_c[:, t, 0:C_Q], r[:, t:t + 1], None, ALU.mult)
                    i = V.tensor_scalar(z_c[:, t, C_Q:C_Q + C_KV], z_c[:, t, C_Q:C_Q + C_KV], r[:, T + t:T + t + 1], None,
                                        ALU.mult)
                i.then_inc(sem["c_n"], 1)
                split_to(14)
                v.wait_ge(sem["c_hi"], at("c_hi", l, 1))
                for k in range(2):
                    V.scalar_tensor_tensor(cT_lo[:, k].rearrange("p t s -> p (t s)"), wk[:, 1, k * SEQ:(k + 1) * SEQ],
                                           p_("cq")[:, k:k + 1], cT_hi[:, k].rearrange("p t s -> p (t s)").bitcast(F32),
                                           ALU.mult, ALU.subtract)
                V.scalar_tensor_tensor(cT_lo[:, 2].rearrange("p t s -> p (t s)"), wk[:, 2, 0:SEQ], p_("ckv"),
                                       cT_hi[:, 2].rearrange("p t s -> p (t s)").bitcast(F32), ALU.mult, ALU.subtract)\
                    .then_inc(sem["c_lo"], 1)
                v.wait_ge(sem["b_sq"], at("b_sq", l, 1))
                link(V.reduce_sum(norm(NORM_B, 0), bE.rearrange("p (g c) -> p g c", c=HD), axis=AX.X))
                mean(NORM_B, slice(0, 8), 1.0 / HD).then_inc(sem["mean"], 1)
                split_to(15)
                tops(1, 1.0)
                v.wait_ge(sem["rstd"], at("rstd", l, NORM_B + 1))
                v.wait_ge(sem["b_tg"], at("b_tg", l, 1))
                g8 = [P, 8, HD]
                link(V.tensor_tensor(bT.rearrange("p (g c) -> p g c", c=HD), wk[:, 3, :].rearrange("p (g c) -> p g c", c=HD),
                                     norm(NORM_B, 2)[:, :, None].to_broadcast(g8), ALU.mult))
                V.tensor_tensor(bT.rearrange("p (g c) -> p g c", c=HD), bT.rearrange("p (g c) -> p g c", c=HD),
                                p_("bo")[:, None, :].to_broadcast(g8), ALU.mult)
                link(V.scalar_tensor_tensor(bK.rearrange("p (t c) -> p t c", t=T), bQ.rearrange("p (t c) -> p t c", t=T),
                                            1.0, z_ig[:, :, BW:2 * BW], ALU.add, ALU.mult))
                V.scalar_tensor_tensor(y[:, 0].rearrange("p t c -> p (t c)"), bT, 0.5, bK, ALU.mult, ALU.mult)\
                    .then_inc(sem["b_y"], 1)
                split_to(16)
                attended(0, 1)
                split_to(17)
                tops(2, 1.0, sinks=True)
                split_to(18)
                attended(1, 1)
                yT_lo_copy(0)
                split_to(19)
                tops(3, 1.0, sinks=True)
                split_to(20)
                attended(2, 0, sinks=True)
                yT_lo_copy(1)
                split_to(21)
                v.wait_ge(sem["c_sq2"], at("c_sq2", l, 1))
                V.reduce_sum(norm(NORM_C2, 0)[:, 0:8], c_s.rearrange("p (g c) -> p g c", c=C_DQ), axis=AX.X)
                link(V.reduce_sum(norm(NORM_C2, 0)[:, 8:16], c_s2.rearrange("p (g c) -> p g c", c=HD), axis=AX.X))
                k8 = norm(NORM_C2, 0)[:, 8:16].rearrange("p (t h) -> p t h", t=T)
                link(V.tensor_tensor(k8, k8, dsm[:, 4, 0:T][:, :, None].to_broadcast([P, T, H]), ALU.add))
                mean(NORM_C2, slice(0, 16), 1.0 / C_DQ).then_inc(sem["mean"], 1)
                split_to(22)
                attended(3, 0, sinks=True)
                merge(0)
                v.wait_ge(sem["rstd"], at("rstd", l, NORM_C2 + 1))
                r = norm(NORM_C2, 2)
                link(V.tensor_tensor(c_q, c_q, r[:, 0:8][:, :, None].to_broadcast([P, 8, C_DQ]), ALU.mult))
                V.tensor_tensor(c_q, c_q, p_("cqn")[:, None, :].to_broadcast([P, 8, C_DQ]), ALU.mult)
                V.tensor_tensor(c_k[:, :, 0:HD], c_kv[:, :, 0:HD], r[:, 8:16][:, :, None].to_broadcast([P, 8, HD]), ALU.mult)
                for t in range(T):
                    i = V.tensor_tensor(c_k[:, 4 * t:4 * t + 4, HD:C_DQ], z_c[:, t, 384:416][:, None, :].to_broadcast([P, H, C_ROPE]),
                                        r[:, 8 + 4 * t:12 + 4 * t][:, :, None].to_broadcast([P, H, C_ROPE]), ALU.mult)
                link(i)
                link(V.tensor_tensor(c_k, c_k, p_("ckn")[:, None, :].to_broadcast([P, 8, C_DQ]), ALU.mult))
                half = C_ROPE // 2
                for n, a in enumerate((c_q, c_k)):
                    rot = c_r[:, 256 * n:256 * n + 256].rearrange("p (g c) -> p g c", c=C_ROPE)
                    for t in range(T):
                        g = slice(4 * t, 4 * t + 4)
                        cos = c_("cos")[:, C_ROPE * t:C_ROPE * (t + 1)][:, None, :]
                        sin = c_("sin")[:, C_ROPE * t:C_ROPE * (t + 1)][:, None, :]
                        V.tensor_tensor(rot[:, g, 0:half], a[:, g, HD + half:C_DQ], sin[:, :, 0:half].to_broadcast([P, H, half]),
                                        ALU.mult)
                        link(V.tensor_tensor(rot[:, g, half:C_ROPE], a[:, g, HD:HD + half],
                                             sin[:, :, half:C_ROPE].to_broadcast([P, H, half]), ALU.mult))
                        i = V.tensor_tensor(a[:, g, HD:C_DQ], a[:, g, HD:C_DQ], cos.to_broadcast([P, H, C_ROPE]), ALU.mult)
                    link(i)
                    i = V.tensor_tensor(a[:, :, HD:C_DQ], a[:, :, HD:C_DQ], rot, ALU.add)
                i.then_inc(sem["c_n2"], 1)
                split_to(24)
                yT_lo_copy(2)
                split_to(26)
                tops(4, C_DQ ** -0.5)
                split_to(27)
                tops(5, C_DQ ** -0.5)
                merge(1)
                split_to(28)
                attended(4, 1)
                split_to(30)
                attended(5, 1)
                split_to(31)
                yT_lo_copy(3)
                split_to(32)
                merge(2)
                split_to(33)
                merge(3)
                transpose_lo(4, None)

                def residual(done, banks, first):
                    for t in range(T):
                        V.tensor_tensor(x[:, t, first * 512:first * 512 + 512], x[:, t, first * 512:first * 512 + 512],
                                        acc[:, banks + t, :], ALU.add).then_inc(done, 1)

                split_to(35)
                v.wait_ge(sem["mm"], at("mm", l, OUT0 + 2))
                residual(sem["xmid"], 0, 0)
                split_to(37)
                v.wait_ge(sem["mm"], at("mm", l, OUT0 + 4))
                residual(sem["xmid"], 2, 1)
                v.wait_ge(sem["xmid"], at("xmid", l, 4))
                norm_x(NORM2, T)
                transpose_lo(8, "ffn")

                def ffn_split(c, i):
                    v.wait_ge(sem["hi"], at("hi", l, i * 4 + (c + 1)))
                    V.tensor_tensor(w_lo[:, c % RING, :], raw[:, c % RAW, :], w_hi[:, c % RING, :].bitcast(F32),
                                    ALU.subtract).then_inc(sem["lo"], 1)

                def swiglu(b, i):
                    for t in range(T):
                        bank = acc[:, 2 * (b % 2) + t, :]
                        v.wait_ge(sem["tanh"], at("tanh", l, i * 4 + (2 * b + t + 1)))
                        if b and t == 0:
                            v.wait_ge(sem["aT"], at("aT", l, i * 2 + (b - 1)))
                        last = V.scalar_tensor_tensor(sw[:, b % 2, t, :], sw[:, b % 2, t, :], 1.0, bank[:, 0:256], ALU.add,
                                                      ALU.mult)
                    last.then_inc(sem["sw"], 1)
                    v.wait_ge(sem["sw"], at("sw", l, i * 2 + (b + 1)))
                    for t in range(T):
                        bank = acc[:, 2 * (b % 2) + t, :]
                        V.tensor_tensor(act[:, b % 2, t, :], sw[:, b % 2, t, :], bank[:, 256:512], ALU.mult)\
                            .then_inc(sem["act"], 1)

                def ffn_lo(b, i):
                    v.wait_ge(sem["aT_hi"], at("aT_hi", l, i * 2 + (b + 1)))
                    if isinstance(i, int):
                        hi, lo = aT_hi[:, b * 512:b * 512 + 512], aT_lo[:, b * 512:b * 512 + 512]
                    else:
                        hi, lo = (a[:, bass.ds(i * 1024 + b * 512, 512)] for a in (aT_hi, aT_lo))
                    V.scalar_tensor_tensor(lo, wk[:, b % 2, :], 0.5, hi.bitcast(F32), ALU.mult, ALU.subtract)\
                        .then_inc(sem["aT_lo"], 1)

                split_to(39)
                swiglu(0, 0)
                with v.Fori(0, FFN_BLOCKS // 2) as i:
                    for b in (1, 2):
                        ffn_split(FFN0 + 2 * b + 3, i)
                        ffn_split(FFN0 + 2 * b + 4, i)
                        swiglu(b, i)
                        ffn_lo(b - 1, i)
                split[0] = DOWN0 + 3
                split_to(DOWN0)
                ffn_lo(FFN_BLOCKS - 1, 0)
                split_to(DOWN0 + DOWN_CHUNKS - 1)
                v.wait_ge(sem["mm"], at("mm", l, DOWN0 + DOWN_CHUNKS))
                residual(sem["xout"], 0, 0)
                split_to(CHUNKS)
                v.wait_ge(sem["mm"], at("mm", l, CHUNKS))
                residual(sem["xout"], 2, 1)
                assert links[0] == LINKS, links[0]
                v.wait_ge(sem["xout"], at("xout", l, 4))

        @block.tensor
        def _(pe):
            M = nc.tensor
            pe.sem_inc(sem["mm"], HEADS["mm"])
            pe.sem_inc(sem["aT"], HEADS["aT"])
            pe.wait_ge(loaded["const"], 16)
            pe.wait_ge(setup, 7)

            with pe.Fori(0, DEPTH) as l:
                def chunk(c, parts, off=0, slot=None):
                    slot = c % RING
                    pe.wait_ge(sem["lo"], at("lo", l, off + (c + 1)))
                    for bank, cols, rows, start, stop in parts:
                        for n, (hi, lo, col) in enumerate(rows):
                            wh, wl = w_hi[:, slot, col:col + cols], w_lo[:, slot, col:col + cols]
                            M.matmul(bank[:, 0:cols], hi, wh, start=start and n == 0, stop=False)
                            M.matmul(bank[:, 0:cols], lo, wh, start=False, stop=False)
                            i = M.matmul(bank[:, 0:cols], hi, wl, start=False, stop=stop and n == len(rows) - 1)
                    i.then_inc(sem["mm"], 1)

                def half_block(c, cols, pair, h, off=0):
                    chunk(c + h, [(acc[:, 2 * pair + t, :], cols,
                                   [(xT_hi[:, t, 4 * h + k, :], xT_lo[:, t, 4 * h + k, :], k * cols) for k in range(4)],
                                   h == 0, h == 1) for t in range(T)], off)

                ident = c_("ident")

                def transposes(bank, tiles, ready):
                    for n, a in enumerate(tiles):
                        w = a.shape[-1]
                        i = M.transpose(bank[0:w, n * P:(n + 1) * P], a, ident)
                    i.then_inc(ready, 1)

                def x_transposes(a):
                    for n in range(4):
                        t, h = n // 2, n % 2
                        transposes(wk[:, n, :], [a[:, t, (4 * h + k) * P:(4 * h + k + 1) * P] for k in range(4)], sem["xT"])

                for t in range(T):
                    pe.wait_ge(sem["xn"], at("xn", l, t + 1))
                x_transposes(xn)
                pe.wait_ge(sem["xT_lo"], at("xT_lo", l, 4))

                def b_level(j, q, k):
                    if j:
                        pe.wait_ge(sem["b_at"], at("b_at", l, 2 * j))
                    for odd in range(2):
                        r = slice(HD * odd, HD * odd + HD)
                        for n in range(4):
                            c = slice(n * P, (n + 1) * P)
                            i = M.matmul(wk[:, odd, c], k[r, c], q[r, c], start=True, stop=True)
                        i.then_inc(sem["b_lev"], 1)

                def qk_rows(branch, h, t, side):
                    base = area["qkT"][0]
                    if branch == BR_C:
                        col = base + 1024 * side + (2 * h + t) * P
                        return arena[0:C_DQ, col:col + P]
                    col = base + (1024 if branch == BR_A else 0) + 512 * side + (h // 2) * SEQ + t * P
                    r = HD * (h % 2)
                    return arena[r:r + HD, col:col + P]

                def scores(u, branch):
                    t = u % 2
                    for odd in range(2):
                        bank = wk[:, odd, :].rearrange("p (h k s) -> p h k s", h=2, k=T)
                        two = [P, 2, P]
                        pre = []
                        for k in range(t + 1):
                            if branch == BR_D and k == t:
                                pre.append((c_("tri"), X[:, t, odd:H:2, :], k))
                            elif branch == BR_D:
                                pre.append((c_("ones"), X[:, k, odd:H:2, :], k))
                                pre.append((c_("tri"), lf[:, H * t + odd:H * t + H:2][:, :, None].to_broadcast(two), k))
                            name = None
                            if k == t:
                                name = "causal" if branch == BR_D else "chunk"
                            elif branch == BR_A:
                                name = "window"
                            if name:
                                pre.append((m_("ident"), m_(name)[:, None, :].to_broadcast(two), k))
                        for n, (a, b, k) in enumerate(pre):
                            M.matmul(bank[:, :, k, :], a, b, start=n == 0, stop=False)
                        for n in range(2 * (t + 1)):
                            hp, k = n // (t + 1), n % (t + 1)
                            h = 2 * hp + odd
                            i = M.matmul(bank[:, hp, k, :], qk_rows(branch, h, t, 0), qk_rows(branch, h, k, 1), start=False,
                                         stop=n == 2 * t + 1)
                    i.then_inc(sem["score"], 1)

                def p_transposes(u):
                    pe.wait_ge(sem["prob"], at("prob", l, u + 1))
                    for k in range(u % 2 + 1):
                        if k == 1 and u:
                            pe.wait_ge(sem["y"], at("y", l, u))
                        transposes(wk[:, 2 + k, :], [prob[:, h, k, :] for h in range(H)], sem["pT"])

                def weighted(u, values):
                    t = u % 2
                    pe.wait_ge(sem["pT_sb"], at("pT_sb", l, PT_DONE[u]))
                    if u:
                        pe.wait_ge(sem["y"], at("y", l, u))
                    for h in range(H):
                        for k in range(t + 1):
                            i = M.matmul(wk[:, 3, h * HD:(h + 1) * HD], pT[:, k, h, :], values(k, h), start=k == 0,
                                         stop=k == t)
                    i.then_inc(sem["pv"], 1)

                def y_transposes(n):
                    transposes(wk[:, 2, :], [y[:, n % 2, t, c * P:(c + 1) * P] for c in range(2) for t in range(T)], sem["yT"])

                def z_first(b):
                    c = 2 * b
                    if b >= 2:
                        pe.wait_ge(sem["z"], at("z", l, 2 * (b - 1)))
                    half_block(c, Z_BLOCKS[b][1], b % 2, 0)

                def z_rest(b):
                    half_block(2 * b, Z_BLOCKS[b][1], b % 2, 1)

                def dv(k, h):
                    return z_dv[:, k, h * HD:(h + 1) * HD]

                def av(k, h):
                    return z_a[:, k, 384 + (h // 2) * HD:384 + (h // 2) * HD + HD]

                def cv(k, h):
                    return c_kv[:, 4 * k + h, HD:2 * HD]

                z_first(0)
                z_rest(0)
                z_first(1)
                pe.wait_ge(sem["z"], at("z", l, 2))
                for col in range(2):
                    transposes(wk[:, col, :], [z_qf[:, t, col * BW + hp * P:col * BW + (hp + 1) * P]
                                               for hp in range(2) for t in range(T)], sem["b_in"])
                z_rest(1)
                z_first(2)
                z_rest(2)
                pe.wait_ge(sem["b_scan"], at("b_scan", l, 1))
                b_level(0, bq, bk)

                def decayed_level(j):
                    pe.wait_ge(sem["b_QK"], at("b_QK", l, j))
                    b_level(j, bQ, bK)

                def ad_transposes(n, q, k):
                    pe.wait_ge(sem["ad_n"], at("ad_n", l, n + 1))
                    if n:
                        pe.wait_ge(sem["ad_sb"], at("ad_sb", l, 2 * n))
                    for side, a in enumerate((q, k)):
                        transposes(wk[:, 2 + side, :], [a[:, t, c * P:(c + 1) * P] for c in range(2) for t in range(T)], sem["ad_T"])

                z_first(3)
                decayed_level(1)
                z_rest(3)
                decayed_level(2)
                z_first(4)
                decayed_level(3)
                z_rest(4)
                decayed_level(4)
                z_first(5)
                decayed_level(5)
                ad_transposes(0, z_dqk[:, :, 0:BW], z_dqk[:, :, BW:2 * BW])
                z_rest(5)
                decayed_level(6)

                def gate_first(g):
                    branch, half = g // 2, g % 2
                    if g < 2:
                        pe.wait_ge(sem["z"], at("z", l, 10 + 2 * g))
                    elif g < 4:
                        pe.wait_ge(sem["gate"], at("gate", l, 2 * (g - 1)))
                    else:
                        pe.wait_ge(sem["merge"], at("merge", l, 4 * (branch - 1)))
                    half_block(GATE0[branch] + 2 * half, 512, half, 0)

                def gate_rest(g):
                    branch, half = g // 2, g % 2
                    half_block(GATE0[branch] + 2 * half, 512, half, 1)

                def project(n):
                    pe.wait_ge(sem["yT_lo"], at("yT_lo", l, n + 1))
                    if n == 0:
                        pe.wait_ge(sem["u"], at("u", l, 4))
                    elif n < 3:
                        pe.wait_ge(sem["gate"], at("gate", l, 4 * n + 8))
                    else:
                        pe.wait_ge(sem["merge"], at("merge", l, 12))
                    chunk(PROJ[n], [(acc[:, 2 * half + t, :], 512,
                                     [(yT_hi[:, n % 2, k, t, :], yT_lo[:, n % 2, k, t, :], k * D + half * 512)
                                      for k in range(2)], True, True) for half in range(2) for t in range(T)])

                def b_cross():
                    pe.wait_ge(sem["b_QK"], at("b_QK", l, LEVELS + 1))
                    pe.wait_ge(sem["ad_sb"], at("ad_sb", l, 4))
                    for odd in range(2):
                        r = slice(HD * odd, HD * odd + HD)
                        for hp in range(2):
                            col = hp * SEQ
                            i = M.matmul(wk[:, 2 + odd, hp * P:(hp + 1) * P], bK[r, col:col + P], bQ[r, col + P:col + 2 * P],
                                         start=True, stop=True)
                        i.then_inc(sem["b_cross"], 1)

                def b_out():
                    pe.wait_ge(sem["b_atx"], at("b_atx", l, 2))
                    pe.wait_ge(sem["b_at"], at("b_at", l, 2 * (LEVELS + 1)))
                    for t in range(T):
                        for h in range(H):
                            o = wk[:, 3, t * BW + h * HD:t * BW + (h + 1) * HD]
                            if t:
                                M.matmul(o, AT[2][:, 2 * (h % 2) + h // 2, :], z_ig[:, 0, h * HD:(h + 1) * HD], start=True, stop=False)
                            i = M.matmul(o, AT[h % 2][:, 2 * (h // 2) + t, :], z_ig[:, t, h * HD:(h + 1) * HD], start=t == 0, stop=True)
                    i.then_inc(sem["b_o"], 1)

                def c_latents():
                    pe.wait_ge(sem["c_n"], at("c_n", l, 1))
                    pe.wait_ge(sem["prob"], at("prob", l, 1))
                    transposes(wk[:, 1, :], [z_c[:, t, c * P:(c + 1) * P] for c in range(2) for t in range(T)], sem["c_T"])
                    transposes(wk[:, 2, :], [z_c[:, t, C_Q:C_Q + C_KV] for t in range(T)], sem["c_T"])

                def first_scores():
                    pe.wait_ge(sem["ad_sb"], at("ad_sb", l, 2))
                    pe.wait_ge(sem["d_x"], at("d_x", l, 1))
                    pe.wait_ge(sem["b_at"], at("b_at", l, 2 * (LEVELS + 1)))
                    scores(0, BR_D)

                def c_transposes():
                    pe.wait_ge(sem["c_n2"], at("c_n2", l, 1))
                    pe.wait_ge(sem["yT_lo"], at("yT_lo", l, 3))
                    for n, (a, h) in enumerate(((c_q, 0), (c_q, 2), (c_k, 0), (c_k, 2))):
                        transposes(wk[:, n, :], [a[:, 4 * t + hh, :] for hh in (h, h + 1) for t in range(T)],
                                   sem["c_T2"])

                gate_first(0)
                decayed_level(7)
                ad_transposes(1, z_a[:, :, 0:BW], kdup)
                gate_rest(0)
                b_cross()
                first_scores()
                gate_first(1)
                b_out()
                c_latents()
                gate_rest(1)
                pe.wait_ge(sem["c_lo"], at("c_lo", l, 1))
                p_transposes(0)
                pe.wait_ge(sem["prob"], at("prob", l, 1))
                scores(1, BR_D)

                gate_first(2)
                pe.wait_ge(sem["b_y"], at("b_y", l, 1))
                weighted(0, dv)
                gate_rest(2)
                p_transposes(1)
                pe.wait_ge(sem["prob"], at("prob", l, 2))
                scores(2, BR_A)

                gate_first(3)
                weighted(1, dv)
                y_transposes(0)
                gate_rest(3)
                pe.wait_ge(sem["yT_lo"], at("yT_lo", l, 1))
                p_transposes(2)
                pe.wait_ge(sem["prob"], at("prob", l, 3))
                scores(3, BR_A)
                pe.wait_ge(sem["c_lo"], at("c_lo", l, 1))
                pe.wait_ge(sem["gate"], at("gate", l, 6))
                chunk(UQ, [(acc[:, t, :], H * C_DQ,
                            [(cT_hi[:, k, t, :], cT_lo[:, k, t, :], k * H * C_DQ) for k in range(2)], True, True)
                           for t in range(T)])
                weighted(2, av)
                pe.wait_ge(sem["y"], at("y", l, 2))
                pe.wait_ge(sem["pT_sb"], at("pT_sb", l, PT_DONE[2]))
                y_transposes(1)
                pe.wait_ge(sem["gate"], at("gate", l, 8))
                chunk(UKV, [(acc[:, 2 + t, :], 512, [(cT_hi[:, 2, t, :], cT_lo[:, 2, t, :], 0)], True, True)
                            for t in range(T)])
                pe.wait_ge(sem["yT_lo"], at("yT_lo", l, 2))
                p_transposes(3)
                project(0)
                weighted(3, av)
                gate_first(4)
                gate_rest(4)
                pe.wait_ge(sem["y"], at("y", l, 4))
                y_transposes(2)
                gate_first(5)
                c_transposes()
                gate_rest(5)
                pe.wait_ge(sem["c_sb2"], at("c_sb2", l, 4))
                scores(4, BR_C)
                project(1)
                p_transposes(4)
                scores(5, BR_C)
                gate_first(6)
                weighted(4, cv)
                gate_rest(6)
                p_transposes(5)
                gate_first(7)
                weighted(5, cv)
                gate_rest(7)
                pe.wait_ge(sem["y"], at("y", l, 6))
                y_transposes(3)
                project(2)
                project(3)

                pe.wait_ge(sem["merge"], at("merge", l, 16))
                x_transposes(merged)
                for half in range(2):
                    for h in range(2):
                        pe.wait_ge(sem["xT_lo"], at("xT_lo", l, 8))
                        chunk(OUT0 + 2 * half + h,
                              [(acc[:, 2 * half + t, :], 512,
                                [(xT_hi[:, t, 4 * h + k, :], xT_lo[:, t, 4 * h + k, :], k * 512) for k in range(4)],
                                h == 0, h == 1) for t in range(T)])

                for t in range(T):
                    pe.wait_ge(sem["xn"], at("xn", l, T + t + 1))
                x_transposes(xn)
                pe.wait_ge(sem["xT_lo"], at("xT_lo", l, 12))
                half_block(FFN0, 512, 0, 0)
                half_block(FFN0, 512, 0, 1)

                def act_transposes(b, i):
                    pe.wait_ge(sem["act"], at("act", l, i * 4 + (2 * b + 2)))
                    transposes(wk[:, b % 2, :], [act[:, b % 2, t, c * P:(c + 1) * P] for c in range(2) for t in range(T)], sem["aT"])

                with pe.Fori(0, FFN_BLOCKS // 2) as i:
                    for b in (1, 2):
                        if b == 2:
                            pe.wait_ge(sem["act"], at("act", l, i * 4 + 2))
                        else:
                            pe.wait_ge(sem["act"], at("act", l, i * 4))
                        half_block(FFN0 + 2 * b, 512, b % 2, 0, off=i * 4)
                        half_block(FFN0 + 2 * b, 512, b % 2, 1, off=i * 4)
                        pe.wait_ge(sem["aT_lo"], at("aT_lo", l, i * 2 + (b - 2) if b == 2 else i * 2))
                        act_transposes(b - 1, i)
                for half in range(2):
                    for n in range(DOWN_CHUNKS):
                        c = DOWN0 + half * DOWN_CHUNKS + n
                        tiles = range(4 * n, min(4 * n + 4, FF_TILES))
                        if half == 0:
                            pe.wait_ge(sem["aT_lo"], at("aT_lo", l, min(2 * n + 2, FFN_BLOCKS)))
                            if n == 0:
                                pe.wait_ge(sem["act"], at("act", l, 2 * FFN_BLOCKS))
                        chunk(c, [(acc[:, 2 * half + t, :], 512,
                                   [(aT_hi[:, k * SEQ + t * P:k * SEQ + (t + 1) * P], aT_lo[:, k * SEQ + t * P:k * SEQ + (t + 1) * P],
                                     (k - 4 * n) * 512) for k in tiles], n == 0, n == DOWN_CHUNKS - 1) for t in range(T)])
                        if c == DOWN0:
                            pe.wait_ge(sem["aT_lo"], at("aT_lo", l, FFN_BLOCKS - 2))
                            act_transposes(FFN_BLOCKS - 1, 0)


def stream_layout(w_in, w_branch, w_out, w_ffn_in, w_ffn_out, c_w_uq, c_w_ukv, np):
    out = np.zeros((DEPTH, CHUNKS, P, CW), np.float32)

    def rows(w, first, n):
        return w[first * P:(first + n) * P].reshape(n, P, -1).transpose(1, 0, 2).reshape(P, -1)

    for l in range(DEPTH):
        def put(c, a):
            out[l, c, :, :a.shape[1]] = a

        def halves(c, w):
            put(c, rows(w, 0, 4))
            put(c + 1, rows(w, 4, 4))

        for b, (col, n) in enumerate(Z_BLOCKS):
            halves(2 * b, w_in[l][:, col:col + n])
        for n, br in enumerate(MERGE_ORDER):
            for h in range(2):
                col = OFF_G + br * D + h * 512
                halves(GATE0[n] + 2 * h, w_in[l][:, col:col + 512])
            put(PROJ[n], rows(w_branch[l, br], 0, 2))
        put(UQ, rows(c_w_uq[l], 0, 2))
        put(UKV, rows(c_w_ukv[l], 0, 1))
        for h in range(2):
            halves(OUT0 + 2 * h, w_out[l][:, h * 512:h * 512 + 512])
        for b in range(FFN_BLOCKS):
            g = w_ffn_in[l][:, b * 256:b * 256 + 256]
            u = w_ffn_in[l][:, D_FF + b * 256:D_FF + b * 256 + 256]
            halves(FFN0 + 2 * b, np.concatenate([g, u], axis=1))
        for h in range(2):
            for n in range(DOWN_CHUNKS):
                k = min(4, FF_TILES - 4 * n)
                put(DOWN0 + h * DOWN_CHUNKS + n, rows(w_ffn_out[l][:, h * 512:h * 512 + 512], 4 * n, k))
    return out.reshape(DEPTH * CHUNKS, P, CW)


def constants(np):
    i = np.arange(P)
    row, col = i[:, None], i[None, :]
    const = np.zeros((P, CONST_N), np.float32)

    def put(name, a):
        col, n = CONST[name]
        const[:, col:col + n] = a

    put("ident", row == col)
    put("tri", row <= col)
    put("stri", col < row)
    put("ones", 1.0)
    put("half", -0.5)
    half = C_ROPE // 2
    inv = np.exp(np.float32(-np.log(10000.0)) * np.arange(half, dtype=np.float32) / np.float32(half))
    ang = (np.arange(T)[None, :, None] * P + i[:, None, None]).astype(np.float32) * inv.astype(np.float32)
    put("cos", np.concatenate([np.cos(ang), np.cos(ang)], axis=-1).reshape(P, -1))
    put("sin", np.concatenate([-np.sin(ang), np.sin(ang)], axis=-1).reshape(P, -1))
    mask = np.zeros((P, MASK_N), np.float32)
    masks = {"ident": row == col, "causal": np.where(col <= row, 0.0, NEG),
             "chunk": np.where(col // CHUNK <= row // CHUNK, 0.0, NEG),
             "window": np.where((row < CHUNK) & (col >= CHUNK), 0.0, NEG)}
    for name, a in masks.items():
        first, n = MASKS[name]
        mask[:, first:first + n] = a
    level = np.zeros((P, LEVELS * P), np.float32)
    for j in range(LEVELS):
        m = 2 ** j
        level[:, j * P:(j + 1) * P] = (row // (2 * m) == col // (2 * m)) & (row % (2 * m) < m) & (col % (2 * m) >= m)
    return const, mask, level


def parameters(v, np):
    par = np.zeros((P, DEPTH, PAR_IN), np.float32)

    def put(name, l, a):
        col, n = PAR[name]
        par[:, l, col:col + n] = a

    for l in range(DEPTH):
        put("mix", l, v["norm_mix_g"][l].reshape(DK, P).T)
        put("ffn", l, v["norm_ffn_g"][l].reshape(DK, P).T)
        put("cq", l, v["c_cq_norm_g"][l].reshape(2, P).T)
        put("ckv", l, v["c_ckv_norm_g"][l].reshape(1, P).T)
        for name, key in (("aq", "a_q_norm_g"), ("ak", "a_k_norm_g"), ("dq", "d_q_norm_g"), ("dk", "d_k_norm_g")):
            put(name, l, np.concatenate([v[key][l]] * 2)[:, None])
        put("lb", l, v["hgrn_lb_logits"][l].reshape(2, P).T)
        for name, key in (("bo", "b_o_norm_g"), ("cqn", "c_q_norm_g"), ("ckn", "c_k_norm_g"), ("sink", "a_sinks"),
                          ("fb", "d_f_bias")):
            put(name, l, v[key][l][None, :])
    return par


def kernel(**inputs):
    import numpy as np
    import concourse.bacc as bacc
    from concourse.bass_utils import run_bass_kernel_spmd

    v = {k: np.asarray(a) for k, a in inputs.items()}
    const, mask, level = constants(np)
    arrays = {
        "in_x": np.ascontiguousarray(v["x"].reshape(T, P, D).transpose(1, 0, 2)),
        "in_stream": stream_layout(v["w_in"], v["w_branch"], v["w_out"], v["w_ffn_in"], v["w_ffn_out"], v["c_w_uq"],
                                   v["c_w_ukv"], np),
        "in_par": parameters(v, np), "in_const": const, "in_mask": mask, "in_level": level,
    }
    nc = bacc.Bacc("TRN2", target_bir_lowering=False, num_devices=1)
    args = [nc.dram_tensor(n, a.shape, mybir.dt.from_np(a.dtype), kind="ExternalInput").ap() for n, a in arrays.items()]
    out = nc.dram_tensor("out_x", (P, T, D), F32, kind="ExternalOutput").ap()
    trunk(nc, *args, out)
    r = run_bass_kernel_spmd(nc, [arrays], core_ids=[0])
    return r.results[0]["out_x"].transpose(1, 0, 2).reshape(1, SEQ, D)
```

```python
from contextlib import ExitStack

import concourse.bass as bass
from concourse import mybir

F32 = mybir.dt.float32
F32R = mybir.dt.float32r
BF16 = mybir.dt.bfloat16
U8 = mybir.dt.uint8
ALU = mybir.AluOpType
ACT = mybir.ActivationFunctionType
AX = mybir.AxisListType

P = 128
SEQ = 256
T = SEQ // P
D = 1024
DK = D // P
DEPTH = 2
CHUNK = 64
H = 4
HD = 64
A_KV = 2
C_Q, C_KV, C_ROPE, C_DQ = 256, 128, 32, 96
D_FF = 2816
FFN_BLOCKS = D_FF // 256
FF_TILES = D_FF // P
BW = H * HD
EPS = 1e-6
NEG = -1e30

OFF_A, OFF_B, OFF_C, OFF_D, OFF_G = 0, 512, 1536, 1952, 2724
Z_BLOCKS = [
    (OFF_B, 512),
    (OFF_D + 512, 260),
    (OFF_B + 512, 512),
    (OFF_D, 512),
    (OFF_A, 512),
    (OFF_C, 416),
]
BR_A, BR_B, BR_C, BR_D = 0, 1, 2, 3
MERGE_ORDER = [BR_B, BR_D, BR_A, BR_C]

CW = 2048
Z0 = 0
GATE = [(12, 14), (16, 18), (23, 25), (28, 31)]
UQ, UKV = 20, 21
PROJ = [22, 27, 30, 33]
PROJ_HALVES = [(0, 1), (0, 1), (1, 0), (0, 1)]
OUT0 = 34
FFN0 = 38
DOWN0 = FFN0 + 2 * FFN_BLOCKS
DOWN_CHUNKS = -(-FF_TILES // 4)
CHUNKS = DOWN0 + 2 * DOWN_CHUNKS
RAW, RING = 2, 4
AHEAD = 2
assert CHUNKS % RING == 0 and FFN_BLOCKS % 2 == 1 and (FFN0 + 2) % RING == 0

PAR_COLS = [("mix", DK), ("ffn", DK), ("cq", 2), ("ckv", 1), ("aq", 1), ("ak", 1), ("dq", 1), ("dk", 1),
            ("lb", 2), ("bo", HD), ("cqn", C_DQ), ("ckn", C_DQ), ("sink", H), ("fb", H)]
DERIVED = [("low", 2), ("oml", 2), ("ga", 1), ("gd", 1)]


def columns(spec):
    first, out = 0, {}
    for name, n in spec:
        out[name] = (first, n)
        first += n
    return out, first


PAR, PAR_IN = columns(PAR_COLS)
PARX, PAR_N = columns(PAR_COLS + DERIVED)

CONST, CONST_N = columns([("ident", P), ("tri", P), ("stri", P), ("ones", P), ("cos", T * C_ROPE), ("sin", T * C_ROPE),
                          ("half", 16)])
MASKS, MASK_N = columns([("ident", P), ("causal", P), ("chunk", P), ("window", P)])
LEVELS = 7

NORM1, NORM_D, NORM_A, NORM_C1, NORM_B, NORM_C2, NORM2 = range(7)
NORM_WIDTH = [T, 16, 12, 2 * T, 8, 16, T]
NORM_AT = [sum(NORM_WIDTH[:i]) for i in range(7)]
NORM_N = sum(NORM_WIDTH)


SETUP = 12
GATE_AFTER = [2, 4, 6, 10]
PT_DONE = [1, 3, 4, 6, 7, 9]
LINKS = 50


def width(c):
    c %= CHUNKS
    if c < 2 * len(Z_BLOCKS):
        return 4 * Z_BLOCKS[c // 2][1]
    if c == UQ:
        return 2 * H * C_DQ
    if c == UKV:
        return H * 2 * HD
    if c >= DOWN0 and (c - DOWN0) % DOWN_CHUNKS == DOWN_CHUNKS - 1:
        return (FF_TILES - 4 * (DOWN_CHUNKS - 1)) * 512
    return CW


SIGNALS = dict(
    hi=CHUNKS, lo=CHUNKS, mm=CHUNKS, par=1, dve=LINKS,
    mixg=1, sumsq=2 * T, mean=7, rstd=7, tok=2,
    xT=6 * T, xT_hi=6 * T, xT_lo=6 * T,
    z=T * len(Z_BLOCKS), gate=4 * 2 * T, u=2 * T, proj=4, merge=4 * 2 * T, xmid=2 * T, xout=2 * T,
    b_in=2, b_e=1, b_tq=1, b_f=1, b_q=1, b_ln=1, b_scan=1, b_d=LEVELS, b_abs=LEVELS, b_E=LEVELS,
    b_QK=LEVELS + 1, b_lev=2 * (LEVELS + 1), b_at=2 * (LEVELS + 1), b_Ex=1, b_cross=2, b_atx=2, b_o=1, b_sq=1, b_tg=1,
    b_y=1,
    d_zf=1, d_abs=1, d_e=1, d_ln=1, d_lf=1, d_x=1, ad_sq=2, ad_n=2, ad_T=4, ad_sb=4,
    c_sq=1, c_n=1, c_T=2, c_hi=1, c_lo=1, c_sq2=1, c_n2=1, c_T2=4, c_sb2=4,
    score=6, top=6, prob=6, pT=9, pT_sb=9, pv=6, y=6, yT=4, yT_hi=4, yT_lo=4,
    tanh=2 * FFN_BLOCKS, act=2 * FFN_BLOCKS, sw=FFN_BLOCKS, aT=FFN_BLOCKS, aT_hi=FFN_BLOCKS, aT_lo=FFN_BLOCKS,
)


HEADS = dict(mm=RING, mixg=1, xT=T, xT_hi=T, xT_lo=T, xout=1, act=1, aT=1, aT_lo=1)


def at(name, layer, k):
    return layer * SIGNALS[name] + ((HEADS[name] if name in HEADS else 0) + k)


def trunk(nc, x_in, stream, par_in, const_in, mask_in, level_in, out):
    ctx = ExitStack()
    with ctx:
        def sb(name, shape, dt=F32):
            return ctx.enter_context(nc.sbuf_tensor(name, shape, dt))

        def new_sem(name):
            return ctx.enter_context(nc.semaphore(name))

        x = sb("x", [P, T, D])
        xT_hi = sb("xT_hi", [P, T, DK, P], F32R)
        xT_lo = sb("xT_lo", [P, T, DK, P], F32R)
        raw = sb("raw", [P, RAW, CW])
        w_hi = sb("w_hi", [P, RING, CW], F32R)
        w_lo = sb("w_lo", [P, RING, CW], F32R)
        par = sb("par", [P, DEPTH + 1, PAR_N])
        now = sb("now", [P, PAR_N])
        mixg = sb("mixg", [P, DK])
        tok = sb("tok", [P, 3, T])
        const = sb("const", [P, CONST_N])
        mask = sb("mask", [P, MASK_N], BF16)
        level = sb("level", [P, LEVELS, P], U8)
        stat = sb("stat", [P, 3, NORM_N])
        small = sb("small", [P, 128])
        dsm = sb("dsm", [P, 5, 2 * H])

        with ExitStack() as attention:
            gates = attention.enter_context(nc.sbuf_tensor("gates", [P, 2, T, D], F32))
            yT_hi = attention.enter_context(nc.sbuf_tensor("yT_hi", [P, 2, 2, T, P], F32R))
            yT_lo = attention.enter_context(nc.sbuf_tensor("yT_lo", [P, 2, 2, T, P], F32R))
            cT_hi = attention.enter_context(nc.sbuf_tensor("cT_hi", [P, 3, T, P], F32R))
            cT_lo = attention.enter_context(nc.sbuf_tensor("cT_lo", [P, 3, T, P], F32R))
            AREA = [("wide", 2 * D), ("zqf", 1024), ("zdv", T * 260), ("zc", T * 416), ("qkT", 2048), ("prob", 1024),
                    ("pT", 1024), ("y", 1024), ("kdup", 512), ("X", 1024)]
            area, area_n = columns(AREA)
            arena = attention.enter_context(nc.sbuf_tensor("arena", [P, area_n], F32))
            with ExitStack() as scans:
                b_area = scans.enter_context(nc.sbuf_tensor("b_area", [P, 4608], F32))
            with ExitStack() as merging:
                mT_hi = merging.enter_context(nc.sbuf_tensor("mT_hi", [P, T, DK, P], F32R))
                mT_lo = merging.enter_context(nc.sbuf_tensor("mT_lo", [P, T, DK, P], F32R))
        with ExitStack() as ffn:
            keep_x_normed = ffn.enter_context(nc.sbuf_tensor("keep_gates", [P, 2, T, D], F32))
            aT_hi = ffn.enter_context(nc.sbuf_tensor("aT_hi", [P, FF_TILES * SEQ], F32R))
            aT_lo = ffn.enter_context(nc.sbuf_tensor("aT_lo", [P, FF_TILES * SEQ], F32R))
        del keep_x_normed

        def region(name, first=0, n=None):
            col, size = area[name]
            return arena[:, col + first:col + (size if n is None else first + n)]

        wide = region("wide")
        merged = wide.rearrange("p (t d) -> p t d", t=T)
        z_ig = region("wide", 0, 1024).rearrange("p (t c) -> p t c", t=T)
        z_dqk = region("wide", 1024, 1024).rearrange("p (t c) -> p t c", t=T)
        z_qf = region("zqf").rearrange("p (t c) -> p t c", t=T)
        z_a = z_qf
        z_dv = region("zdv").rearrange("p (t c) -> p t c", t=T)
        z_c = region("zc").rearrange("p (t c) -> p t c", t=T)
        z_of = [z_qf, z_dv, z_ig, z_dqk, z_a, z_c]
        prob = region("prob").rearrange("p (h k s) -> p h k s", k=T, h=H)
        pT = region("pT").rearrange("p (k h s) -> p k h s", k=T, h=H)
        y = region("y").rearrange("p (b t c) -> p b t c", b=2, t=T)
        kdup = region("kdup").rearrange("p (t c) -> p t c", t=T)
        X = region("X").rearrange("p (t h s) -> p t h s", t=T, h=H)
        bq, bk, bT, bE, bQ, bK = (b_area[:, 512 * i:512 * i + 512] for i in range(6))
        AT = [b_area[:, 3072 + 512 * i:3584 + 512 * i].rearrange("p (h s) -> p h s", h=H) for i in range(3)]
        c_q = b_area[:, 0:768].rearrange("p (g c) -> p g c", c=C_DQ)
        c_k = b_area[:, 768:1536].rearrange("p (g c) -> p g c", c=C_DQ)
        c_kv = b_area[:, 1536:2560].rearrange("p (g c) -> p g c", c=2 * HD)
        c_s = b_area[:, 2560:3328]
        c_s2 = b_area[:, 3328:3840]
        c_r = b_area[:, 3840:4352]
        staged = b_area[:, 0:MASK_N + LEVELS * P]
        square = region("prob")
        junk = region("y", 0, 768)

        act = gates[:, 0, :, :].rearrange("p a b -> p (a b)")[:, 0:1024].rearrange("p (b t c) -> p b t c", b=2, t=T)
        sw = gates[:, 1, :, :].rearrange("p a b -> p (a b)")[:, 0:1024].rearrange("p (b t c) -> p b t c", b=2, t=T)

        acc = ctx.enter_context(nc.psum_tensor("acc", [P, 4, 512], F32))
        wk = ctx.enter_context(nc.psum_tensor("wk", [P, 4, 512], F32))

        raw_loaded = [new_sem(f"raw_loaded{i}") for i in range(RAW)]
        loaded = {n: new_sem(f"loaded_{n}") for n in ("x0", "x1", "par", "const", "mask", "level")}
        stored = new_sem("stored")
        setup = new_sem("setup")
        sem = {n: new_sem(f"s_{n}") for n in SIGNALS}

        def p_(name):
            col, n = PARX[name]
            return now[:, col:col + n]

        def c_(name, rows=P):
            col, n = CONST[name]
            return const[0:rows, col:col + n]

        def m_(name):
            col, n = MASKS[name]
            return mask[:, col:col + n]

        def norm(which, row):
            return stat[:, row, NORM_AT[which]:NORM_AT[which] + NORM_WIDTH[which]]

        mx, negm, rowsum, rden, esink = (small[:, 24 * i:24 * i + 24] for i in range(5))
        lf = dsm[:, 0, :]

        block = ctx.enter_context(nc.Block())

        @block.sync
        def _(sp):
            sp.dma_start(x[:, :, 0:512], x_in[:, :, 0:512]).then_inc(loaded["x0"], 16)
            sp.dma_start(x[:, :, 512:1024], x_in[:, :, 512:1024]).then_inc(loaded["x1"], 16)
            for slot in range(RAW):
                sp.dma_start(raw[:, slot, :], stream[slot]).then_inc(raw_loaded[slot], 16)
            with sp.Fori(0, DEPTH * CHUNKS // RAW - 1) as i:
                for slot in range(RAW):
                    sp.wait_ge(sem["lo"], i * RAW + (slot + 1))
                    sp.dma_start(raw[:, slot, :],
                                 stream[bass.ds(i * RAW + (RAW + slot), 1), :, :].rearrange("a p n -> (a p) n"))\
                        .then_inc(raw_loaded[slot], 16)
            for slot in range(AHEAD):
                sp.wait_ge(sem["lo"], DEPTH * CHUNKS - RAW + slot + 1)
                sp.dma_start(raw[:, slot, :], stream[slot]).then_inc(raw_loaded[slot], 16)
            sp.wait_ge(sem["xout"], at("xout", DEPTH - 1, T))
            sp.dma_start(out[:, :, 0:512], x[:, :, 0:512]).then_inc(stored, 16)
            sp.wait_ge(sem["xout"], at("xout", DEPTH - 1, 2 * T))
            sp.dma_start(out[:, :, 512:1024], x[:, :, 512:1024]).then_inc(stored, 16)
            sp.wait_ge(stored, 32)

        @block.gpsimd
        def _(pool):
            pool.wait_ge(loaded["const"], 16)
            with pool.Fori(0, DEPTH) as l:
                for which in range(7):
                    pool.wait_ge(sem["mean"], at("mean", l, which + 1))
                    nc.gpsimd.tensor_tensor(norm(which, 2), norm(which, 1), c_("half")[:, 0:NORM_WIDTH[which]],
                                            ALU.pow).then_inc(sem["rstd"], 1)

        @block.scalar
        def _(act_e):
            e = act_e
            e.dma_start(const[:, :], const_in).then_inc(loaded["const"], 16)
            e.dma_start(par[:, 0:DEPTH, 0:PAR_IN], par_in).then_inc(loaded["par"], 16)
            e.dma_start(staged[:, 0:MASK_N], mask_in).then_inc(loaded["mask"], 16)
            e.dma_start(staged[:, MASK_N:MASK_N + LEVELS * P], level_in).then_inc(loaded["level"], 16)

            def split_chunk(c, l):
                e.wait_ge(sem["mm"], at("mm", l, c - (RING - 1)))
                e.wait_ge(raw_loaded[c % RAW], (l * (CHUNKS // RAW) + (c // RAW + 1)) * 16)
                n = width(c)
                nc.scalar.activation(w_hi[:, c % RING, 0:n], raw[:, c % RAW, 0:n], ACT.Copy).then_inc(sem["hi"], 1)

            def transpose_hi(l, k, h, bank, gain):
                for t in range(T):
                    e.wait_ge(sem["xT"], at("xT", l, k * T + t + 1))
                    for j in range(4):
                        col = 4 * h + j
                        i = nc.scalar.activation(xT_hi[:, t, col, :], wk[:, bank + t, j * P:(j + 1) * P], ACT.Copy,
                                                 scale=gain[:, col:col + 1])
                    i.then_inc(sem["xT_hi"], 1)

            e.wait_ge(setup, 2)
            nc.scalar.activation(small[:, 8:12], small[:, 4:8], ACT.Exp).then_inc(setup, 1)
            e.wait_ge(sem["mixg"], at("mixg", 0, 0))
            transpose_hi(0, -1, 0, 2, mixg)
            for c in range(AHEAD):
                split_chunk(c, 0)

            with e.Fori(0, DEPTH) as l:
                split = [AHEAD]

                def split_to(p):
                    while split[0] < min(p + RING, CHUNKS + AHEAD):
                        split_chunk(split[0], l)
                        split[0] += 1

                def merged_hi(h):
                    for t in range(T):
                        e.wait_ge(sem["xT"], at("xT", l, (1 + h) * T + t + 1))
                        nc.scalar.activation(mT_hi[:, t, 4 * h:4 * h + 4, :].rearrange("p k s -> p (k s)"),
                                             wk[:, 2 * h + t, :], ACT.Copy, scale=0.5).then_inc(sem["xT_hi"], 1)

                def evacuate_z(b):
                    e.wait_ge(sem["mm"], at("mm", l, 2 * b + 2))
                    for t in range(T):
                        n = Z_BLOCKS[b][1]
                        nc.scalar.activation(z_of[b][:, t, 0:n], acc[:, 2 * (b % 2) + t, 0:n], ACT.Copy,
                                             scale=norm(NORM1, 2)[:, t:t + 1])\
                            .then_inc(sem["z"], 1)

                def gate_tanh(g):
                    branch, half = g // 2, g % 2
                    e.wait_ge(sem["mm"], at("mm", l, GATE[branch][half] + 2))
                    if branch >= 2:
                        e.wait_ge(sem["merge"], at("merge", l, 4 * (branch - 2) + T * (half + 1)))
                    for t in range(T):
                        nc.scalar.activation(gates[:, branch % 2, t, half * 512:half * 512 + 512],
                                             acc[:, 2 * half + t, :], ACT.Tanh, scale=tok[:, 0, t:t + 1])\
                            .then_inc(sem["gate"], 1)

                def exps(u, scale):
                    t = u % 2
                    e.wait_ge(sem["top"], at("top", l, u + 1))
                    if u:
                        e.wait_ge(sem["pT"], at("pT", l, PT_DONE[u - 1]))
                    if u // 2 == 1:
                        c = slice(4 * u, 4 * u + 4)
                        nc.scalar.activation(esink[:, c], esink[:, c], ACT.Exp)
                    for h in range(H):
                        col = (h // 2) * SEQ
                        i = nc.scalar.activation(prob[:, h, 0:t + 1, :].rearrange("p k s -> p (k s)"),
                                                 wk[:, h % 2, col:col + (t + 1) * P], ACT.Exp,
                                                 bias=negm[:, 4 * u + h:4 * u + h + 1], scale=scale,
                                                 accum_out=rowsum[:, 4 * u + h:4 * u + h + 1])
                    i.then_inc(sem["prob"], 1)

                def pT_copy(u):
                    if u:
                        e.wait_ge(sem["pv"], at("pv", l, u))
                    for k in range(u % 2 + 1):
                        n = (PT_DONE[u - 1] if u else 0) + k + 1
                        e.wait_ge(sem["pT"], at("pT", l, n))
                        nc.scalar.activation(pT[:, k, :, :].rearrange("p h s -> p (h s)"), wk[:, 2 + k, :], ACT.Copy)\
                            .then_inc(sem["pT_sb"], 1)

                def yT_hi_copy(n):
                    e.wait_ge(sem["yT"], at("yT", l, n + 1))
                    if n >= 2:
                        e.wait_ge(sem["mm"], at("mm", l, PROJ[n - 2] + 1))
                    nc.scalar.activation(yT_hi[:, n % 2].rearrange("p c t s -> p (c t s)"), wk[:, 2, :], ACT.Copy)\
                        .then_inc(sem["yT_hi"], 1)

                def squares(first):
                    for t in range(T):
                        nc.scalar.activation(wide[:, t * D:(t + 1) * D], x[:, t, :], ACT.Square,
                                             accum_out=norm(first, 0)[:, t:t + 1]).then_inc(sem["sumsq"], 1)

                transpose_hi(l, 0, 1, 0, mixg)
                split_to(-1)
                e.wait_ge(sem["xout"], at("xout", l, 0))
                squares(NORM1)
                split_to(1)
                e.wait_ge(sem["rstd"], at("rstd", l, NORM1 + 1))
                evacuate_z(0)
                split_to(2)
                e.wait_ge(sem["b_in"], at("b_in", l, 2))
                nc.scalar.activation(bE, wk[:, 1, :], ACT.Exp, scale=-1.0).then_inc(sem["b_e"], 1)
                nc.scalar.activation(bQ, wk[:, 0, :], ACT.Tanh, scale=0.5).then_inc(sem["b_tq"], 1)
                split_to(3)
                evacuate_z(1)
                e.wait_ge(sem["d_zf"], at("d_zf", l, 1))
                nc.scalar.activation(dsm[:, 1, :], lf, ACT.Abs).then_inc(sem["d_abs"], 1)
                e.wait_ge(sem["d_abs"], at("d_abs", l, 1))
                nc.scalar.activation(dsm[:, 2, :], dsm[:, 1, :], ACT.Exp, scale=-1.0).then_inc(sem["d_e"], 1)
                e.wait_ge(sem["d_e"], at("d_e", l, 1))
                nc.scalar.activation(dsm[:, 3, :], dsm[:, 2, :], ACT.Ln, bias=1.0).then_inc(sem["d_ln"], 1)
                e.wait_ge(sem["b_f"], at("b_f", l, 1))
                nc.scalar.activation(bK, bK, ACT.Ln).then_inc(sem["b_ln"], 1)

                def level_exp(j):
                    e.wait_ge(sem["b_d"], at("b_d", l, j))
                    nc.scalar.activation(bE, bE, ACT.Abs).then_inc(sem["b_abs"], 1)
                    e.wait_ge(sem["b_abs"], at("b_abs", l, j))
                    nc.scalar.activation(bE, bE, ACT.Exp, scale=-1.0).then_inc(sem["b_E"], 1)

                split_to(4)
                level_exp(1)
                split_to(5)
                evacuate_z(2)
                level_exp(2)
                split_to(6)
                level_exp(3)
                split_to(7)
                evacuate_z(3)
                e.wait_ge(sem["z"], at("z", l, 8))
                nc.scalar.activation(square[:, 0:1024], region("wide", 1024, 1024), ACT.Square)\
                    .then_inc(sem["ad_sq"], 1)
                level_exp(4)
                split_to(8)
                level_exp(5)
                split_to(9)
                evacuate_z(4)
                e.wait_ge(sem["z"], at("z", l, 10))
                e.wait_ge(sem["mean"], at("mean", l, NORM_D + 1))
                nc.scalar.activation(square[:, 0:768].rearrange("p (t c) -> p t c", t=T), z_a[:, :, 0:384], ACT.Square)\
                    .then_inc(sem["ad_sq"], 1)
                level_exp(6)
                split_to(10)
                level_exp(7)
                e.wait_ge(sem["par"], at("par", l, 1))
                e.wait_ge(sem["ad_T"], at("ad_T", l, 1))
                nc.scalar.activation(region("qkT", 0, 512), wk[:, 2, :], ACT.Copy).then_inc(sem["ad_sb"], 1)
                e.wait_ge(sem["ad_T"], at("ad_T", l, 2))
                nc.scalar.activation(region("qkT", 512, 512), wk[:, 3, :], ACT.Copy, scale=p_("gd"))\
                    .then_inc(sem["ad_sb"], 1)
                split_to(11)
                evacuate_z(5)
                e.wait_ge(sem["z"], at("z", l, 12))
                for t in range(T):
                    nc.scalar.activation(junk[:, t * C_Q:(t + 1) * C_Q], z_c[:, t, 0:C_Q], ACT.Square,
                                         accum_out=norm(NORM_C1, 0)[:, t:t + 1])
                for t in range(T):
                    i = nc.scalar.activation(junk[:, (4 + t) * C_KV:(5 + t) * C_KV], z_c[:, t, C_Q:C_Q + C_KV], ACT.Square,
                                             accum_out=norm(NORM_C1, 0)[:, T + t:T + t + 1])
                i.then_inc(sem["c_sq"], 1)
                e.wait_ge(sem["b_QK"], at("b_QK", l, LEVELS))
                for hp in range(2):
                    nc.scalar.activation(bE[:, hp * SEQ:hp * SEQ + P], bT[:, hp * SEQ:hp * SEQ + P], ACT.Exp,
                                         scale=-1.0, bias=bT[:, hp * SEQ + P - 1:hp * SEQ + P])
                    i = nc.scalar.activation(bE[:, hp * SEQ + P:(hp + 1) * SEQ], bT[:, hp * SEQ + P:(hp + 1) * SEQ],
                                             ACT.Exp)
                i.then_inc(sem["b_Ex"], 1)
                split_to(12)
                e.wait_ge(sem["ad_T"], at("ad_T", l, 3))
                nc.scalar.activation(region("qkT", 1024, 512), wk[:, 2, :], ACT.Copy).then_inc(sem["ad_sb"], 1)
                e.wait_ge(sem["ad_T"], at("ad_T", l, 4))
                nc.scalar.activation(region("qkT", 1536, 512), wk[:, 3, :], ACT.Copy, scale=p_("ga"))\
                    .then_inc(sem["ad_sb"], 1)
                split_to(13)
                for odd in range(2):
                    e.wait_ge(sem["b_cross"], at("b_cross", l, odd + 1))
                    nc.scalar.activation(AT[2][:, 2 * odd:2 * odd + 2, :].rearrange("p h s -> p (h s)"),
                                         wk[:, 2 + odd, 0:2 * P], ACT.Copy).then_inc(sem["b_atx"], 1)
                e.wait_ge(sem["tok"], at("tok", l, 1))
                gate_tanh(0)
                exps(0, 1.0)
                split_to(14)
                e.wait_ge(sem["c_T"], at("c_T", l, 2))
                for k in range(2):
                    nc.scalar.activation(cT_hi[:, k].rearrange("p t s -> p (t s)"), wk[:, 1, k * SEQ:(k + 1) * SEQ],
                                         ACT.Copy, scale=p_("cq")[:, k:k + 1])
                nc.scalar.activation(cT_hi[:, 2].rearrange("p t s -> p (t s)"), wk[:, 2, 0:SEQ], ACT.Copy,
                                     scale=p_("ckv")).then_inc(sem["c_hi"], 1)
                e.wait_ge(sem["b_o"], at("b_o", l, 1))
                e.wait_ge(sem["b_QK"], at("b_QK", l, LEVELS + 1))
                nc.scalar.activation(bE, wk[:, 3, :], ACT.Square).then_inc(sem["b_sq"], 1)
                nc.scalar.activation(bQ.rearrange("p (t c) -> p t c", t=T), z_ig[:, :, BW:2 * BW], ACT.Tanh, scale=0.5)\
                    .then_inc(sem["b_tg"], 1)
                split_to(15)
                gate_tanh(1)
                pT_copy(0)
                exps(1, 1.0)
                split_to(16)
                split_to(17)
                gate_tanh(2)
                pT_copy(1)
                exps(2, 1.0)
                split_to(18)
                yT_hi_copy(0)
                split_to(19)
                gate_tanh(3)
                pT_copy(2)
                exps(3, 1.0)
                split_to(20)
                yT_hi_copy(1)
                e.wait_ge(sem["mm"], at("mm", l, UQ + 1))
                e.wait_ge(sem["b_y"], at("b_y", l, 1))
                for t in range(T):
                    nc.scalar.activation(c_q[:, 4 * t:4 * t + 4, :].rearrange("p g c -> p (g c)"),
                                         acc[:, t, 0:H * C_DQ], ACT.Copy).then_inc(sem["u"], 1)
                split_to(21)
                e.wait_ge(sem["mm"], at("mm", l, UKV + 1))
                for t in range(T):
                    nc.scalar.activation(c_kv[:, 4 * t:4 * t + 4, :].rearrange("p g c -> p (g c)"), acc[:, 2 + t, :],
                                         ACT.Copy).then_inc(sem["u"], 1)
                pT_copy(3)
                e.wait_ge(sem["u"], at("u", l, 4))
                nc.scalar.activation(c_s.rearrange("p (g c) -> p g c", c=C_DQ), c_q, ACT.Square)
                nc.scalar.activation(c_s2.rearrange("p (g c) -> p g c", c=HD), c_kv[:, :, 0:HD], ACT.Square)
                for t in range(T):
                    i = nc.scalar.activation(c_r[:, 32 * t:32 * t + 32], z_c[:, t, 384:416], ACT.Square,
                                             accum_out=dsm[:, 4, t:t + 1])
                i.then_inc(sem["c_sq2"], 1)
                split_to(24)
                gate_tanh(4)
                yT_hi_copy(2)
                split_to(25)
                for n in range(4):
                    e.wait_ge(sem["c_T2"], at("c_T2", l, n + 1))
                    nc.scalar.activation(arena[0:C_DQ, area["qkT"][0] + 512 * n:area["qkT"][0] + 512 * n + 512],
                                         wk[0:C_DQ, n, :], ACT.Copy).then_inc(sem["c_sb2"], 1)
                split_to(26)
                gate_tanh(5)
                exps(4, C_DQ ** -0.5)
                split_to(27)
                pT_copy(4)
                exps(5, C_DQ ** -0.5)
                split_to(29)
                gate_tanh(6)
                pT_copy(5)
                split_to(31)
                yT_hi_copy(3)
                split_to(32)
                gate_tanh(7)
                split_to(33)
                merged_hi(0)
                merged_hi(1)
                split_to(36)
                transpose_hi(l, 3, 0, 0, p_("ffn"))
                split_to(37)
                transpose_hi(l, 4, 1, 2, p_("ffn"))
                e.wait_ge(sem["xmid"], at("xmid", l, 4))
                squares(NORM2)

                def ffn_split(c, i):
                    e.wait_ge(sem["mm"], at("mm", l, i * 4 + (c - (RING - 1))))
                    e.wait_ge(raw_loaded[c % RAW], (l * (CHUNKS // RAW) + i * 2 + (c // RAW + 1)) * 16)
                    nc.scalar.activation(w_hi[:, c % RING, :], raw[:, c % RAW, :], ACT.Copy).then_inc(sem["hi"], 1)

                def ffn_tanh(b, i):
                    e.wait_ge(sem["mm"], at("mm", l, i * 4 + (FFN0 + 2 * b + 2)))
                    for t in range(T):
                        nc.scalar.activation(sw[:, b % 2, t, :], acc[:, 2 * (b % 2) + t, 0:256], ACT.Tanh,
                                             scale=tok[:, 1, t:t + 1]).then_inc(sem["tanh"], 1)

                def ffn_hi(b, i):
                    e.wait_ge(sem["aT"], at("aT", l, i * 2 + (b + 1)))
                    to = aT_hi[:, b * 512:b * 512 + 512] if isinstance(i, int) else aT_hi[:, bass.ds(i * 1024 + b * 512, 512)]
                    nc.scalar.activation(to, wk[:, b % 2, :], ACT.Copy, scale=0.5).then_inc(sem["aT_hi"], 1)

                split_to(39)
                e.wait_ge(sem["tok"], at("tok", l, 2))
                ffn_tanh(0, 0)
                with e.Fori(0, FFN_BLOCKS // 2) as i:
                    for b in (1, 2):
                        ffn_split(FFN0 + 2 * b + 3, i)
                        ffn_split(FFN0 + 2 * b + 4, i)
                        ffn_tanh(b, i)
                        ffn_hi(b - 1, i)
                split[0] = DOWN0 + 3
                split_to(DOWN0)
                ffn_hi(FFN_BLOCKS - 1, 0)
                split_to(DOWN0 + DOWN_CHUNKS + 1)
                e.wait_ge(sem["mixg"], at("mixg", l, 1))
                transpose_hi(l, 5, 0, 2, mixg)
                split_to(CHUNKS)

        @block.vector
        def _(v):
            V = nc.vector
            v.wait_ge(loaded["par"], 16)
            V.tensor_copy(mixg[:, :], par[:, 0, PARX["mix"][0]:PARX["mix"][0] + DK]).then_inc(sem["mixg"], 1)
            V.memset(par[:, DEPTH, :], 1.0)
            lb = PARX["lb"][0]
            lo_, om_ = PARX["low"][0], PARX["oml"][0]
            V.tensor_tensor(small[:, 0:2], par[:, 0, lb:lb + 2], par[:, 1, lb:lb + 2], ALU.max).then_inc(setup, 1)
            v.wait_ge(setup, 1)
            V.tensor_tensor(small[:, 4:8].rearrange("p (l c) -> p l c", l=2), par[:, 0:DEPTH, lb:lb + 2],
                            small[:, 0:2][:, None, :].to_broadcast([P, 2, 2]), ALU.subtract).then_inc(setup, 1)

            def split_chunk(c, l):
                n = width(c)
                v.wait_ge(sem["hi"], at("hi", l, c + 1))
                V.tensor_tensor(w_lo[:, c % RING, 0:n], raw[:, c % RAW, 0:n], w_hi[:, c % RING, 0:n].bitcast(F32),
                                ALU.subtract).then_inc(sem["lo"], 1)

            def transpose_lo(l, k, h, bank, gain):
                for t in range(T):
                    v.wait_ge(sem["xT_hi"], at("xT_hi", l, k * T + t + 1))
                    for j in range(4):
                        col = 4 * h + j
                        i = V.scalar_tensor_tensor(xT_lo[:, t, col, :], wk[:, bank + t, j * P:(j + 1) * P],
                                                   gain[:, col:col + 1], xT_hi[:, t, col, :].bitcast(F32), ALU.mult,
                                                   ALU.subtract)
                    i.then_inc(sem["xT_lo"], 1)

            v.wait_ge(sem["mixg"], at("mixg", 0, 0))
            transpose_lo(0, -1, 0, 2, mixg)
            v.wait_ge(setup, 3)
            V.tensor_tensor(small[:, 12:14], small[:, 8:10], small[:, 10:12], ALU.add).then_inc(setup, 1)
            v.wait_ge(setup, 4)
            V.reciprocal(small[:, 14:16], small[:, 12:14]).then_inc(setup, 1)
            v.wait_ge(setup, 5)
            V.tensor_tensor(par[:, 1, lo_:lo_ + 2], small[:, 10:12], small[:, 14:16], ALU.mult).then_inc(setup, 1)
            V.memset(par[:, 0, lo_:lo_ + 2], 0.0).then_inc(setup, 1)
            v.wait_ge(setup, 7)
            V.tensor_scalar(par[:, 0:DEPTH, om_:om_ + 2], par[:, 0:DEPTH, lo_:lo_ + 2], -1.0, 1.0, ALU.mult, ALU.add)\
                .then_inc(setup, 1)
            for name, q, k in (("ga", "aq", "ak"), ("gd", "dq", "dk")):
                col = PARX[name][0]
                V.scalar_tensor_tensor(par[:, 0:DEPTH, col:col + 1], par[:, 0:DEPTH, PARX[q][0]:PARX[q][0] + 1], HD ** -0.5,
                                       par[:, 0:DEPTH, PARX[k][0]:PARX[k][0] + 1], ALU.mult, ALU.mult).then_inc(setup, 1)
            v.wait_ge(loaded["x0"], 16)
            v.wait_ge(loaded["x1"], 16)
            v.sem_inc(sem["xout"], HEADS["xout"])
            v.sem_inc(sem["act"], HEADS["act"])
            v.sem_inc(sem["aT_lo"], HEADS["aT_lo"])
            split_chunk(0, 0)
            v.wait_ge(loaded["mask"], 16)
            v.wait_ge(loaded["level"], 16)
            V.tensor_copy(level[:, :, :].rearrange("p l s -> p (l s)"), staged[:, MASK_N:MASK_N + LEVELS * P])\
                .then_inc(setup, 1)
            V.tensor_copy(mask[:, :], staged[:, 0:MASK_N]).then_inc(setup, 1)
            split_chunk(1, 0)
            v.wait_ge(setup, SETUP)
            v.wait_ge(loaded["const"], 16)

            with v.Fori(0, DEPTH) as l:
                split = [AHEAD]
                links = [0]

                def link(i):
                    i.then_inc(sem["dve"], 1)
                    links[0] += 1
                    v.wait_ge(sem["dve"], at("dve", l, links[0]))

                def split_to(p):
                    while split[0] < min(p + RING, CHUNKS + AHEAD):
                        split_chunk(split[0], l)
                        split[0] += 1

                def merged_lo(h):
                    for t in range(T):
                        v.wait_ge(sem["xT_hi"], at("xT_hi", l, (1 + h) * T + t + 1))
                        cols = slice(4 * h, 4 * h + 4)
                        V.scalar_tensor_tensor(mT_lo[:, t, cols, :].rearrange("p k s -> p (k s)"), wk[:, 2 * h + t, :], 0.5,
                                               mT_hi[:, t, cols, :].rearrange("p k s -> p (k s)").bitcast(F32),
                                               ALU.mult, ALU.subtract).then_inc(sem["xT_lo"], 1)

                def mean(which, cols, scale):
                    i = V.tensor_scalar(norm(which, 1)[:, cols], norm(which, 0)[:, cols], scale, EPS, ALU.mult, ALU.add)
                    return i

                def norm_x(n, which):
                    v.wait_ge(sem["sumsq"], at("sumsq", l, (n + 1) * T))
                    mean(which, slice(0, T), 1.0 / D).then_inc(sem["mean"], 1)

                def norm_halved(n, which):
                    v.wait_ge(sem["rstd"], at("rstd", l, which + 1))
                    if n == 1:
                        V.tensor_tensor(tok[:, 2, :], norm(which, 2), norm(which, 2), ALU.mult)
                    V.tensor_scalar(tok[:, n, :], norm(which, 2), 0.5, None, ALU.mult).then_inc(sem["tok"], 1)

                def tops(u, scale, sinks=False):
                    t = u % 2
                    c = slice(4 * u, 4 * u + 4)
                    v.wait_ge(sem["score"], at("score", l, u + 1))
                    link(V.reduce_max(mx[:, c].rearrange("p (h o) -> p h o", h=2),
                                      wk[:, 0:2, :].rearrange("p o (h m) -> p h o m", h=2)[:, :, :, 0:(t + 1) * P], axis=AX.X))
                    if sinks:
                        link(V.tensor_tensor(mx[:, c], mx[:, c], p_("sink"), ALU.max))
                        link(V.tensor_tensor(esink[:, c], p_("sink"), mx[:, c], ALU.subtract))
                    V.tensor_scalar(negm[:, c], mx[:, c], -scale, None, ALU.mult).then_inc(sem["top"], 1)

                def attended(u, b, sinks=False):
                    t = u % 2
                    c = slice(4 * u, 4 * u + 4)
                    v.wait_ge(sem["pv"], at("pv", l, u + 1))
                    if sinks:
                        link(V.tensor_tensor(rowsum[:, c], rowsum[:, c], esink[:, c], ALU.add))
                    link(V.reciprocal(rden[:, c], rowsum[:, c]))
                    V.tensor_tensor(y[:, b, t, :].rearrange("p (h c) -> p h c", h=H),
                                    wk[:, 3, 0:BW].rearrange("p (h c) -> p h c", h=H),
                                    rden[:, c][:, :, None].to_broadcast([P, H, HD]), ALU.mult).then_inc(sem["y"], 1)

                def yT_lo_copy(n):
                    v.wait_ge(sem["yT_hi"], at("yT_hi", l, n + 1))
                    V.tensor_tensor(yT_lo[:, n % 2].rearrange("p c t s -> p (c t s)"), wk[:, 2, :],
                                    yT_hi[:, n % 2].rearrange("p c t s -> p (c t s)").bitcast(F32), ALU.subtract)\
                        .then_inc(sem["yT_lo"], 1)

                def merge(n):
                    for first, half in enumerate(PROJ_HALVES[n]):
                        if first == 0:
                            v.wait_ge(sem["proj"], at("proj", l, n + 1))
                        else:
                            v.wait_ge(sem["mm"], at("mm", l, PROJ[n] + 1))
                        v.wait_ge(sem["gate"], at("gate", l, 4 * n + 2 * half + 2))
                        for t in range(T):
                            cols = slice(half * 512, half * 512 + 512)
                            g = gates[:, n % 2, t, cols]
                            to = merged[:, t, cols]
                            bank = acc[:, 2 * half + t, :]
                            if n == 0:
                                V.scalar_tensor_tensor(to, g, 1.0, bank, ALU.add, ALU.mult).then_inc(sem["merge"], 1)
                                continue
                            link(V.scalar_tensor_tensor(g, g, 1.0, bank, ALU.add, ALU.mult))
                            V.tensor_tensor(to, to, g, ALU.add).then_inc(sem["merge"], 1)

                transpose_lo(l, 0, 1, 0, mixg)
                V.tensor_copy(now[:, :], par[:, bass.ds(l, 1), :].rearrange("p a n -> p (a n)")).then_inc(sem["par"], 1)
                split_to(-1)
                norm_x(0, NORM1)
                split_to(1)
                norm_halved(0, NORM1)
                v.wait_ge(sem["par"], at("par", l, 1))
                split_to(2)
                v.wait_ge(sem["b_tq"], at("b_tq", l, 1))
                V.scalar_tensor_tensor(bq, bQ, 1.0, wk[:, 0, :], ALU.add, ALU.mult).then_inc(sem["b_q"], 1)
                link(V.tensor_scalar(bE, bE, 1.0, None, ALU.add))
                link(V.reciprocal(bT, bE))
                for hp in range(2):
                    c = slice(hp * SEQ, (hp + 1) * SEQ)
                    i = V.tensor_scalar(bT[:, c], bT[:, c], p_("oml")[:, hp:hp + 1], p_("low")[:, hp:hp + 1], ALU.mult,
                                        ALU.add)
                link(i)
                V.tensor_scalar(bk, bT, -0.5, 0.5, ALU.mult, ALU.add)
                V.tensor_scalar(bK, bT, 1e-19, None, ALU.max).then_inc(sem["b_f"], 1)
                split_to(3)
                v.wait_ge(sem["z"], at("z", l, 4))
                V.tensor_tensor(lf.rearrange("p (t h) -> p t h", t=T), z_dv[:, :, BW:BW + H],
                                p_("fb")[:, None, :].to_broadcast([P, T, H]), ALU.add).then_inc(sem["d_zf"], 1)
                split_to(4)
                v.wait_ge(sem["b_ln"], at("b_ln", l, 1))
                for n in range(4):
                    c = slice(n * P, (n + 1) * P)
                    i = V.tensor_tensor_scan(bT[:, c], c_("ones"), bK[:, c], 0.0, ALU.mult, ALU.add)
                i.then_inc(sem["b_scan"], 1)
                v.wait_ge(sem["b_scan"], at("b_scan", l, 1))

                def level_diff(j):
                    m = 2 ** j // 2
                    if j > 1:
                        v.wait_ge(sem["b_QK"], at("b_QK", l, j - 1))
                    blocks = bT.rearrange("p (n m) -> p n m", m=2 * m)
                    V.tensor_tensor(bE.rearrange("p (n m) -> p n m", m=2 * m), blocks,
                                    blocks[:, :, m - 1:m].to_broadcast([P, 512 // (2 * m), 2 * m]), ALU.subtract)\
                        .then_inc(sem["b_d"], 1)

                def level_qk(j):
                    v.wait_ge(sem["b_E"], at("b_E", l, j))
                    if j > 1:
                        v.wait_ge(sem["b_lev"], at("b_lev", l, 2 * j))
                    V.tensor_tensor(bQ, bq, bE, ALU.mult)
                    V.tensor_tensor(bK, bk, bE, ALU.mult).then_inc(sem["b_QK"], 1)

                def level_take(j):
                    for odd in range(2):
                        bank = wk[:, odd, :].rearrange("p (h s) -> p h s", h=H)
                        if j == 0:
                            v.wait_ge(sem["b_lev"], at("b_lev", l, odd + 1))
                            V.tensor_tensor(AT[odd], bank, c_("ident")[:, None, :].to_broadcast([P, H, P]), ALU.mult)\
                                .then_inc(sem["b_at"], 1)
                        else:
                            V.copy_predicated(AT[odd], level[:, j - 1, :][:, None, :].to_broadcast([P, H, P]), bank)\
                                .then_inc(sem["b_at"], 1)

                level_diff(1)
                v.wait_ge(sem["d_ln"], at("d_ln", l, 1))
                link(V.tensor_scalar(dsm[:, 4, :], lf, 0.0, None, ALU.min))
                V.tensor_tensor(lf, dsm[:, 4, :], dsm[:, 3, :], ALU.subtract).then_inc(sem["d_lf"], 1)
                v.wait_ge(sem["d_lf"], at("d_lf", l, 1))
                for t in range(T):
                    i = V.tensor_tensor(X[:, t], c_("stri")[:, None, :].to_broadcast([P, H, P]),
                                        lf[:, H * t:H * t + H][:, :, None].to_broadcast([P, H, P]), ALU.mult)
                i.then_inc(sem["d_x"], 1)
                for j in range(1, LEVELS + 1):
                    split_to(4 + j)
                    level_qk(j)
                    level_take(j - 1)
                    if j < LEVELS:
                        level_diff(j + 1)
                    if j == 4:
                        v.wait_ge(sem["ad_sq"], at("ad_sq", l, 1))
                        link(V.reduce_sum(norm(NORM_D, 0), square[:, 0:1024].rearrange("p (g c) -> p g c", c=HD),
                                          axis=AX.X))
                        mean(NORM_D, slice(0, 16), 1.0 / HD).then_inc(sem["mean"], 1)
                    if j == 5:
                        v.wait_ge(sem["rstd"], at("rstd", l, NORM_D + 1))
                        zq = region("wide", 1024, 1024).rearrange("p (g c) -> p g c", c=HD)
                        V.tensor_tensor(zq, zq, norm(NORM_D, 2)[:, :, None].to_broadcast([P, 16, HD]), ALU.mult)\
                            .then_inc(sem["ad_n"], 1)
                    if j == 6:
                        v.wait_ge(sem["ad_sq"], at("ad_sq", l, 2))
                        link(V.reduce_sum(norm(NORM_A, 0), square[:, 0:768].rearrange("p (g c) -> p g c", c=HD),
                                          axis=AX.X))
                        mean(NORM_A, slice(0, 12), 1.0 / HD).then_inc(sem["mean"], 1)
                    if j == 7:
                        v.wait_ge(sem["rstd"], at("rstd", l, NORM_A + 1))
                        for t in range(T):
                            r = norm(NORM_A, 2)[:, 6 * t:6 * t + 6]
                            q = z_a[:, t, 0:BW].rearrange("p (h c) -> p h c", h=H)
                            V.tensor_tensor(q, q, r[:, 0:H][:, :, None].to_broadcast([P, H, HD]), ALU.mult)
                            k = z_a[:, t, BW:BW + P].rearrange("p (h c) -> p h c", h=A_KV)
                            for dup in range(2):
                                i = V.tensor_tensor(kdup[:, t, :].rearrange("p (h d c) -> p h d c", h=A_KV, d=2)[:, :, dup],
                                                    k, r[:, H:H + A_KV][:, :, None].to_broadcast([P, A_KV, HD]), ALU.mult)
                        i.then_inc(sem["ad_n"], 1)
                split_to(12)
                v.wait_ge(sem["b_Ex"], at("b_Ex", l, 1))
                v.wait_ge(sem["b_lev"], at("b_lev", l, 2 * (LEVELS + 1)))
                halves = [a.rearrange("p (h t s) -> p h t s", h=2, t=T) for a in (bq, bk, bE, bQ, bK)]
                V.tensor_tensor(halves[3][:, :, 1], halves[0][:, :, 1], halves[2][:, :, 1], ALU.mult)
                V.tensor_tensor(halves[4][:, :, 0], halves[1][:, :, 0], halves[2][:, :, 0], ALU.mult)\
                    .then_inc(sem["b_QK"], 1)
                level_take(LEVELS)
                v.wait_ge(sem["c_sq"], at("c_sq", l, 1))
                mean(NORM_C1, slice(0, T), 1.0 / C_Q)
                mean(NORM_C1, slice(T, 2 * T), 1.0 / C_KV).then_inc(sem["mean"], 1)
                split_to(13)
                tops(0, 1.0)
                v.wait_ge(sem["rstd"], at("rstd", l, NORM_C1 + 1))
                for t in range(T):
                    r = norm(NORM_C1, 2)
                    V.tensor_scalar(z_c[:, t, 0:C_Q], z_c[:, t, 0:C_Q], r[:, t:t + 1], None, ALU.mult)
                    i = V.tensor_scalar(z_c[:, t, C_Q:C_Q + C_KV], z_c[:, t, C_Q:C_Q + C_KV], r[:, T + t:T + t + 1], None,
                                        ALU.mult)
                i.then_inc(sem["c_n"], 1)
                split_to(14)
                v.wait_ge(sem["c_hi"], at("c_hi", l, 1))
                for k in range(2):
                    V.scalar_tensor_tensor(cT_lo[:, k].rearrange("p t s -> p (t s)"), wk[:, 1, k * SEQ:(k + 1) * SEQ],
                                           p_("cq")[:, k:k + 1], cT_hi[:, k].rearrange("p t s -> p (t s)").bitcast(F32),
                                           ALU.mult, ALU.subtract)
                V.scalar_tensor_tensor(cT_lo[:, 2].rearrange("p t s -> p (t s)"), wk[:, 2, 0:SEQ], p_("ckv"),
                                       cT_hi[:, 2].rearrange("p t s -> p (t s)").bitcast(F32), ALU.mult, ALU.subtract)\
                    .then_inc(sem["c_lo"], 1)
                v.wait_ge(sem["b_sq"], at("b_sq", l, 1))
                link(V.reduce_sum(norm(NORM_B, 0), bE.rearrange("p (g c) -> p g c", c=HD), axis=AX.X))
                mean(NORM_B, slice(0, 8), 1.0 / HD).then_inc(sem["mean"], 1)
                split_to(15)
                tops(1, 1.0)
                v.wait_ge(sem["rstd"], at("rstd", l, NORM_B + 1))
                v.wait_ge(sem["b_tg"], at("b_tg", l, 1))
                g8 = [P, 8, HD]
                link(V.tensor_tensor(bT.rearrange("p (g c) -> p g c", c=HD), wk[:, 3, :].rearrange("p (g c) -> p g c", c=HD),
                                     norm(NORM_B, 2)[:, :, None].to_broadcast(g8), ALU.mult))
                V.tensor_tensor(bT.rearrange("p (g c) -> p g c", c=HD), bT.rearrange("p (g c) -> p g c", c=HD),
                                p_("bo")[:, None, :].to_broadcast(g8), ALU.mult)
                link(V.scalar_tensor_tensor(bK.rearrange("p (t c) -> p t c", t=T), bQ.rearrange("p (t c) -> p t c", t=T),
                                            1.0, z_ig[:, :, BW:2 * BW], ALU.add, ALU.mult))
                V.scalar_tensor_tensor(y[:, 0].rearrange("p t c -> p (t c)"), bT, 0.5, bK, ALU.mult, ALU.mult)\
                    .then_inc(sem["b_y"], 1)
                split_to(16)
                attended(0, 1)
                split_to(17)
                tops(2, 1.0, sinks=True)
                split_to(18)
                attended(1, 1)
                yT_lo_copy(0)
                split_to(19)
                tops(3, 1.0, sinks=True)
                split_to(20)
                attended(2, 0, sinks=True)
                yT_lo_copy(1)
                split_to(21)
                v.wait_ge(sem["c_sq2"], at("c_sq2", l, 1))
                V.reduce_sum(norm(NORM_C2, 0)[:, 0:8], c_s.rearrange("p (g c) -> p g c", c=C_DQ), axis=AX.X)
                link(V.reduce_sum(norm(NORM_C2, 0)[:, 8:16], c_s2.rearrange("p (g c) -> p g c", c=HD), axis=AX.X))
                k8 = norm(NORM_C2, 0)[:, 8:16].rearrange("p (t h) -> p t h", t=T)
                link(V.tensor_tensor(k8, k8, dsm[:, 4, 0:T][:, :, None].to_broadcast([P, T, H]), ALU.add))
                mean(NORM_C2, slice(0, 16), 1.0 / C_DQ).then_inc(sem["mean"], 1)
                split_to(22)
                attended(3, 0, sinks=True)
                merge(0)
                v.wait_ge(sem["rstd"], at("rstd", l, NORM_C2 + 1))
                r = norm(NORM_C2, 2)
                link(V.tensor_tensor(c_q, c_q, r[:, 0:8][:, :, None].to_broadcast([P, 8, C_DQ]), ALU.mult))
                V.tensor_tensor(c_q, c_q, p_("cqn")[:, None, :].to_broadcast([P, 8, C_DQ]), ALU.mult)
                V.tensor_tensor(c_k[:, :, 0:HD], c_kv[:, :, 0:HD], r[:, 8:16][:, :, None].to_broadcast([P, 8, HD]), ALU.mult)
                for t in range(T):
                    i = V.tensor_tensor(c_k[:, 4 * t:4 * t + 4, HD:C_DQ], z_c[:, t, 384:416][:, None, :].to_broadcast([P, H, C_ROPE]),
                                        r[:, 8 + 4 * t:12 + 4 * t][:, :, None].to_broadcast([P, H, C_ROPE]), ALU.mult)
                link(i)
                link(V.tensor_tensor(c_k, c_k, p_("ckn")[:, None, :].to_broadcast([P, 8, C_DQ]), ALU.mult))
                half = C_ROPE // 2
                for n, a in enumerate((c_q, c_k)):
                    rot = c_r[:, 256 * n:256 * n + 256].rearrange("p (g c) -> p g c", c=C_ROPE)
                    for t in range(T):
                        g = slice(4 * t, 4 * t + 4)
                        cos = c_("cos")[:, C_ROPE * t:C_ROPE * (t + 1)][:, None, :]
                        sin = c_("sin")[:, C_ROPE * t:C_ROPE * (t + 1)][:, None, :]
                        V.tensor_tensor(rot[:, g, 0:half], a[:, g, HD + half:C_DQ], sin[:, :, 0:half].to_broadcast([P, H, half]),
                                        ALU.mult)
                        link(V.tensor_tensor(rot[:, g, half:C_ROPE], a[:, g, HD:HD + half],
                                             sin[:, :, half:C_ROPE].to_broadcast([P, H, half]), ALU.mult))
                        i = V.tensor_tensor(a[:, g, HD:C_DQ], a[:, g, HD:C_DQ], cos.to_broadcast([P, H, C_ROPE]), ALU.mult)
                    link(i)
                    i = V.tensor_tensor(a[:, :, HD:C_DQ], a[:, :, HD:C_DQ], rot, ALU.add)
                i.then_inc(sem["c_n2"], 1)
                split_to(24)
                yT_lo_copy(2)
                split_to(26)
                tops(4, C_DQ ** -0.5)
                split_to(27)
                tops(5, C_DQ ** -0.5)
                merge(1)
                split_to(28)
                attended(4, 1)
                split_to(30)
                merge(2)
                attended(5, 1)
                split_to(31)
                yT_lo_copy(3)
                split_to(33)
                merge(3)
                merged_lo(0)
                merged_lo(1)

                def residual(done, banks, first):
                    for t in range(T):
                        V.tensor_tensor(x[:, t, first * 512:first * 512 + 512], x[:, t, first * 512:first * 512 + 512],
                                        acc[:, banks + t, :], ALU.add).then_inc(done, 1)

                split_to(35)
                v.wait_ge(sem["mm"], at("mm", l, OUT0 + 3))
                residual(sem["xmid"], 0, 0)
                split_to(36)
                transpose_lo(l, 3, 0, 0, p_("ffn"))
                v.wait_ge(sem["mm"], at("mm", l, OUT0 + 4))
                residual(sem["xmid"], 2, 1)
                split_to(37)
                transpose_lo(l, 4, 1, 2, p_("ffn"))
                V.tensor_copy(mixg[:, :], par[:, bass.ds(l + 1, 1), PARX["mix"][0]:PARX["mix"][0] + DK]
                              .rearrange("p a n -> p (a n)")).then_inc(sem["mixg"], 1)
                norm_x(1, NORM2)

                def ffn_split(c, i):
                    v.wait_ge(sem["hi"], at("hi", l, i * 4 + (c + 1)))
                    V.tensor_tensor(w_lo[:, c % RING, :], raw[:, c % RAW, :], w_hi[:, c % RING, :].bitcast(F32),
                                    ALU.subtract).then_inc(sem["lo"], 1)

                def swiglu(b, i):
                    for t in range(T):
                        bank = acc[:, 2 * (b % 2) + t, :]
                        v.wait_ge(sem["tanh"], at("tanh", l, i * 4 + (2 * b + t + 1)))
                        if b and t == 0:
                            v.wait_ge(sem["aT"], at("aT", l, i * 2 + (b - 1)))
                        last = V.scalar_tensor_tensor(sw[:, b % 2, t, :], sw[:, b % 2, t, :], 1.0, bank[:, 0:256], ALU.add,
                                                      ALU.mult)
                    last.then_inc(sem["sw"], 1)
                    v.wait_ge(sem["sw"], at("sw", l, i * 2 + (b + 1)))
                    for t in range(T):
                        bank = acc[:, 2 * (b % 2) + t, :]
                        V.scalar_tensor_tensor(act[:, b % 2, t, :], sw[:, b % 2, t, :], tok[:, 2, t:t + 1],
                                               bank[:, 256:512], ALU.mult, ALU.mult).then_inc(sem["act"], 1)

                def ffn_lo(b, i):
                    v.wait_ge(sem["aT_hi"], at("aT_hi", l, i * 2 + (b + 1)))
                    if isinstance(i, int):
                        hi, lo = aT_hi[:, b * 512:b * 512 + 512], aT_lo[:, b * 512:b * 512 + 512]
                    else:
                        hi, lo = (a[:, bass.ds(i * 1024 + b * 512, 512)] for a in (aT_hi, aT_lo))
                    V.scalar_tensor_tensor(lo, wk[:, b % 2, :], 0.5, hi.bitcast(F32), ALU.mult, ALU.subtract)\
                        .then_inc(sem["aT_lo"], 1)

                split_to(38)
                norm_halved(1, NORM2)
                split_to(39)
                v.wait_ge(sem["tok"], at("tok", l, 2))
                swiglu(0, 0)
                with v.Fori(0, FFN_BLOCKS // 2) as i:
                    for b in (1, 2):
                        ffn_split(FFN0 + 2 * b + 3, i)
                        ffn_split(FFN0 + 2 * b + 4, i)
                        swiglu(b, i)
                        ffn_lo(b - 1, i)
                split[0] = DOWN0 + 3
                split_to(DOWN0)
                ffn_lo(FFN_BLOCKS - 1, 0)
                split_to(DOWN0 + DOWN_CHUNKS - 1)
                v.wait_ge(sem["mm"], at("mm", l, DOWN0 + DOWN_CHUNKS))
                residual(sem["xout"], 0, 0)
                split_to(DOWN0 + DOWN_CHUNKS + 1)
                v.wait_ge(sem["mixg"], at("mixg", l, 1))
                transpose_lo(l, 5, 0, 2, mixg)
                split_to(CHUNKS)
                v.wait_ge(sem["mm"], at("mm", l, CHUNKS))
                residual(sem["xout"], 2, 1)
                assert links[0] == LINKS, links[0]

        @block.tensor
        def _(pe):
            M = nc.tensor
            pe.sem_inc(sem["mm"], HEADS["mm"])
            pe.sem_inc(sem["aT"], HEADS["aT"])
            ident = c_("ident")

            def transposes(bank, tiles, ready):
                for n, a in enumerate(tiles):
                    w = a.shape[-1]
                    i = M.transpose(bank[0:w, n * P:(n + 1) * P], a, ident)
                i.then_inc(ready, 1)

            def half_transposes(a, h, bank):
                for t in range(T):
                    transposes(wk[:, bank + t, :], [a[:, t, (4 * h + k) * P:(4 * h + k + 1) * P] for k in range(4)],
                               sem["xT"])

            pe.wait_ge(loaded["const"], 16)
            pe.wait_ge(loaded["x0"], 16)
            half_transposes(x, 0, 2)

            with pe.Fori(0, DEPTH) as l:
                def products(c, parts):
                    slot = c % RING
                    for bank, cols, rows, start, stop in parts:
                        for n, (hi, lo, col) in enumerate(rows):
                            wh, wl = w_hi[:, slot, col:col + cols], w_lo[:, slot, col:col + cols]
                            M.matmul(bank[:, 0:cols], hi, wh, start=start and n == 0, stop=False)
                            M.matmul(bank[:, 0:cols], lo, wh, start=False, stop=False)
                            i = M.matmul(bank[:, 0:cols], hi, wl, start=False, stop=stop and n == len(rows) - 1)
                    return i

                def chunk(c, parts, off=0):
                    pe.wait_ge(sem["lo"], at("lo", l, off + (c + 1)))
                    products(c, parts).then_inc(sem["mm"], 1)

                def x_parts(cols, pair, h):
                    return [(acc[:, 2 * pair + t, :], cols,
                             [(xT_hi[:, t, 4 * h + k, :], xT_lo[:, t, 4 * h + k, :], k * cols) for k in range(4)],
                             h == 0, h == 1) for t in range(T)]

                def half_block(c, cols, pair, h, off=0):
                    chunk(c + h, x_parts(cols, pair, h), off)

                def opening_block(c, cols, k, complete, bank):
                    first, second = x_parts(cols, 0, 0), x_parts(cols, 0, 1)
                    pe.wait_ge(sem["lo"], at("lo", l, c + 1))
                    pe.wait_ge(sem["xT_lo"], at("xT_lo", l, k * T + 1))
                    products(c, first[:1])
                    pe.wait_ge(sem["xT_lo"], at("xT_lo", l, k * T + 2))
                    pe.wait_ge(complete[0], complete[1])
                    half_transposes(x, 1, bank)
                    products(c, first[1:]).then_inc(sem["mm"], 1)
                    pe.wait_ge(sem["lo"], at("lo", l, c + 2))
                    pe.wait_ge(sem["xT_lo"], at("xT_lo", l, (k + 1) * T + 1))
                    products(c + 1, second[:1])
                    pe.wait_ge(sem["xT_lo"], at("xT_lo", l, (k + 1) * T + 2))
                    products(c + 1, second[1:]).then_inc(sem["mm"], 1)

                def b_level(j, q, k):
                    if j:
                        pe.wait_ge(sem["b_at"], at("b_at", l, 2 * j))
                    for odd in range(2):
                        r = slice(HD * odd, HD * odd + HD)
                        for n in range(4):
                            c = slice(n * P, (n + 1) * P)
                            i = M.matmul(wk[:, odd, c], k[r, c], q[r, c], start=True, stop=True)
                        i.then_inc(sem["b_lev"], 1)

                def qk_rows(branch, h, t, side):
                    base = area["qkT"][0]
                    if branch == BR_C:
                        col = base + 1024 * side + (2 * h + t) * P
                        return arena[0:C_DQ, col:col + P]
                    col = base + (1024 if branch == BR_A else 0) + 512 * side + (h // 2) * SEQ + t * P
                    r = HD * (h % 2)
                    return arena[r:r + HD, col:col + P]

                def scores(u, branch):
                    t = u % 2
                    for odd in range(2):
                        bank = wk[:, odd, :].rearrange("p (h k s) -> p h k s", h=2, k=T)
                        two = [P, 2, P]
                        pre = []
                        for k in range(t + 1):
                            if branch == BR_D and k == t:
                                pre.append((c_("tri"), X[:, t, odd:H:2, :], k))
                            elif branch == BR_D:
                                pre.append((c_("ones"), X[:, k, odd:H:2, :], k))
                                pre.append((c_("tri"), lf[:, H * t + odd:H * t + H:2][:, :, None].to_broadcast(two), k))
                            name = None
                            if k == t:
                                name = "causal" if branch == BR_D else "chunk"
                            elif branch == BR_A:
                                name = "window"
                            if name:
                                pre.append((m_("ident"), m_(name)[:, None, :].to_broadcast(two), k))
                        for n, (a, b, k) in enumerate(pre):
                            M.matmul(bank[:, :, k, :], a, b, start=n == 0, stop=False)
                        for n in range(2 * (t + 1)):
                            hp, k = n // (t + 1), n % (t + 1)
                            h = 2 * hp + odd
                            i = M.matmul(bank[:, hp, k, :], qk_rows(branch, h, t, 0), qk_rows(branch, h, k, 1), start=False,
                                         stop=n == 2 * t + 1)
                    i.then_inc(sem["score"], 1)

                def p_transposes(u):
                    pe.wait_ge(sem["prob"], at("prob", l, u + 1))
                    for k in range(u % 2 + 1):
                        if k == 1 and u:
                            pe.wait_ge(sem["y"], at("y", l, u))
                        transposes(wk[:, 2 + k, :], [prob[:, h, k, :] for h in range(H)], sem["pT"])

                def weighted(u, values):
                    t = u % 2
                    pe.wait_ge(sem["pT_sb"], at("pT_sb", l, PT_DONE[u]))
                    if u:
                        pe.wait_ge(sem["y"], at("y", l, u))
                    for h in range(H):
                        for k in range(t + 1):
                            i = M.matmul(wk[:, 3, h * HD:(h + 1) * HD], pT[:, k, h, :], values(k, h), start=k == 0,
                                         stop=k == t)
                    i.then_inc(sem["pv"], 1)

                def y_transposes(n):
                    transposes(wk[:, 2, :], [y[:, n % 2, t, c * P:(c + 1) * P] for c in range(2) for t in range(T)], sem["yT"])

                def z_first(b):
                    c = 2 * b
                    if b >= 2:
                        pe.wait_ge(sem["z"], at("z", l, 2 * (b - 1)))
                    half_block(c, Z_BLOCKS[b][1], b % 2, 0)

                def z_rest(b):
                    half_block(2 * b, Z_BLOCKS[b][1], b % 2, 1)

                def dv(k, h):
                    return z_dv[:, k, h * HD:(h + 1) * HD]

                def av(k, h):
                    return z_a[:, k, 384 + (h // 2) * HD:384 + (h // 2) * HD + HD]

                def cv(k, h):
                    return c_kv[:, 4 * k + h, HD:2 * HD]

                opening_block(0, Z_BLOCKS[0][1], -1, (sem["xout"], at("xout", l, 0)), 0)
                z_first(1)
                pe.wait_ge(setup, SETUP)
                pe.wait_ge(sem["z"], at("z", l, 2))
                for col in range(2):
                    transposes(wk[:, col, :], [z_qf[:, t, col * BW + hp * P:col * BW + (hp + 1) * P]
                                               for hp in range(2) for t in range(T)], sem["b_in"])
                z_rest(1)
                z_first(2)
                z_rest(2)

                def decayed_level(j):
                    pe.wait_ge(sem["b_QK"], at("b_QK", l, j))
                    b_level(j, bQ, bK)

                def ad_transposes(n, q, k):
                    pe.wait_ge(sem["ad_n"], at("ad_n", l, n + 1))
                    if n:
                        pe.wait_ge(sem["ad_sb"], at("ad_sb", l, 2 * n))
                    for side, a in enumerate((q, k)):
                        transposes(wk[:, 2 + side, :], [a[:, t, c * P:(c + 1) * P] for c in range(2) for t in range(T)], sem["ad_T"])

                z_first(3)
                pe.wait_ge(sem["b_scan"], at("b_scan", l, 1))
                b_level(0, bq, bk)
                decayed_level(1)
                z_rest(3)
                decayed_level(2)
                z_first(4)
                decayed_level(3)
                z_rest(4)
                decayed_level(4)
                z_first(5)
                decayed_level(5)
                ad_transposes(0, z_dqk[:, :, 0:BW], z_dqk[:, :, BW:2 * BW])
                z_rest(5)
                decayed_level(6)

                def gate_first(g):
                    branch, half = g // 2, g % 2
                    if g < 2:
                        pe.wait_ge(sem["z"], at("z", l, 10 + 2 * g))
                    elif g < 4:
                        pe.wait_ge(sem["gate"], at("gate", l, 2 * (g - 1)))
                    else:
                        pe.wait_ge(sem["merge"], at("merge", l, GATE_AFTER[g - 4]))
                    half_block(GATE[branch][half], 512, half, 0)

                def gate_rest(g):
                    branch, half = g // 2, g % 2
                    half_block(GATE[branch][half], 512, half, 1)

                def project(n):
                    pe.wait_ge(sem["yT_lo"], at("yT_lo", l, n + 1))
                    pe.wait_ge(sem["lo"], at("lo", l, PROJ[n] + 1))
                    for first, half in enumerate(PROJ_HALVES[n]):
                        if n == 0:
                            pe.wait_ge(sem["u"], at("u", l, T * (half + 1)))
                        elif n == 1 or n == 2 and half == 0:
                            pe.wait_ge(sem["gate"], at("gate", l, 4 * n + 4 + T * (half + 1)))
                        elif n == 2:
                            pe.wait_ge(sem["merge"], at("merge", l, 8))
                        elif half == 0:
                            pe.wait_ge(sem["merge"], at("merge", l, 12))
                        else:
                            pe.wait_ge(sem["gate"], at("gate", l, 16))
                        products(PROJ[n], [(acc[:, 2 * half + t, :], 512,
                                            [(yT_hi[:, n % 2, k, t, :], yT_lo[:, n % 2, k, t, :], k * D + half * 512)
                                             for k in range(2)], True, True) for t in range(T)])\
                            .then_inc(sem["mm"] if first else sem["proj"], 1)

                def b_cross():
                    pe.wait_ge(sem["b_QK"], at("b_QK", l, LEVELS + 1))
                    pe.wait_ge(sem["ad_sb"], at("ad_sb", l, 4))
                    for odd in range(2):
                        r = slice(HD * odd, HD * odd + HD)
                        for hp in range(2):
                            col = hp * SEQ
                            i = M.matmul(wk[:, 2 + odd, hp * P:(hp + 1) * P], bK[r, col:col + P], bQ[r, col + P:col + 2 * P],
                                         start=True, stop=True)
                        i.then_inc(sem["b_cross"], 1)

                def b_out():
                    pe.wait_ge(sem["b_atx"], at("b_atx", l, 2))
                    pe.wait_ge(sem["b_at"], at("b_at", l, 2 * (LEVELS + 1)))
                    for t in range(T):
                        for h in range(H):
                            o = wk[:, 3, t * BW + h * HD:t * BW + (h + 1) * HD]
                            if t:
                                M.matmul(o, AT[2][:, 2 * (h % 2) + h // 2, :], z_ig[:, 0, h * HD:(h + 1) * HD], start=True, stop=False)
                            i = M.matmul(o, AT[h % 2][:, 2 * (h // 2) + t, :], z_ig[:, t, h * HD:(h + 1) * HD], start=t == 0, stop=True)
                    i.then_inc(sem["b_o"], 1)

                def c_latents():
                    pe.wait_ge(sem["c_n"], at("c_n", l, 1))
                    pe.wait_ge(sem["prob"], at("prob", l, 1))
                    transposes(wk[:, 1, :], [z_c[:, t, c * P:(c + 1) * P] for c in range(2) for t in range(T)], sem["c_T"])
                    transposes(wk[:, 2, :], [z_c[:, t, C_Q:C_Q + C_KV] for t in range(T)], sem["c_T"])

                def first_scores():
                    pe.wait_ge(sem["ad_sb"], at("ad_sb", l, 2))
                    pe.wait_ge(sem["d_x"], at("d_x", l, 1))
                    pe.wait_ge(sem["b_at"], at("b_at", l, 2 * (LEVELS + 1)))
                    scores(0, BR_D)

                def c_transposes():
                    pe.wait_ge(sem["c_n2"], at("c_n2", l, 1))
                    pe.wait_ge(sem["yT_lo"], at("yT_lo", l, 3))
                    for n, (a, h) in enumerate(((c_q, 0), (c_q, 2), (c_k, 0), (c_k, 2))):
                        transposes(wk[:, n, :], [a[:, 4 * t + hh, :] for hh in (h, h + 1) for t in range(T)],
                                   sem["c_T2"])

                gate_first(0)
                decayed_level(7)
                ad_transposes(1, z_a[:, :, 0:BW], kdup)
                gate_rest(0)
                b_cross()
                first_scores()
                gate_first(1)
                b_out()
                c_latents()
                gate_rest(1)
                pe.wait_ge(sem["c_lo"], at("c_lo", l, 1))
                p_transposes(0)
                pe.wait_ge(sem["prob"], at("prob", l, 1))
                scores(1, BR_D)

                gate_first(2)
                pe.wait_ge(sem["b_y"], at("b_y", l, 1))
                weighted(0, dv)
                gate_rest(2)
                p_transposes(1)
                pe.wait_ge(sem["prob"], at("prob", l, 2))
                scores(2, BR_A)

                gate_first(3)
                weighted(1, dv)
                y_transposes(0)
                gate_rest(3)
                pe.wait_ge(sem["yT_lo"], at("yT_lo", l, 1))
                p_transposes(2)
                pe.wait_ge(sem["prob"], at("prob", l, 3))
                scores(3, BR_A)
                pe.wait_ge(sem["c_lo"], at("c_lo", l, 1))
                pe.wait_ge(sem["gate"], at("gate", l, 6))
                chunk(UQ, [(acc[:, t, :], H * C_DQ,
                            [(cT_hi[:, k, t, :], cT_lo[:, k, t, :], k * H * C_DQ) for k in range(2)], True, True)
                           for t in range(T)])
                weighted(2, av)
                pe.wait_ge(sem["y"], at("y", l, 2))
                pe.wait_ge(sem["pT_sb"], at("pT_sb", l, PT_DONE[2]))
                y_transposes(1)
                pe.wait_ge(sem["gate"], at("gate", l, 8))
                chunk(UKV, [(acc[:, 2 + t, :], 512, [(cT_hi[:, 2, t, :], cT_lo[:, 2, t, :], 0)], True, True)
                            for t in range(T)])
                pe.wait_ge(sem["yT_lo"], at("yT_lo", l, 2))
                p_transposes(3)
                project(0)
                weighted(3, av)
                gate_first(4)
                gate_rest(4)
                pe.wait_ge(sem["y"], at("y", l, 4))
                y_transposes(2)
                gate_first(5)
                c_transposes()
                gate_rest(5)
                pe.wait_ge(sem["c_sb2"], at("c_sb2", l, 4))
                scores(4, BR_C)
                project(1)
                p_transposes(4)
                scores(5, BR_C)
                gate_first(6)
                weighted(4, cv)
                gate_rest(6)
                p_transposes(5)
                project(2)
                weighted(5, cv)
                gate_first(7)
                pe.wait_ge(sem["y"], at("y", l, 6))
                y_transposes(3)
                gate_rest(7)
                project(3)

                def out_parts(h, half):
                    return [(acc[:, 2 * half + t, :], 512,
                             [(mT_hi[:, t, 4 * h + k, :], mT_lo[:, t, 4 * h + k, :], k * 512) for k in range(4)],
                             h == 0, h == 1) for t in range(T)]

                pe.wait_ge(sem["merge"], at("merge", l, 14))
                half_transposes(merged, 0, 0)
                pe.wait_ge(sem["merge"], at("merge", l, 16))
                half_transposes(merged, 1, 2)
                pe.wait_ge(sem["xT_lo"], at("xT_lo", l, 2 * T))
                chunk(OUT0, out_parts(0, 0))
                chunk(OUT0 + 1, out_parts(0, 1))
                pe.wait_ge(sem["xT_lo"], at("xT_lo", l, 3 * T))
                chunk(OUT0 + 2, out_parts(1, 0))
                pe.wait_ge(sem["lo"], at("lo", l, OUT0 + 4))
                products(OUT0 + 3, out_parts(1, 1)[:1])
                pe.wait_ge(sem["xmid"], at("xmid", l, T))
                half_transposes(x, 0, 0)
                products(OUT0 + 3, out_parts(1, 1)[1:]).then_inc(sem["mm"], 1)

                opening_block(FFN0, 512, 3, (sem["xmid"], at("xmid", l, 2 * T)), 2)

                def act_transposes(b, i):
                    pe.wait_ge(sem["act"], at("act", l, i * 4 + (2 * b + 2)))
                    transposes(wk[:, b % 2, :], [act[:, b % 2, t, c * P:(c + 1) * P] for c in range(2) for t in range(T)], sem["aT"])

                with pe.Fori(0, FFN_BLOCKS // 2) as i:
                    for b in (1, 2):
                        if b == 2:
                            pe.wait_ge(sem["act"], at("act", l, i * 4 + 2))
                        else:
                            pe.wait_ge(sem["act"], at("act", l, i * 4))
                        half_block(FFN0 + 2 * b, 512, b % 2, 0, off=i * 4)
                        half_block(FFN0 + 2 * b, 512, b % 2, 1, off=i * 4)
                        pe.wait_ge(sem["aT_lo"], at("aT_lo", l, i * 2 + (b - 2) if b == 2 else i * 2))
                        act_transposes(b - 1, i)
                for half in range(2):
                    for n in range(DOWN_CHUNKS):
                        c = DOWN0 + half * DOWN_CHUNKS + n
                        tiles = range(4 * n, min(4 * n + 4, FF_TILES))
                        if half == 0:
                            pe.wait_ge(sem["aT_lo"], at("aT_lo", l, min(2 * n + 2, FFN_BLOCKS)))
                            if n == 0:
                                pe.wait_ge(sem["act"], at("act", l, 2 * FFN_BLOCKS))
                        chunk(c, [(acc[:, 2 * half + t, :], 512,
                                   [(aT_hi[:, k * SEQ + t * P:k * SEQ + (t + 1) * P], aT_lo[:, k * SEQ + t * P:k * SEQ + (t + 1) * P],
                                     (k - 4 * n) * 512) for k in tiles], n == 0, n == DOWN_CHUNKS - 1) for t in range(T)])
                        if c == DOWN0 + DOWN_CHUNKS + 1:
                            pe.wait_ge(sem["xout"], at("xout", l, T))
                            half_transposes(x, 0, 2)
                        if c == DOWN0:
                            pe.wait_ge(sem["aT_lo"], at("aT_lo", l, FFN_BLOCKS - 2))
                            act_transposes(FFN_BLOCKS - 1, 0)


def stream_layout(w_in, w_branch, w_out, w_ffn_in, w_ffn_out, c_w_uq, c_w_ukv, np):
    out = np.zeros((DEPTH, CHUNKS, P, CW), np.float32)

    def rows(w, first, n):
        return w[first * P:(first + n) * P].reshape(n, P, -1).transpose(1, 0, 2).reshape(P, -1)

    for l in range(DEPTH):
        def put(c, a):
            out[l, c, :, :a.shape[1]] = a

        def halves(c, w):
            put(c, rows(w, 0, 4))
            put(c + 1, rows(w, 4, 4))

        for b, (col, n) in enumerate(Z_BLOCKS):
            halves(2 * b, w_in[l][:, col:col + n])
        for n, br in enumerate(MERGE_ORDER):
            for h in range(2):
                col = OFF_G + br * D + h * 512
                halves(GATE[n][h], w_in[l][:, col:col + 512])
            put(PROJ[n], rows(w_branch[l, br], 0, 2))
        put(UQ, rows(c_w_uq[l], 0, 2))
        put(UKV, rows(c_w_ukv[l], 0, 1))
        for h in range(2):
            for half in range(2):
                put(OUT0 + 2 * h + half, rows(w_out[l][:, half * 512:half * 512 + 512], 4 * h, 4))
        for b in range(FFN_BLOCKS):
            g = w_ffn_in[l][:, b * 256:b * 256 + 256]
            u = w_ffn_in[l][:, D_FF + b * 256:D_FF + b * 256 + 256]
            halves(FFN0 + 2 * b, np.concatenate([g, u], axis=1))
        for h in range(2):
            for n in range(DOWN_CHUNKS):
                k = min(4, FF_TILES - 4 * n)
                put(DOWN0 + h * DOWN_CHUNKS + n, rows(w_ffn_out[l][:, h * 512:h * 512 + 512], 4 * n, k))
    return out.reshape(DEPTH * CHUNKS, P, CW)


def constants(np):
    i = np.arange(P)
    row, col = i[:, None], i[None, :]
    const = np.zeros((P, CONST_N), np.float32)

    def put(name, a):
        col, n = CONST[name]
        const[:, col:col + n] = a

    put("ident", row == col)
    put("tri", row <= col)
    put("stri", col < row)
    put("ones", 1.0)
    put("half", -0.5)
    half = C_ROPE // 2
    inv = np.exp(np.float32(-np.log(10000.0)) * np.arange(half, dtype=np.float32) / np.float32(half))
    ang = (np.arange(T)[None, :, None] * P + i[:, None, None]).astype(np.float32) * inv.astype(np.float32)
    put("cos", np.concatenate([np.cos(ang), np.cos(ang)], axis=-1).reshape(P, -1))
    put("sin", np.concatenate([-np.sin(ang), np.sin(ang)], axis=-1).reshape(P, -1))
    mask = np.zeros((P, MASK_N), np.float32)
    masks = {"ident": row == col, "causal": np.where(col <= row, 0.0, NEG),
             "chunk": np.where(col // CHUNK <= row // CHUNK, 0.0, NEG),
             "window": np.where((row < CHUNK) & (col >= CHUNK), 0.0, NEG)}
    for name, a in masks.items():
        first, n = MASKS[name]
        mask[:, first:first + n] = a
    level = np.zeros((P, LEVELS * P), np.float32)
    for j in range(LEVELS):
        m = 2 ** j
        level[:, j * P:(j + 1) * P] = (row // (2 * m) == col // (2 * m)) & (row % (2 * m) < m) & (col % (2 * m) >= m)
    return const, mask, level


def parameters(v, np):
    par = np.zeros((P, DEPTH, PAR_IN), np.float32)

    def put(name, l, a):
        col, n = PAR[name]
        par[:, l, col:col + n] = a

    for l in range(DEPTH):
        put("mix", l, v["norm_mix_g"][l].reshape(DK, P).T)
        put("ffn", l, v["norm_ffn_g"][l].reshape(DK, P).T)
        put("cq", l, v["c_cq_norm_g"][l].reshape(2, P).T)
        put("ckv", l, v["c_ckv_norm_g"][l].reshape(1, P).T)
        for name, key in (("aq", "a_q_norm_g"), ("ak", "a_k_norm_g"), ("dq", "d_q_norm_g"), ("dk", "d_k_norm_g")):
            put(name, l, np.concatenate([v[key][l]] * 2)[:, None])
        put("lb", l, v["hgrn_lb_logits"][l].reshape(2, P).T)
        for name, key in (("bo", "b_o_norm_g"), ("cqn", "c_q_norm_g"), ("ckn", "c_k_norm_g"), ("sink", "a_sinks"),
                          ("fb", "d_f_bias")):
            put(name, l, v[key][l][None, :])
    return par


def kernel(**inputs):
    import numpy as np
    import concourse.bacc as bacc
    from concourse.bass_utils import run_bass_kernel_spmd

    v = {k: np.asarray(a) for k, a in inputs.items()}
    const, mask, level = constants(np)
    arrays = {
        "in_x": np.ascontiguousarray(v["x"].reshape(T, P, D).transpose(1, 0, 2)),
        "in_stream": stream_layout(v["w_in"], v["w_branch"], v["w_out"], v["w_ffn_in"], v["w_ffn_out"], v["c_w_uq"],
                                   v["c_w_ukv"], np),
        "in_par": parameters(v, np), "in_const": const, "in_mask": mask, "in_level": level,
    }
    nc = bacc.Bacc("TRN2", target_bir_lowering=False, num_devices=1)
    args = [nc.dram_tensor(n, a.shape, mybir.dt.from_np(a.dtype), kind="ExternalInput").ap() for n, a in arrays.items()]
    out = nc.dram_tensor("out_x", (P, T, D), F32, kind="ExternalOutput").ap()
    trunk(nc, *args, out)
    r = run_bass_kernel_spmd(nc, [arrays], core_ids=[0])
    return r.results[0]["out_x"].transpose(1, 0, 2).reshape(1, SEQ, D)
```

```python
from contextlib import ExitStack

import concourse.bass as bass
from concourse import mybir

F32 = mybir.dt.float32
F32R = mybir.dt.float32r
BF16 = mybir.dt.bfloat16
U8 = mybir.dt.uint8
ALU = mybir.AluOpType
ACT = mybir.ActivationFunctionType
AX = mybir.AxisListType

P = 128
SEQ = 256
T = SEQ // P
D = 1024
DK = D // P
DEPTH = 2
CHUNK = 64
H = 4
HD = 64
A_KV = 2
C_Q, C_KV, C_ROPE, C_DQ = 256, 128, 32, 96
D_FF = 2816
FFN_BLOCKS = D_FF // 256
FF_TILES = D_FF // P
BW = H * HD
EPS = 1e-6
NEG = -1e30

OFF_A, OFF_B, OFF_C, OFF_D, OFF_G = 0, 512, 1536, 1952, 2724
Z_BLOCKS = [
    (OFF_B, 512),
    (OFF_D + 512, 260),
    (OFF_B + 512, 512),
    (OFF_D, 512),
    (OFF_A, 512),
    (OFF_C, 416),
]
BR_A, BR_B, BR_C, BR_D = 0, 1, 2, 3
MERGE_ORDER = [BR_B, BR_D, BR_A, BR_C]

CW = 2048
GATE = [((12, 13), (14, 15)), ((16, 17), (18, 19)), ((23, 24), (25, 26)), ((28, 29), (31, 33))]
UQ, UKV = 20, 21
PROJ = [22, 27, 30, 32]
PROJ_HALVES = [(0, 1), (0, 1), (1, 0), (0, 1)]
PROJ_PAIR = [(0, 1), (0, 1), (1, 0), (0, 0)]
OUT0 = 34
OUT = [(0, 1), (0, 0), (1, 0), (1, 1)]
FFN0 = 38
DOWN0 = FFN0 + 2 * FFN_BLOCKS
DOWN_CHUNKS = -(-FF_TILES // 4)
DOWN = [(1, 0)] + [(0, n) for n in range(DOWN_CHUNKS)] + [(1, n) for n in range(1, DOWN_CHUNKS)]
DOWN_HALF = DOWN0 + 1 + DOWN_CHUNKS
CHUNKS = DOWN0 + 2 * DOWN_CHUNKS
RAW, RING = 2, 4
HALF = CW // 2
AHEAD = 2
assert CHUNKS % RING == 0 and FFN_BLOCKS % 2 == 1 and (FFN0 + 2) % RING == 0

PAR_COLS = [("mix", DK), ("ffn", DK), ("cq", 2), ("ckv", 1), ("aq", 1), ("ak", 1), ("dq", 1), ("dk", 1),
            ("lb", 2), ("bo", HD), ("cqn", C_DQ), ("ckn", C_DQ), ("sink", H), ("fb", H)]
DERIVED = [("low", 2), ("oml", 2), ("ga", 1), ("gd", 1)]


def columns(spec):
    first, out = 0, {}
    for name, n in spec:
        out[name] = (first, n)
        first += n
    return out, first


PAR, PAR_IN = columns(PAR_COLS)
PARX, PAR_N = columns(PAR_COLS + DERIVED)

CONST, CONST_N = columns([("ident", P), ("tri", P), ("stri", P), ("ones", P), ("cos", T * C_ROPE), ("sin", T * C_ROPE),
                          ("half", 16)])
MASKS, MASK_N = columns([("ident", P), ("causal", P), ("chunk", P), ("window", P)])
LEVELS = 7

NORM1, NORM_D, NORM_A, NORM_C1, NORM_B, NORM_C2, NORM2 = range(7)
NORM_WIDTH = [T, 16, 12, 2 * T, 8, 16, T]
NORM_AT = [sum(NORM_WIDTH[:i]) for i in range(7)]
NORM_N = sum(NORM_WIDTH)


SETUP = 12
GATE_AFTER = [2, 4, 6, 10]
PT_DONE = [1, 3, 4, 6, 7, 9]
LINKS = 38


def pieces(c):
    n = width(c)
    if n <= HALF + 128:
        return [(slice(0, n), 2)]
    return [(slice(0, HALF), 1), (slice(HALF, n), 1)]


def width(c):
    c %= CHUNKS
    if c < 2 * len(Z_BLOCKS):
        return 4 * Z_BLOCKS[c // 2][1]
    if c == UQ:
        return 2 * H * C_DQ
    if c == UKV:
        return H * 2 * HD
    if c >= DOWN0 and DOWN[c - DOWN0][1] == DOWN_CHUNKS - 1:
        return (FF_TILES - 4 * (DOWN_CHUNKS - 1)) * 512
    return CW


SIGNALS = dict(
    hi=2 * CHUNKS, lo=2 * CHUNKS, mm=CHUNKS, par=1, dve=LINKS,
    mixg=1, sumsq=2 * T, mean=7, rstd=7, tok=2,
    xT=6 * T, xT_hi=6 * T, xT_lo=6 * T,
    z=T * len(Z_BLOCKS), gate=4 * 2 * T, u=2 * T, proj=4, last_gate=1, gated=3 * 2 * T, merge=4 * 2 * T, xmid=2 * T, xout=2 * T,
    b_in=2, b_e=1, b_tq=1, b_f=1, b_q=1, b_ln=1, b_scan=1, b_d=LEVELS, b_abs=LEVELS, b_E=LEVELS,
    b_QK=LEVELS + 1, b_lev=2 * (LEVELS + 1), b_at=2 * (LEVELS + 1), b_Ex=1, b_cross=2, b_atx=2, b_o=1, b_sq=1, b_tg=1,
    b_y=1,
    d_zf=1, d_abs=1, d_e=1, d_ln=1, d_lf=1, d_x=1, ad_sq=2, ad_n=2, ad_T=4, ad_sb=4,
    c_sq=1, c_n=1, c_T=2, c_hi=1, c_lo=1, c_sq2=1, c_n2=1, c_T2=4, c_sb2=4,
    score=6, top=6, prob=6, pT=9, pT_sb=9, pv=6, y=6, yT=4, yT_hi=4, yT_lo=4,
    tanh=2 * FFN_BLOCKS, act=2 * FFN_BLOCKS, sw=FFN_BLOCKS, aT=FFN_BLOCKS, aT_hi=FFN_BLOCKS, aT_lo=FFN_BLOCKS,
)


HEADS = dict(mm=RING, mixg=1, xT=T, xT_hi=T, xT_lo=T, xout=1, act=1, aT=1, aT_lo=1)


def at(name, layer, k):
    return layer * SIGNALS[name] + ((HEADS[name] if name in HEADS else 0) + k)


def trunk(nc, x_in, stream, par_in, const_in, mask_in, level_in, out):
    ctx = ExitStack()
    with ctx:
        def sb(name, shape, dt=F32):
            return ctx.enter_context(nc.sbuf_tensor(name, shape, dt))

        def new_sem(name):
            return ctx.enter_context(nc.semaphore(name))

        x = sb("x", [P, T, D])
        xT_hi = sb("xT_hi", [P, T, DK, P], F32R)
        xT_lo = sb("xT_lo", [P, T, DK, P], F32R)
        raw = sb("raw", [P, RAW, CW])
        w_hi = sb("w_hi", [P, RING, CW], F32R)
        w_lo = sb("w_lo", [P, RING, CW], F32R)
        par = sb("par", [P, DEPTH + 1, PAR_N])
        now = sb("now", [P, PAR_N])
        mixg = sb("mixg", [P, DK])
        tok = sb("tok", [P, 3, T])
        const = sb("const", [P, CONST_N])
        mask = sb("mask", [P, MASK_N], BF16)
        level = sb("level", [P, LEVELS, P], U8)
        stat = sb("stat", [P, 3, NORM_N])
        small = sb("small", [P, 128])
        dsm = sb("dsm", [P, 5, 2 * H])

        with ExitStack() as attention:
            gates = attention.enter_context(nc.sbuf_tensor("gates", [P, 2, T, D], F32))
            yT_hi = attention.enter_context(nc.sbuf_tensor("yT_hi", [P, 2, 2, T, P], F32R))
            yT_lo = attention.enter_context(nc.sbuf_tensor("yT_lo", [P, 2, 2, T, P], F32R))
            cT_hi = attention.enter_context(nc.sbuf_tensor("cT_hi", [P, 3, T, P], F32R))
            cT_lo = attention.enter_context(nc.sbuf_tensor("cT_lo", [P, 3, T, P], F32R))
            AREA = [("wide", 2 * D), ("zqf", 1024), ("zdv", T * 260), ("zc", T * 416), ("qkT", 2048), ("prob", 1024),
                    ("pT", 1024), ("y", 1024), ("kdup", 512), ("X", 1024)]
            area, area_n = columns(AREA)
            arena = attention.enter_context(nc.sbuf_tensor("arena", [P, area_n], F32))
            with ExitStack() as scans:
                b_area = scans.enter_context(nc.sbuf_tensor("b_area", [P, 4608], F32))
            with ExitStack() as merging:
                mT_hi = merging.enter_context(nc.sbuf_tensor("mT_hi", [P, T, DK, P], F32R))
                mT_lo = merging.enter_context(nc.sbuf_tensor("mT_lo", [P, T, DK, P], F32R))
        with ExitStack() as ffn:
            keep_x_normed = ffn.enter_context(nc.sbuf_tensor("keep_gates", [P, 2, T, D], F32))
            aT_hi = ffn.enter_context(nc.sbuf_tensor("aT_hi", [P, FF_TILES * SEQ], F32R))
            aT_lo = ffn.enter_context(nc.sbuf_tensor("aT_lo", [P, FF_TILES * SEQ], F32R))
        del keep_x_normed

        def region(name, first=0, n=None):
            col, size = area[name]
            return arena[:, col + first:col + (size if n is None else first + n)]

        wide = region("wide")
        merged = wide.rearrange("p (t d) -> p t d", t=T)
        z_ig = region("wide", 0, 1024).rearrange("p (t c) -> p t c", t=T)
        z_dqk = region("wide", 1024, 1024).rearrange("p (t c) -> p t c", t=T)
        z_qf = region("zqf").rearrange("p (t c) -> p t c", t=T)
        z_a = z_qf
        z_dv = region("zdv").rearrange("p (t c) -> p t c", t=T)
        z_c = region("zc").rearrange("p (t c) -> p t c", t=T)
        z_of = [z_qf, z_dv, z_ig, z_dqk, z_a, z_c]
        prob = region("prob").rearrange("p (h k s) -> p h k s", k=T, h=H)
        pT = region("pT").rearrange("p (k h s) -> p k h s", k=T, h=H)
        y = region("y").rearrange("p (b t c) -> p b t c", b=2, t=T)
        kdup = region("kdup").rearrange("p (t c) -> p t c", t=T)
        X = region("X").rearrange("p (t h s) -> p t h s", t=T, h=H)
        bq, bk, bT, bE, bQ, bK = (b_area[:, 512 * i:512 * i + 512] for i in range(6))
        AT = [b_area[:, 3072 + 512 * i:3584 + 512 * i].rearrange("p (h s) -> p h s", h=H) for i in range(3)]
        c_q = b_area[:, 0:768].rearrange("p (g c) -> p g c", c=C_DQ)
        c_k = b_area[:, 768:1536].rearrange("p (g c) -> p g c", c=C_DQ)
        c_kv = b_area[:, 1536:2560].rearrange("p (g c) -> p g c", c=2 * HD)
        c_s = b_area[:, 2560:3328]
        c_s2 = b_area[:, 3328:3840]
        c_r = b_area[:, 3840:4352]
        staged = b_area[:, 0:MASK_N + LEVELS * P]
        square = region("prob")
        junk = region("y", 0, 768)

        act = gates[:, 0, :, :].rearrange("p a b -> p (a b)")[:, 0:1024].rearrange("p (b t c) -> p b t c", b=2, t=T)
        sw = gates[:, 1, :, :].rearrange("p a b -> p (a b)")[:, 0:1024].rearrange("p (b t c) -> p b t c", b=2, t=T)

        acc = ctx.enter_context(nc.psum_tensor("acc", [P, 4, 512], F32))
        wk = ctx.enter_context(nc.psum_tensor("wk", [P, 4, 512], F32))

        raw_loaded = [[new_sem(f"raw_loaded{i}_{h}") for h in range(2)] for i in range(RAW)]
        loaded = {n: new_sem(f"loaded_{n}") for n in ("x0", "x1", "ident", "par", "const", "mask", "level")}
        stored = new_sem("stored")
        setup = new_sem("setup")
        sem = {n: new_sem(f"s_{n}") for n in SIGNALS}

        def p_(name):
            col, n = PARX[name]
            return now[:, col:col + n]

        def c_(name, rows=P):
            col, n = CONST[name]
            return const[0:rows, col:col + n]

        def m_(name):
            col, n = MASKS[name]
            return mask[:, col:col + n]

        def norm(which, row):
            return stat[:, row, NORM_AT[which]:NORM_AT[which] + NORM_WIDTH[which]]

        mx, negm, rowsum, rden, esink = (small[:, 24 * i:24 * i + 24] for i in range(5))
        lf = dsm[:, 0, :]

        block = ctx.enter_context(nc.Block())

        @block.sync
        def _(sp):
            sp.dma_start(x[:, :, 0:512], x_in[:, :, 0:512]).then_inc(loaded["x0"], 16)
            sp.dma_start(par[:, 0:DEPTH, 0:PAR_IN], par_in).then_inc(loaded["par"], 16)
            sp.dma_start(raw[:, 0, 0:HALF], stream[0][:, 0:HALF]).then_inc(raw_loaded[0][0], 16)
            sp.dma_start(raw[:, 0, HALF:CW], stream[0][:, HALF:CW]).then_inc(raw_loaded[0][1], 16)
            sp.dma_start(x[:, :, 512:1024], x_in[:, :, 512:1024]).then_inc(loaded["x1"], 16)
            sp.dma_start(raw[:, 1, 0:HALF], stream[1][:, 0:HALF]).then_inc(raw_loaded[1][0], 16)
            sp.dma_start(raw[:, 1, HALF:CW], stream[1][:, HALF:CW]).then_inc(raw_loaded[1][1], 16)
            sp.dma_start(staged[:, 0:MASK_N], mask_in).then_inc(loaded["mask"], 16)
            sp.dma_start(staged[:, MASK_N:MASK_N + LEVELS * P], level_in).then_inc(loaded["level"], 16)
            with sp.Fori(0, DEPTH * CHUNKS // RAW - 1) as i:
                for slot in range(RAW):
                    for h in range(2):
                        sp.wait_ge(sem["lo"], i * (2 * RAW) + (2 * slot + h + 1))
                        sp.dma_start(raw[:, slot, h * HALF:(h + 1) * HALF],
                                     stream[bass.ds(i * RAW + (RAW + slot), 1), :, h * HALF:(h + 1) * HALF]
                                     .rearrange("a p n -> (a p) n")).then_inc(raw_loaded[slot][h], 16)
            for slot in range(AHEAD):
                for h in range(2):
                    sp.wait_ge(sem["lo"], 2 * (DEPTH * CHUNKS - RAW + slot) + h + 1)
                    sp.dma_start(raw[:, slot, h * HALF:(h + 1) * HALF], stream[slot][:, h * HALF:(h + 1) * HALF])\
                        .then_inc(raw_loaded[slot][h], 16)
            sp.wait_ge(sem["xout"], at("xout", DEPTH - 1, T))
            sp.dma_start(out[:, :, 0:512], x[:, :, 0:512]).then_inc(stored, 16)
            for t in range(T):
                sp.wait_ge(sem["xout"], at("xout", DEPTH - 1, T + t + 1))
                sp.dma_start(out[:, t, 512:1024], x[:, t, 512:1024]).then_inc(stored, 16)
            sp.wait_ge(stored, 16 * (1 + T))

        @block.gpsimd
        def _(pool):
            pool.wait_ge(loaded["const"], 16)
            with pool.Fori(0, DEPTH) as l:
                for which in range(7):
                    pool.wait_ge(sem["mean"], at("mean", l, which + 1))
                    nc.gpsimd.tensor_tensor(norm(which, 2), norm(which, 1), c_("half")[:, 0:NORM_WIDTH[which]],
                                            ALU.pow).then_inc(sem["rstd"], 1)

        @block.scalar
        def _(act_e):
            e = act_e
            e.dma_start(const[:, 0:P], const_in[:, 0:P]).then_inc(loaded["ident"], 16)
            e.dma_start(const[:, P:CONST_N], const_in[:, P:CONST_N]).then_inc(loaded["const"], 16)

            def split_chunk(c, l):
                e.wait_ge(sem["mm"], at("mm", l, c - (RING - 1)))
                for cols, halves in pieces(c):
                    for h in range(2) if halves == 2 else [cols.start // HALF]:
                        e.wait_ge(raw_loaded[c % RAW][h], (l * (CHUNKS // RAW) + (c // RAW + 1)) * 16)
                    nc.scalar.activation(w_hi[:, c % RING, cols], raw[:, c % RAW, cols], ACT.Copy)\
                        .then_inc(sem["hi"], halves)

            def transpose_hi(l, k, h, bank, gain):
                for t in range(T):
                    e.wait_ge(sem["xT"], at("xT", l, k * T + t + 1))
                    for j in range(4):
                        col = 4 * h + j
                        i = nc.scalar.activation(xT_hi[:, t, col, :], wk[:, bank + t, j * P:(j + 1) * P], ACT.Copy,
                                                 scale=gain[:, col:col + 1])
                    i.then_inc(sem["xT_hi"], 1)

            e.wait_ge(setup, 2)
            nc.scalar.activation(small[:, 8:12], small[:, 4:8], ACT.Exp).then_inc(setup, 1)
            e.wait_ge(sem["mixg"], at("mixg", 0, 0))
            transpose_hi(0, -1, 0, 2, mixg)
            for c in range(AHEAD):
                split_chunk(c, 0)

            with e.Fori(0, DEPTH) as l:
                split = [AHEAD]

                def split_to(p):
                    while split[0] < min(p + RING, CHUNKS + AHEAD):
                        split_chunk(split[0], l)
                        split[0] += 1

                def merged_hi(h):
                    for t in range(T):
                        e.wait_ge(sem["xT"], at("xT", l, (1 + h) * T + t + 1))
                        nc.scalar.activation(mT_hi[:, t, 4 * h:4 * h + 4, :].rearrange("p k s -> p (k s)"),
                                             wk[:, 2 * h + t, :], ACT.Copy, scale=0.5).then_inc(sem["xT_hi"], 1)

                def evacuate_z(b):
                    e.wait_ge(sem["mm"], at("mm", l, 2 * b + 2))
                    for t in range(T):
                        n = Z_BLOCKS[b][1]
                        nc.scalar.activation(z_of[b][:, t, 0:n], acc[:, 2 * (b % 2) + t, 0:n], ACT.Copy,
                                             scale=norm(NORM1, 2)[:, t:t + 1])\
                            .then_inc(sem["z"], 1)

                def gate_tanh(g):
                    branch, half = g // 2, g % 2
                    if g < 7:
                        e.wait_ge(sem["mm"], at("mm", l, GATE[branch][half][1] + 1))
                    else:
                        e.wait_ge(sem["last_gate"], at("last_gate", l, 1))
                    if branch >= 2:
                        e.wait_ge(sem["merge"], at("merge", l, 4 * (branch - 2) + T * (half + 1)))
                    for t in range(T):
                        nc.scalar.activation(gates[:, branch % 2, t, half * 512:half * 512 + 512],
                                             acc[:, 2 * half + t, :], ACT.Tanh, scale=tok[:, 0, t:t + 1])\
                            .then_inc(sem["gate"], 1)

                def exps(u, scale):
                    t = u % 2
                    e.wait_ge(sem["top"], at("top", l, u + 1))
                    if u:
                        e.wait_ge(sem["pT"], at("pT", l, PT_DONE[u - 1]))
                    if u // 2 == 1:
                        c = slice(4 * u, 4 * u + 4)
                        nc.scalar.activation(esink[:, c], esink[:, c], ACT.Exp)
                    for h in range(H):
                        col = (h // 2) * SEQ
                        i = nc.scalar.activation(prob[:, h, 0:t + 1, :].rearrange("p k s -> p (k s)"),
                                                 wk[:, h % 2, col:col + (t + 1) * P], ACT.Exp,
                                                 bias=negm[:, 4 * u + h:4 * u + h + 1], scale=scale,
                                                 accum_out=rowsum[:, 4 * u + h:4 * u + h + 1])
                    i.then_inc(sem["prob"], 1)

                def pT_copy(u):
                    if u:
                        e.wait_ge(sem["pv"], at("pv", l, u))
                    for k in range(u % 2 + 1):
                        n = (PT_DONE[u - 1] if u else 0) + k + 1
                        e.wait_ge(sem["pT"], at("pT", l, n))
                        nc.scalar.activation(pT[:, k, :, :].rearrange("p h s -> p (h s)"), wk[:, 2 + k, :], ACT.Copy)\
                            .then_inc(sem["pT_sb"], 1)

                def yT_hi_copy(n):
                    e.wait_ge(sem["yT"], at("yT", l, n + 1))
                    if n >= 2:
                        e.wait_ge(sem["mm"], at("mm", l, PROJ[n - 2] + 1))
                    nc.scalar.activation(yT_hi[:, n % 2].rearrange("p c t s -> p (c t s)"), wk[:, 2, :], ACT.Copy)\
                        .then_inc(sem["yT_hi"], 1)

                def squares(first):
                    for t in range(T):
                        nc.scalar.activation(wide[:, t * D:(t + 1) * D], x[:, t, :], ACT.Square,
                                             accum_out=norm(first, 0)[:, t:t + 1]).then_inc(sem["sumsq"], 1)

                transpose_hi(l, 0, 1, 0, mixg)
                split_to(-1)
                e.wait_ge(sem["xout"], at("xout", l, 0))
                squares(NORM1)
                split_to(0)
                e.wait_ge(sem["rstd"], at("rstd", l, NORM1 + 1))
                evacuate_z(0)
                split_to(1)
                e.wait_ge(sem["b_in"], at("b_in", l, 2))
                nc.scalar.activation(bE, wk[:, 1, :], ACT.Exp, scale=-1.0).then_inc(sem["b_e"], 1)
                nc.scalar.activation(bQ, wk[:, 0, :], ACT.Tanh, scale=0.5).then_inc(sem["b_tq"], 1)
                split_to(2)
                evacuate_z(1)
                e.wait_ge(sem["d_zf"], at("d_zf", l, 1))
                nc.scalar.activation(dsm[:, 1, :], lf, ACT.Abs).then_inc(sem["d_abs"], 1)
                e.wait_ge(sem["d_abs"], at("d_abs", l, 1))
                nc.scalar.activation(dsm[:, 2, :], dsm[:, 1, :], ACT.Exp, scale=-1.0).then_inc(sem["d_e"], 1)
                e.wait_ge(sem["d_e"], at("d_e", l, 1))
                nc.scalar.activation(dsm[:, 3, :], dsm[:, 2, :], ACT.Ln, bias=1.0).then_inc(sem["d_ln"], 1)
                split_to(3)
                e.wait_ge(sem["b_f"], at("b_f", l, 1))
                nc.scalar.activation(bK, bK, ACT.Ln).then_inc(sem["b_ln"], 1)

                def level_exp(j):
                    e.wait_ge(sem["b_d"], at("b_d", l, j))
                    nc.scalar.activation(bE, bE, ACT.Abs).then_inc(sem["b_abs"], 1)
                    e.wait_ge(sem["b_abs"], at("b_abs", l, j))
                    nc.scalar.activation(bE, bE, ACT.Exp, scale=-1.0).then_inc(sem["b_E"], 1)

                split_to(4)
                level_exp(1)
                split_to(5)
                evacuate_z(2)
                level_exp(2)
                split_to(6)
                level_exp(3)
                split_to(7)
                evacuate_z(3)
                e.wait_ge(sem["z"], at("z", l, 8))
                nc.scalar.activation(square[:, 0:1024], region("wide", 1024, 1024), ACT.Square)\
                    .then_inc(sem["ad_sq"], 1)
                level_exp(4)
                split_to(8)
                level_exp(5)
                split_to(9)
                evacuate_z(4)
                e.wait_ge(sem["z"], at("z", l, 10))
                e.wait_ge(sem["mean"], at("mean", l, NORM_D + 1))
                nc.scalar.activation(square[:, 0:768].rearrange("p (t c) -> p t c", t=T), z_a[:, :, 0:384], ACT.Square)\
                    .then_inc(sem["ad_sq"], 1)
                level_exp(6)
                split_to(10)
                level_exp(7)
                e.wait_ge(sem["par"], at("par", l, 1))
                e.wait_ge(sem["ad_T"], at("ad_T", l, 1))
                nc.scalar.activation(region("qkT", 0, 512), wk[:, 2, :], ACT.Copy).then_inc(sem["ad_sb"], 1)
                e.wait_ge(sem["ad_T"], at("ad_T", l, 2))
                nc.scalar.activation(region("qkT", 512, 512), wk[:, 3, :], ACT.Copy, scale=p_("gd"))\
                    .then_inc(sem["ad_sb"], 1)
                split_to(11)
                evacuate_z(5)
                e.wait_ge(sem["z"], at("z", l, 12))
                for t in range(T):
                    nc.scalar.activation(junk[:, t * C_Q:(t + 1) * C_Q], z_c[:, t, 0:C_Q], ACT.Square,
                                         accum_out=norm(NORM_C1, 0)[:, t:t + 1])
                for t in range(T):
                    i = nc.scalar.activation(junk[:, (4 + t) * C_KV:(5 + t) * C_KV], z_c[:, t, C_Q:C_Q + C_KV], ACT.Square,
                                             accum_out=norm(NORM_C1, 0)[:, T + t:T + t + 1])
                i.then_inc(sem["c_sq"], 1)
                e.wait_ge(sem["b_QK"], at("b_QK", l, LEVELS))
                for hp in range(2):
                    nc.scalar.activation(bE[:, hp * SEQ:hp * SEQ + P], bT[:, hp * SEQ:hp * SEQ + P], ACT.Exp,
                                         scale=-1.0, bias=bT[:, hp * SEQ + P - 1:hp * SEQ + P])
                    i = nc.scalar.activation(bE[:, hp * SEQ + P:(hp + 1) * SEQ], bT[:, hp * SEQ + P:(hp + 1) * SEQ],
                                             ACT.Exp)
                i.then_inc(sem["b_Ex"], 1)
                split_to(12)
                e.wait_ge(sem["ad_T"], at("ad_T", l, 3))
                nc.scalar.activation(region("qkT", 1024, 512), wk[:, 2, :], ACT.Copy).then_inc(sem["ad_sb"], 1)
                e.wait_ge(sem["ad_T"], at("ad_T", l, 4))
                nc.scalar.activation(region("qkT", 1536, 512), wk[:, 3, :], ACT.Copy, scale=p_("ga"))\
                    .then_inc(sem["ad_sb"], 1)
                split_to(13)
                for odd in range(2):
                    e.wait_ge(sem["b_cross"], at("b_cross", l, odd + 1))
                    nc.scalar.activation(AT[2][:, 2 * odd:2 * odd + 2, :].rearrange("p h s -> p (h s)"),
                                         wk[:, 2 + odd, 0:2 * P], ACT.Copy).then_inc(sem["b_atx"], 1)
                e.wait_ge(sem["tok"], at("tok", l, 1))
                gate_tanh(0)
                exps(0, 1.0)
                split_to(14)
                e.wait_ge(sem["c_T"], at("c_T", l, 2))
                for k in range(2):
                    nc.scalar.activation(cT_hi[:, k].rearrange("p t s -> p (t s)"), wk[:, 1, k * SEQ:(k + 1) * SEQ],
                                         ACT.Copy, scale=p_("cq")[:, k:k + 1])
                nc.scalar.activation(cT_hi[:, 2].rearrange("p t s -> p (t s)"), wk[:, 2, 0:SEQ], ACT.Copy,
                                     scale=p_("ckv")).then_inc(sem["c_hi"], 1)
                e.wait_ge(sem["b_o"], at("b_o", l, 1))
                e.wait_ge(sem["b_QK"], at("b_QK", l, LEVELS + 1))
                nc.scalar.activation(bE, wk[:, 3, :], ACT.Square).then_inc(sem["b_sq"], 1)
                nc.scalar.activation(bQ.rearrange("p (t c) -> p t c", t=T), z_ig[:, :, BW:2 * BW], ACT.Tanh, scale=0.5)\
                    .then_inc(sem["b_tg"], 1)
                split_to(15)
                gate_tanh(1)
                pT_copy(0)
                exps(1, 1.0)
                split_to(16)
                split_to(17)
                gate_tanh(2)
                pT_copy(1)
                exps(2, 1.0)
                split_to(18)
                yT_hi_copy(0)
                split_to(19)
                gate_tanh(3)
                pT_copy(2)
                yT_hi_copy(1)
                exps(3, 1.0)
                e.wait_ge(sem["mm"], at("mm", l, UQ + 1))
                e.wait_ge(sem["b_y"], at("b_y", l, 1))
                for t in range(T):
                    nc.scalar.activation(c_q[:, 4 * t:4 * t + 4, :].rearrange("p g c -> p (g c)"),
                                         acc[:, t, 0:H * C_DQ], ACT.Copy).then_inc(sem["u"], 1)
                split_to(20)
                e.wait_ge(sem["mm"], at("mm", l, UKV + 1))
                for t in range(T):
                    nc.scalar.activation(c_kv[:, 4 * t:4 * t + 4, :].rearrange("p g c -> p (g c)"), acc[:, 2 + t, :],
                                         ACT.Copy).then_inc(sem["u"], 1)
                pT_copy(3)
                split_to(21)
                e.wait_ge(sem["u"], at("u", l, 4))
                nc.scalar.activation(c_s.rearrange("p (g c) -> p g c", c=C_DQ), c_q, ACT.Square)
                nc.scalar.activation(c_s2.rearrange("p (g c) -> p g c", c=HD), c_kv[:, :, 0:HD], ACT.Square)
                for t in range(T):
                    i = nc.scalar.activation(c_r[:, 32 * t:32 * t + 32], z_c[:, t, 384:416], ACT.Square,
                                             accum_out=dsm[:, 4, t:t + 1])
                i.then_inc(sem["c_sq2"], 1)
                split_to(24)
                gate_tanh(4)
                yT_hi_copy(2)
                for n in range(4):
                    e.wait_ge(sem["c_T2"], at("c_T2", l, n + 1))
                    nc.scalar.activation(arena[0:C_DQ, area["qkT"][0] + 512 * n:area["qkT"][0] + 512 * n + 512],
                                         wk[0:C_DQ, n, :], ACT.Copy).then_inc(sem["c_sb2"], 1)
                gate_tanh(5)
                split_to(25)
                exps(4, C_DQ ** -0.5)
                split_to(26)
                pT_copy(4)
                exps(5, C_DQ ** -0.5)
                split_to(27)
                split_to(28)
                gate_tanh(6)
                pT_copy(5)
                split_to(31)
                yT_hi_copy(3)
                split_to(32)
                gate_tanh(7)
                merged_hi(0)
                split_to(34)
                merged_hi(1)
                split_to(36)
                transpose_hi(l, 3, 0, 0, p_("ffn"))
                split_to(37)
                transpose_hi(l, 4, 1, 2, p_("ffn"))
                e.wait_ge(sem["xmid"], at("xmid", l, 4))
                squares(NORM2)

                def ffn_split(c, i):
                    e.wait_ge(sem["mm"], at("mm", l, i * 4 + (c - (RING - 1))))
                    for h in range(2):
                        cols = slice(h * HALF, (h + 1) * HALF)
                        e.wait_ge(raw_loaded[c % RAW][h], (l * (CHUNKS // RAW) + i * 2 + (c // RAW + 1)) * 16)
                        nc.scalar.activation(w_hi[:, c % RING, cols], raw[:, c % RAW, cols], ACT.Copy)\
                            .then_inc(sem["hi"], 1)

                def ffn_tanh(b, i):
                    e.wait_ge(sem["mm"], at("mm", l, i * 4 + (FFN0 + 2 * b + 2)))
                    for t in range(T):
                        nc.scalar.activation(sw[:, b % 2, t, :], acc[:, 2 * (b % 2) + t, 0:256], ACT.Tanh,
                                             scale=tok[:, 1, t:t + 1]).then_inc(sem["tanh"], 1)

                def ffn_hi(b, i):
                    e.wait_ge(sem["aT"], at("aT", l, i * 2 + (b + 1)))
                    to = aT_hi[:, b * 512:b * 512 + 512] if isinstance(i, int) else aT_hi[:, bass.ds(i * 1024 + b * 512, 512)]
                    nc.scalar.activation(to, wk[:, b % 2, :], ACT.Copy, scale=0.5).then_inc(sem["aT_hi"], 1)

                split_to(39)
                e.wait_ge(sem["tok"], at("tok", l, 2))
                ffn_tanh(0, 0)
                with e.Fori(0, FFN_BLOCKS // 2) as i:
                    for b in (1, 2):
                        ffn_split(FFN0 + 2 * b + 3, i)
                        ffn_split(FFN0 + 2 * b + 4, i)
                        ffn_tanh(b, i)
                        ffn_hi(b - 1, i)
                split[0] = DOWN0 + 3
                split_to(DOWN0)
                ffn_hi(FFN_BLOCKS - 1, 0)
                split_to(DOWN_HALF + 1)
                e.wait_ge(sem["mixg"], at("mixg", l, 1))
                transpose_hi(l, 5, 0, 2, mixg)
                split_to(CHUNKS)

        @block.vector
        def _(v):
            V = nc.vector
            v.wait_ge(loaded["par"], 16)
            V.tensor_copy(mixg[:, :], par[:, 0, PARX["mix"][0]:PARX["mix"][0] + DK]).then_inc(sem["mixg"], 1)
            V.memset(par[:, DEPTH, :], 1.0)
            lb = PARX["lb"][0]
            lo_, om_ = PARX["low"][0], PARX["oml"][0]
            V.tensor_tensor(small[:, 0:2], par[:, 0, lb:lb + 2], par[:, 1, lb:lb + 2], ALU.max).then_inc(setup, 1)
            v.wait_ge(setup, 1)
            V.tensor_tensor(small[:, 4:8].rearrange("p (l c) -> p l c", l=2), par[:, 0:DEPTH, lb:lb + 2],
                            small[:, 0:2][:, None, :].to_broadcast([P, 2, 2]), ALU.subtract).then_inc(setup, 1)

            def split_chunk(c, l):
                done = 2 * c
                for cols, halves in pieces(c):
                    done += halves
                    v.wait_ge(sem["hi"], at("hi", l, done))
                    V.tensor_tensor(w_lo[:, c % RING, cols], raw[:, c % RAW, cols], w_hi[:, c % RING, cols].bitcast(F32),
                                    ALU.subtract).then_inc(sem["lo"], halves)

            def transpose_lo(l, k, h, bank, gain):
                for t in range(T):
                    v.wait_ge(sem["xT_hi"], at("xT_hi", l, k * T + t + 1))
                    for j in range(4):
                        col = 4 * h + j
                        i = V.scalar_tensor_tensor(xT_lo[:, t, col, :], wk[:, bank + t, j * P:(j + 1) * P],
                                                   gain[:, col:col + 1], xT_hi[:, t, col, :].bitcast(F32), ALU.mult,
                                                   ALU.subtract)
                    i.then_inc(sem["xT_lo"], 1)

            v.wait_ge(sem["mixg"], at("mixg", 0, 0))
            transpose_lo(0, -1, 0, 2, mixg)
            split_chunk(0, 0)
            v.wait_ge(setup, 3)
            V.tensor_tensor(small[:, 12:14], small[:, 8:10], small[:, 10:12], ALU.add).then_inc(setup, 1)
            v.wait_ge(setup, 4)
            V.reciprocal(small[:, 14:16], small[:, 12:14]).then_inc(setup, 1)
            v.wait_ge(setup, 5)
            V.tensor_tensor(par[:, 1, lo_:lo_ + 2], small[:, 10:12], small[:, 14:16], ALU.mult).then_inc(setup, 1)
            V.memset(par[:, 0, lo_:lo_ + 2], 0.0).then_inc(setup, 1)
            v.wait_ge(setup, 7)
            V.tensor_scalar(par[:, 0:DEPTH, om_:om_ + 2], par[:, 0:DEPTH, lo_:lo_ + 2], -1.0, 1.0, ALU.mult, ALU.add)\
                .then_inc(setup, 1)
            for name, q, k in (("ga", "aq", "ak"), ("gd", "dq", "dk")):
                col = PARX[name][0]
                V.scalar_tensor_tensor(par[:, 0:DEPTH, col:col + 1], par[:, 0:DEPTH, PARX[q][0]:PARX[q][0] + 1], HD ** -0.5,
                                       par[:, 0:DEPTH, PARX[k][0]:PARX[k][0] + 1], ALU.mult, ALU.mult).then_inc(setup, 1)
            v.wait_ge(loaded["x0"], 16)
            v.wait_ge(loaded["x1"], 16)
            v.sem_inc(sem["xout"], HEADS["xout"])
            v.sem_inc(sem["act"], HEADS["act"])
            v.sem_inc(sem["aT_lo"], HEADS["aT_lo"])
            split_chunk(1, 0)
            v.wait_ge(loaded["mask"], 16)
            v.wait_ge(loaded["level"], 16)
            V.tensor_copy(level[:, :, :].rearrange("p l s -> p (l s)"), staged[:, MASK_N:MASK_N + LEVELS * P])\
                .then_inc(setup, 1)
            V.tensor_copy(mask[:, :], staged[:, 0:MASK_N]).then_inc(setup, 1)
            v.wait_ge(setup, SETUP)
            v.wait_ge(loaded["ident"], 16)
            v.wait_ge(loaded["const"], 16)

            with v.Fori(0, DEPTH) as l:
                split = [AHEAD]
                links = [0]

                def link(i):
                    i.then_inc(sem["dve"], 1)
                    links[0] += 1
                    v.wait_ge(sem["dve"], at("dve", l, links[0]))

                def split_to(p):
                    while split[0] < min(p + RING, CHUNKS + AHEAD):
                        split_chunk(split[0], l)
                        split[0] += 1

                def merged_lo(h):
                    for t in range(T):
                        v.wait_ge(sem["xT_hi"], at("xT_hi", l, (1 + h) * T + t + 1))
                        cols = slice(4 * h, 4 * h + 4)
                        V.scalar_tensor_tensor(mT_lo[:, t, cols, :].rearrange("p k s -> p (k s)"), wk[:, 2 * h + t, :], 0.5,
                                               mT_hi[:, t, cols, :].rearrange("p k s -> p (k s)").bitcast(F32),
                                               ALU.mult, ALU.subtract).then_inc(sem["xT_lo"], 1)

                def mean(which, cols, scale):
                    i = V.tensor_scalar(norm(which, 1)[:, cols], norm(which, 0)[:, cols], scale, EPS, ALU.mult, ALU.add)
                    return i

                def norm_x(n, which):
                    v.wait_ge(sem["sumsq"], at("sumsq", l, (n + 1) * T))
                    mean(which, slice(0, T), 1.0 / D).then_inc(sem["mean"], 1)

                def norm_halved(n, which):
                    v.wait_ge(sem["rstd"], at("rstd", l, which + 1))
                    if n == 1:
                        V.tensor_tensor(tok[:, 2, :], norm(which, 2), norm(which, 2), ALU.mult)
                    V.tensor_scalar(tok[:, n, :], norm(which, 2), 0.5, None, ALU.mult).then_inc(sem["tok"], 1)

                def tops(u, scale, sinks=False):
                    t = u % 2
                    c = slice(4 * u, 4 * u + 4)
                    v.wait_ge(sem["score"], at("score", l, u + 1))
                    link(V.reduce_max(mx[:, c].rearrange("p (h o) -> p h o", h=2),
                                      wk[:, 0:2, :].rearrange("p o (h m) -> p h o m", h=2)[:, :, :, 0:(t + 1) * P], axis=AX.X))
                    if sinks:
                        link(V.tensor_tensor(mx[:, c], mx[:, c], p_("sink"), ALU.max))
                        link(V.tensor_tensor(esink[:, c], p_("sink"), mx[:, c], ALU.subtract))
                    V.tensor_scalar(negm[:, c], mx[:, c], -scale, None, ALU.mult).then_inc(sem["top"], 1)

                def attended(u, b, sinks=False):
                    t = u % 2
                    c = slice(4 * u, 4 * u + 4)
                    v.wait_ge(sem["pv"], at("pv", l, u + 1))
                    if sinks:
                        link(V.tensor_tensor(rowsum[:, c], rowsum[:, c], esink[:, c], ALU.add))
                    link(V.reciprocal(rden[:, c], rowsum[:, c]))
                    V.tensor_tensor(y[:, b, t, :].rearrange("p (h c) -> p h c", h=H),
                                    wk[:, 3, 0:BW].rearrange("p (h c) -> p h c", h=H),
                                    rden[:, c][:, :, None].to_broadcast([P, H, HD]), ALU.mult).then_inc(sem["y"], 1)

                def yT_lo_copy(n):
                    v.wait_ge(sem["yT_hi"], at("yT_hi", l, n + 1))
                    V.tensor_tensor(yT_lo[:, n % 2].rearrange("p c t s -> p (c t s)"), wk[:, 2, :],
                                    yT_hi[:, n % 2].rearrange("p c t s -> p (c t s)").bitcast(F32), ALU.subtract)\
                        .then_inc(sem["yT_lo"], 1)

                def merge_half(n, second):
                    half, bank = PROJ_HALVES[n][second], 2 * PROJ_PAIR[n][second]
                    if second:
                        v.wait_ge(sem["mm"], at("mm", l, PROJ[n] + 1 if n < 3 else OUT0))
                    else:
                        v.wait_ge(sem["proj"], at("proj", l, n + 1))
                    v.wait_ge(sem["gate"], at("gate", l, 4 * n + 2 * half + 2))
                    cols = slice(half * 512, half * 512 + 512)
                    if n == 0:
                        for t in range(T):
                            V.scalar_tensor_tensor(merged[:, t, cols], gates[:, 0, t, cols], 1.0, acc[:, bank + t, :],
                                                   ALU.add, ALU.mult).then_inc(sem["merge"], 1)
                        return
                    for t in range(T):
                        g = gates[:, n % 2, t, cols]
                        V.scalar_tensor_tensor(g, g, 1.0, acc[:, bank + t, :], ALU.add, ALU.mult)\
                            .then_inc(sem["gated"], 1)
                    for t in range(T):
                        g = gates[:, n % 2, t, cols]
                        v.wait_ge(sem["gated"], at("gated", l, 4 * (n - 1) + 2 * second + t + 1))
                        V.tensor_tensor(merged[:, t, cols], merged[:, t, cols], g, ALU.add).then_inc(sem["merge"], 1)

                transpose_lo(l, 0, 1, 0, mixg)
                V.tensor_copy(now[:, :], par[:, bass.ds(l, 1), :].rearrange("p a n -> p (a n)")).then_inc(sem["par"], 1)
                split_to(-1)
                norm_x(0, NORM1)
                split_to(1)
                norm_halved(0, NORM1)
                v.wait_ge(sem["par"], at("par", l, 1))
                v.wait_ge(sem["b_tq"], at("b_tq", l, 1))
                V.scalar_tensor_tensor(bq, bQ, 1.0, wk[:, 0, :], ALU.add, ALU.mult).then_inc(sem["b_q"], 1)
                link(V.tensor_scalar(bE, bE, 1.0, None, ALU.add))
                split_to(2)
                v.wait_ge(sem["z"], at("z", l, 4))
                V.tensor_tensor(lf.rearrange("p (t h) -> p t h", t=T), z_dv[:, :, BW:BW + H],
                                p_("fb")[:, None, :].to_broadcast([P, T, H]), ALU.add).then_inc(sem["d_zf"], 1)
                link(V.reciprocal(bT, bE))
                for hp in range(2):
                    c = slice(hp * SEQ, (hp + 1) * SEQ)
                    i = V.tensor_scalar(bT[:, c], bT[:, c], p_("oml")[:, hp:hp + 1], p_("low")[:, hp:hp + 1], ALU.mult,
                                        ALU.add)
                link(i)
                V.tensor_scalar(bk, bT, -0.5, 0.5, ALU.mult, ALU.add)
                V.tensor_scalar(bK, bT, 1e-19, None, ALU.max).then_inc(sem["b_f"], 1)
                v.wait_ge(sem["b_ln"], at("b_ln", l, 1))
                for n in range(4):
                    c = slice(n * P, (n + 1) * P)
                    i = V.tensor_tensor_scan(bT[:, c], c_("ones"), bK[:, c], 0.0, ALU.mult, ALU.add)
                i.then_inc(sem["b_scan"], 1)
                v.wait_ge(sem["b_scan"], at("b_scan", l, 1))

                def level_diff(j):
                    m = 2 ** j // 2
                    if j > 1:
                        v.wait_ge(sem["b_QK"], at("b_QK", l, j - 1))
                    blocks = bT.rearrange("p (n m) -> p n m", m=2 * m)
                    V.tensor_tensor(bE.rearrange("p (n m) -> p n m", m=2 * m), blocks,
                                    blocks[:, :, m - 1:m].to_broadcast([P, 512 // (2 * m), 2 * m]), ALU.subtract)\
                        .then_inc(sem["b_d"], 1)

                def sides(a, m):
                    two = a.rearrange("p (n two m) -> p n two m", two=2, m=m)
                    return two[:, :, 0], two[:, :, 1]

                def level_qk(j):
                    v.wait_ge(sem["b_E"], at("b_E", l, j))
                    if j > 1:
                        v.wait_ge(sem["b_lev"], at("b_lev", l, 2 * j))
                    m = 2 ** j // 2
                    V.tensor_tensor(sides(bQ, m)[1], sides(bq, m)[1], sides(bE, m)[1], ALU.mult)
                    V.tensor_tensor(sides(bK, m)[0], sides(bk, m)[0], sides(bE, m)[0], ALU.mult).then_inc(sem["b_QK"], 1)

                def level_take(j):
                    for odd in range(2):
                        bank = wk[:, odd, :].rearrange("p (h s) -> p h s", h=H)
                        if j == 0:
                            v.wait_ge(sem["b_lev"], at("b_lev", l, odd + 1))
                            V.tensor_tensor(AT[odd], bank, c_("ident")[:, None, :].to_broadcast([P, H, P]), ALU.mult)\
                                .then_inc(sem["b_at"], 1)
                        else:
                            m = 2 ** j // 2
                            n = P // (2 * m)
                            right = [a.rearrange("p h (n two m) -> p h n two m", two=2, m=m)[:, :, :, 1]
                                     for a in (AT[odd], bank)]
                            pairs = level[:, j - 1, :].rearrange("p (n two m) -> p n two m", two=2, m=m)[:, :, 1]
                            V.copy_predicated(right[0], pairs[:, None].to_broadcast([P, H, n, m]), right[1])\
                                .then_inc(sem["b_at"], 1)

                level_diff(1)
                split_to(3)
                v.wait_ge(sem["d_ln"], at("d_ln", l, 1))
                link(V.tensor_scalar(dsm[:, 4, :], lf, 0.0, None, ALU.min))
                V.tensor_tensor(lf, dsm[:, 4, :], dsm[:, 3, :], ALU.subtract).then_inc(sem["d_lf"], 1)
                v.wait_ge(sem["d_lf"], at("d_lf", l, 1))
                for t in range(T):
                    i = V.tensor_tensor(X[:, t], c_("stri")[:, None, :].to_broadcast([P, H, P]),
                                        lf[:, H * t:H * t + H][:, :, None].to_broadcast([P, H, P]), ALU.mult)
                i.then_inc(sem["d_x"], 1)
                split_to(4)
                for j in range(1, LEVELS + 1):
                    level_qk(j)
                    level_take(j - 1)
                    if j < LEVELS:
                        level_diff(j + 1)
                    if j == 4:
                        v.wait_ge(sem["ad_sq"], at("ad_sq", l, 1))
                        link(V.reduce_sum(norm(NORM_D, 0), square[:, 0:1024].rearrange("p (g c) -> p g c", c=HD),
                                          axis=AX.X))
                        mean(NORM_D, slice(0, 16), 1.0 / HD).then_inc(sem["mean"], 1)
                    if j == 5:
                        v.wait_ge(sem["rstd"], at("rstd", l, NORM_D + 1))
                        zq = region("wide", 1024, 1024).rearrange("p (g c) -> p g c", c=HD)
                        V.tensor_tensor(zq, zq, norm(NORM_D, 2)[:, :, None].to_broadcast([P, 16, HD]), ALU.mult)\
                            .then_inc(sem["ad_n"], 1)
                    if j == 6:
                        v.wait_ge(sem["ad_sq"], at("ad_sq", l, 2))
                        link(V.reduce_sum(norm(NORM_A, 0), square[:, 0:768].rearrange("p (g c) -> p g c", c=HD),
                                          axis=AX.X))
                        mean(NORM_A, slice(0, 12), 1.0 / HD).then_inc(sem["mean"], 1)
                    if j == 7:
                        v.wait_ge(sem["rstd"], at("rstd", l, NORM_A + 1))
                        for t in range(T):
                            r = norm(NORM_A, 2)[:, 6 * t:6 * t + 6]
                            q = z_a[:, t, 0:BW].rearrange("p (h c) -> p h c", h=H)
                            V.tensor_tensor(q, q, r[:, 0:H][:, :, None].to_broadcast([P, H, HD]), ALU.mult)
                            k = z_a[:, t, BW:BW + P].rearrange("p (h c) -> p h c", h=A_KV)
                            for dup in range(2):
                                i = V.tensor_tensor(kdup[:, t, :].rearrange("p (h d c) -> p h d c", h=A_KV, d=2)[:, :, dup],
                                                    k, r[:, H:H + A_KV][:, :, None].to_broadcast([P, A_KV, HD]), ALU.mult)
                        i.then_inc(sem["ad_n"], 1)
                    split_to(4 + j)
                split_to(12)
                v.wait_ge(sem["b_Ex"], at("b_Ex", l, 1))
                v.wait_ge(sem["b_lev"], at("b_lev", l, 2 * (LEVELS + 1)))
                halves = [a.rearrange("p (h t s) -> p h t s", h=2, t=T) for a in (bq, bk, bE, bQ, bK)]
                V.tensor_tensor(halves[3][:, :, 1], halves[0][:, :, 1], halves[2][:, :, 1], ALU.mult)
                V.tensor_tensor(halves[4][:, :, 0], halves[1][:, :, 0], halves[2][:, :, 0], ALU.mult)\
                    .then_inc(sem["b_QK"], 1)
                level_take(LEVELS)
                v.wait_ge(sem["c_sq"], at("c_sq", l, 1))
                mean(NORM_C1, slice(0, T), 1.0 / C_Q)
                mean(NORM_C1, slice(T, 2 * T), 1.0 / C_KV).then_inc(sem["mean"], 1)
                split_to(13)
                tops(0, 1.0)
                v.wait_ge(sem["rstd"], at("rstd", l, NORM_C1 + 1))
                for t in range(T):
                    r = norm(NORM_C1, 2)
                    V.tensor_scalar(z_c[:, t, 0:C_Q], z_c[:, t, 0:C_Q], r[:, t:t + 1], None, ALU.mult)
                    i = V.tensor_scalar(z_c[:, t, C_Q:C_Q + C_KV], z_c[:, t, C_Q:C_Q + C_KV], r[:, T + t:T + t + 1], None,
                                        ALU.mult)
                i.then_inc(sem["c_n"], 1)
                split_to(14)
                v.wait_ge(sem["c_hi"], at("c_hi", l, 1))
                for k in range(2):
                    V.scalar_tensor_tensor(cT_lo[:, k].rearrange("p t s -> p (t s)"), wk[:, 1, k * SEQ:(k + 1) * SEQ],
                                           p_("cq")[:, k:k + 1], cT_hi[:, k].rearrange("p t s -> p (t s)").bitcast(F32),
                                           ALU.mult, ALU.subtract)
                V.scalar_tensor_tensor(cT_lo[:, 2].rearrange("p t s -> p (t s)"), wk[:, 2, 0:SEQ], p_("ckv"),
                                       cT_hi[:, 2].rearrange("p t s -> p (t s)").bitcast(F32), ALU.mult, ALU.subtract)\
                    .then_inc(sem["c_lo"], 1)
                v.wait_ge(sem["b_sq"], at("b_sq", l, 1))
                link(V.reduce_sum(norm(NORM_B, 0), bE.rearrange("p (g c) -> p g c", c=HD), axis=AX.X))
                mean(NORM_B, slice(0, 8), 1.0 / HD).then_inc(sem["mean"], 1)
                split_to(15)
                tops(1, 1.0)
                v.wait_ge(sem["rstd"], at("rstd", l, NORM_B + 1))
                v.wait_ge(sem["b_tg"], at("b_tg", l, 1))
                g8 = [P, 8, HD]
                link(V.tensor_tensor(bT.rearrange("p (g c) -> p g c", c=HD), wk[:, 3, :].rearrange("p (g c) -> p g c", c=HD),
                                     norm(NORM_B, 2)[:, :, None].to_broadcast(g8), ALU.mult))
                V.tensor_tensor(bT.rearrange("p (g c) -> p g c", c=HD), bT.rearrange("p (g c) -> p g c", c=HD),
                                p_("bo")[:, None, :].to_broadcast(g8), ALU.mult)
                link(V.scalar_tensor_tensor(bK.rearrange("p (t c) -> p t c", t=T), bQ.rearrange("p (t c) -> p t c", t=T),
                                            1.0, z_ig[:, :, BW:2 * BW], ALU.add, ALU.mult))
                V.scalar_tensor_tensor(y[:, 0].rearrange("p t c -> p (t c)"), bT, 0.5, bK, ALU.mult, ALU.mult)\
                    .then_inc(sem["b_y"], 1)
                split_to(16)
                attended(0, 1)
                split_to(17)
                tops(2, 1.0, sinks=True)
                split_to(18)
                attended(1, 1)
                yT_lo_copy(0)
                split_to(19)
                tops(3, 1.0, sinks=True)
                yT_lo_copy(1)
                attended(2, 0, sinks=True)
                split_to(20)
                merge_half(0, 0)
                split_to(21)
                v.wait_ge(sem["c_sq2"], at("c_sq2", l, 1))
                V.reduce_sum(norm(NORM_C2, 0)[:, 0:8], c_s.rearrange("p (g c) -> p g c", c=C_DQ), axis=AX.X)
                link(V.reduce_sum(norm(NORM_C2, 0)[:, 8:16], c_s2.rearrange("p (g c) -> p g c", c=HD), axis=AX.X))
                k8 = norm(NORM_C2, 0)[:, 8:16].rearrange("p (t h) -> p t h", t=T)
                link(V.tensor_tensor(k8, k8, dsm[:, 4, 0:T][:, :, None].to_broadcast([P, T, H]), ALU.add))
                mean(NORM_C2, slice(0, 16), 1.0 / C_DQ).then_inc(sem["mean"], 1)
                merge_half(0, 1)
                attended(3, 0, sinks=True)
                split_to(22)
                v.wait_ge(sem["rstd"], at("rstd", l, NORM_C2 + 1))
                r = norm(NORM_C2, 2)
                link(V.tensor_tensor(c_q, c_q, r[:, 0:8][:, :, None].to_broadcast([P, 8, C_DQ]), ALU.mult))
                V.tensor_tensor(c_q, c_q, p_("cqn")[:, None, :].to_broadcast([P, 8, C_DQ]), ALU.mult)
                V.tensor_tensor(c_k[:, :, 0:HD], c_kv[:, :, 0:HD], r[:, 8:16][:, :, None].to_broadcast([P, 8, HD]), ALU.mult)
                for t in range(T):
                    i = V.tensor_tensor(c_k[:, 4 * t:4 * t + 4, HD:C_DQ], z_c[:, t, 384:416][:, None, :].to_broadcast([P, H, C_ROPE]),
                                        r[:, 8 + 4 * t:12 + 4 * t][:, :, None].to_broadcast([P, H, C_ROPE]), ALU.mult)
                link(i)
                link(V.tensor_tensor(c_k, c_k, p_("ckn")[:, None, :].to_broadcast([P, 8, C_DQ]), ALU.mult))
                half = C_ROPE // 2
                for n, a in enumerate((c_q, c_k)):
                    rot = c_r[:, 256 * n:256 * n + 256].rearrange("p (g c) -> p g c", c=C_ROPE)
                    for t in range(T):
                        g = slice(4 * t, 4 * t + 4)
                        cos = c_("cos")[:, C_ROPE * t:C_ROPE * (t + 1)][:, None, :]
                        sin = c_("sin")[:, C_ROPE * t:C_ROPE * (t + 1)][:, None, :]
                        V.tensor_tensor(rot[:, g, 0:half], a[:, g, HD + half:C_DQ], sin[:, :, 0:half].to_broadcast([P, H, half]),
                                        ALU.mult)
                        link(V.tensor_tensor(rot[:, g, half:C_ROPE], a[:, g, HD:HD + half],
                                             sin[:, :, half:C_ROPE].to_broadcast([P, H, half]), ALU.mult))
                        i = V.tensor_tensor(a[:, g, HD:C_DQ], a[:, g, HD:C_DQ], cos.to_broadcast([P, H, C_ROPE]), ALU.mult)
                    link(i)
                    i = V.tensor_tensor(a[:, :, HD:C_DQ], a[:, :, HD:C_DQ], rot, ALU.add)
                i.then_inc(sem["c_n2"], 1)
                yT_lo_copy(2)
                split_to(24)
                tops(4, C_DQ ** -0.5)
                split_to(25)
                merge_half(1, 0)
                split_to(26)
                tops(5, C_DQ ** -0.5)
                split_to(27)
                merge_half(1, 1)
                attended(4, 1)
                split_to(28)
                split_to(29)
                merge_half(2, 0)
                split_to(30)
                attended(5, 1)
                merge_half(2, 1)
                yT_lo_copy(3)
                split_to(31)
                split_to(32)
                merge_half(3, 0)
                merged_lo(0)
                merge_half(3, 1)
                split_to(33)
                merged_lo(1)

                def residual(done, banks, first):
                    for t in range(T):
                        V.tensor_tensor(x[:, t, first * 512:first * 512 + 512], x[:, t, first * 512:first * 512 + 512],
                                        acc[:, banks + t, :], ALU.add).then_inc(done, 1)

                split_to(35)
                v.wait_ge(sem["mm"], at("mm", l, OUT0 + 3))
                residual(sem["xmid"], 0, 0)
                split_to(36)
                transpose_lo(l, 3, 0, 0, p_("ffn"))
                v.wait_ge(sem["mm"], at("mm", l, OUT0 + 4))
                residual(sem["xmid"], 2, 1)
                split_to(37)
                transpose_lo(l, 4, 1, 2, p_("ffn"))
                V.tensor_copy(mixg[:, :], par[:, bass.ds(l + 1, 1), PARX["mix"][0]:PARX["mix"][0] + DK]
                              .rearrange("p a n -> p (a n)")).then_inc(sem["mixg"], 1)
                norm_x(1, NORM2)

                def ffn_split(c, i):
                    for h in range(2):
                        cols = slice(h * HALF, (h + 1) * HALF)
                        v.wait_ge(sem["hi"], at("hi", l, i * 8 + (2 * c + h + 1)))
                        V.tensor_tensor(w_lo[:, c % RING, cols], raw[:, c % RAW, cols],
                                        w_hi[:, c % RING, cols].bitcast(F32), ALU.subtract).then_inc(sem["lo"], 1)

                def swiglu(b, i):
                    for t in range(T):
                        bank = acc[:, 2 * (b % 2) + t, :]
                        v.wait_ge(sem["tanh"], at("tanh", l, i * 4 + (2 * b + t + 1)))
                        if b and t == 0:
                            v.wait_ge(sem["aT"], at("aT", l, i * 2 + (b - 1)))
                        last = V.scalar_tensor_tensor(sw[:, b % 2, t, :], sw[:, b % 2, t, :], 1.0, bank[:, 0:256], ALU.add,
                                                      ALU.mult)
                    last.then_inc(sem["sw"], 1)
                    v.wait_ge(sem["sw"], at("sw", l, i * 2 + (b + 1)))
                    for t in range(T):
                        bank = acc[:, 2 * (b % 2) + t, :]
                        V.scalar_tensor_tensor(act[:, b % 2, t, :], sw[:, b % 2, t, :], tok[:, 2, t:t + 1],
                                               bank[:, 256:512], ALU.mult, ALU.mult).then_inc(sem["act"], 1)

                def ffn_lo(b, i):
                    v.wait_ge(sem["aT_hi"], at("aT_hi", l, i * 2 + (b + 1)))
                    if isinstance(i, int):
                        hi, lo = aT_hi[:, b * 512:b * 512 + 512], aT_lo[:, b * 512:b * 512 + 512]
                    else:
                        hi, lo = (a[:, bass.ds(i * 1024 + b * 512, 512)] for a in (aT_hi, aT_lo))
                    V.scalar_tensor_tensor(lo, wk[:, b % 2, :], 0.5, hi.bitcast(F32), ALU.mult, ALU.subtract)\
                        .then_inc(sem["aT_lo"], 1)

                split_to(38)
                norm_halved(1, NORM2)
                split_to(39)
                v.wait_ge(sem["tok"], at("tok", l, 2))
                swiglu(0, 0)
                with v.Fori(0, FFN_BLOCKS // 2) as i:
                    for b in (1, 2):
                        ffn_split(FFN0 + 2 * b + 3, i)
                        ffn_split(FFN0 + 2 * b + 4, i)
                        swiglu(b, i)
                        ffn_lo(b - 1, i)
                split[0] = DOWN0 + 3
                split_to(DOWN0)
                ffn_lo(FFN_BLOCKS - 1, 0)
                split_to(DOWN_HALF - 1)
                v.wait_ge(sem["mm"], at("mm", l, DOWN_HALF))
                residual(sem["xout"], 0, 0)
                split_to(DOWN_HALF + 1)
                v.wait_ge(sem["mixg"], at("mixg", l, 1))
                transpose_lo(l, 5, 0, 2, mixg)
                split_to(CHUNKS)
                v.wait_ge(sem["mm"], at("mm", l, CHUNKS))
                residual(sem["xout"], 2, 1)
                assert links[0] == LINKS, links[0]

        @block.tensor
        def _(pe):
            M = nc.tensor
            pe.sem_inc(sem["mm"], HEADS["mm"])
            pe.sem_inc(sem["aT"], HEADS["aT"])
            ident = c_("ident")

            def transposes(bank, tiles, ready):
                for n, a in enumerate(tiles):
                    w = a.shape[-1]
                    i = M.transpose(bank[0:w, n * P:(n + 1) * P], a, ident)
                i.then_inc(ready, 1)

            def half_transposes(a, h, bank):
                for t in range(T):
                    transposes(wk[:, bank + t, :], [a[:, t, (4 * h + k) * P:(4 * h + k + 1) * P] for k in range(4)],
                               sem["xT"])

            pe.wait_ge(loaded["ident"], 16)
            pe.wait_ge(loaded["x0"], 16)
            half_transposes(x, 0, 2)

            with pe.Fori(0, DEPTH) as l:
                def products(c, parts):
                    slot = c % RING
                    for bank, cols, rows, start, stop in parts:
                        for n, (hi, lo, col) in enumerate(rows):
                            wh, wl = w_hi[:, slot, col:col + cols], w_lo[:, slot, col:col + cols]
                            M.matmul(bank[:, 0:cols], hi, wh, start=start and n == 0, stop=False)
                            M.matmul(bank[:, 0:cols], lo, wh, start=False, stop=False)
                            i = M.matmul(bank[:, 0:cols], hi, wl, start=False, stop=stop and n == len(rows) - 1)
                    return i

                def chunk(c, parts, off=0):
                    pe.wait_ge(sem["lo"], at("lo", l, off * 2 + 2 * (c + 1)))
                    products(c, parts).then_inc(sem["mm"], 1)

                def x_parts(cols, pair, h):
                    return [(acc[:, 2 * pair + t, :], cols,
                             [(xT_hi[:, t, 4 * h + k, :], xT_lo[:, t, 4 * h + k, :], k * cols) for k in range(4)],
                             h == 0, h == 1) for t in range(T)]

                def half_block(c, cols, pair, h, off=0):
                    chunk(c, x_parts(cols, pair, h), off)

                def opening_block(c, cols, k, complete, bank):
                    first, second = x_parts(cols, 0, 0), x_parts(cols, 0, 1)
                    pe.wait_ge(sem["lo"], at("lo", l, 2 * (c + 1)))
                    pe.wait_ge(sem["xT_lo"], at("xT_lo", l, k * T + 1))
                    products(c, first[:1])
                    pe.wait_ge(sem["xT_lo"], at("xT_lo", l, k * T + 2))
                    pe.wait_ge(complete[0], complete[1])
                    half_transposes(x, 1, bank)
                    products(c, first[1:]).then_inc(sem["mm"], 1)
                    pe.wait_ge(sem["lo"], at("lo", l, 2 * (c + 2)))
                    pe.wait_ge(sem["xT_lo"], at("xT_lo", l, (k + 1) * T + 1))
                    products(c + 1, second[:1])
                    pe.wait_ge(sem["xT_lo"], at("xT_lo", l, (k + 1) * T + 2))
                    products(c + 1, second[1:]).then_inc(sem["mm"], 1)

                def b_level(j, q, k):
                    if j:
                        pe.wait_ge(sem["b_at"], at("b_at", l, 2 * j))
                    for n in range(4):
                        c = slice(n * P, (n + 1) * P)
                        for odd in range(2):
                            r = slice(HD * odd, HD * odd + HD)
                            to, keys, queries = wk[:, odd, c], k[r, c], q[r, c]
                            if j:
                                m = 2 ** j // 2
                                to, queries = (a.rearrange("p (n two m) -> p n two m", two=2, m=m)[:, :, 1]
                                               for a in (to, queries))
                            i = M.matmul(to, keys, queries, start=True, stop=True)
                            if n == 3:
                                i.then_inc(sem["b_lev"], 1)

                def qk_rows(branch, h, t, side):
                    base = area["qkT"][0]
                    if branch == BR_C:
                        col = base + 1024 * side + (2 * h + t) * P
                        return arena[0:C_DQ, col:col + P]
                    col = base + (1024 if branch == BR_A else 0) + 512 * side + (h // 2) * SEQ + t * P
                    r = HD * (h % 2)
                    return arena[r:r + HD, col:col + P]

                def scores(u, branch):
                    t = u % 2
                    banks = [wk[:, odd, :].rearrange("p (h k s) -> p h k s", h=2, k=T) for odd in range(2)]
                    two = [P, 2, P]
                    for odd in range(2):
                        pre = []
                        for k in range(t + 1):
                            if branch == BR_D and k == t:
                                pre.append((c_("tri"), X[:, t, odd:H:2, :], k))
                            elif branch == BR_D:
                                pre.append((c_("ones"), X[:, k, odd:H:2, :], k))
                                pre.append((c_("tri"), lf[:, H * t + odd:H * t + H:2][:, :, None].to_broadcast(two), k))
                            name = None
                            if k == t:
                                name = "causal" if branch == BR_D else "chunk"
                            elif branch == BR_A:
                                name = "window"
                            if name:
                                pre.append((m_("ident"), m_(name)[:, None, :].to_broadcast(two), k))
                        for n, (a, b, k) in enumerate(pre):
                            M.matmul(banks[odd][:, :, k, :], a, b, start=n == 0, stop=False)
                    for n in range(2 * (t + 1)):
                        hp, k = n // (t + 1), n % (t + 1)
                        for odd in range(2):
                            h = 2 * hp + odd
                            i = M.matmul(banks[odd][:, hp, k, :], qk_rows(branch, h, t, 0), qk_rows(branch, h, k, 1),
                                         start=False, stop=n == 2 * t + 1)
                    i.then_inc(sem["score"], 1)

                def p_transposes(u):
                    pe.wait_ge(sem["prob"], at("prob", l, u + 1))
                    for k in range(u % 2 + 1):
                        if k == 1 and u:
                            pe.wait_ge(sem["y"], at("y", l, u))
                        transposes(wk[:, 2 + k, :], [prob[:, h, k, :] for h in range(H)], sem["pT"])

                def weighted(u, values):
                    t = u % 2
                    pe.wait_ge(sem["pT_sb"], at("pT_sb", l, PT_DONE[u]))
                    if u:
                        pe.wait_ge(sem["y"], at("y", l, u))
                    for h in range(H):
                        for k in range(t + 1):
                            i = M.matmul(wk[:, 3, h * HD:(h + 1) * HD], pT[:, k, h, :], values(k, h), start=k == 0,
                                         stop=k == t)
                    i.then_inc(sem["pv"], 1)

                def y_transposes(n):
                    transposes(wk[:, 2, :], [y[:, n % 2, t, c * P:(c + 1) * P] for c in range(2) for t in range(T)], sem["yT"])

                def z_first(b):
                    c = 2 * b
                    if b >= 2:
                        pe.wait_ge(sem["z"], at("z", l, 2 * (b - 1)))
                    half_block(c, Z_BLOCKS[b][1], b % 2, 0)

                def z_rest(b):
                    half_block(2 * b + 1, Z_BLOCKS[b][1], b % 2, 1)

                def dv(k, h):
                    return z_dv[:, k, h * HD:(h + 1) * HD]

                def av(k, h):
                    return z_a[:, k, 384 + (h // 2) * HD:384 + (h // 2) * HD + HD]

                def cv(k, h):
                    return c_kv[:, 4 * k + h, HD:2 * HD]

                opening_block(0, Z_BLOCKS[0][1], -1, (sem["xout"], at("xout", l, 0)), 0)
                z_first(1)
                pe.wait_ge(setup, SETUP)
                pe.wait_ge(loaded["const"], 16)
                pe.wait_ge(sem["z"], at("z", l, 2))
                for col in range(2):
                    transposes(wk[:, col, :], [z_qf[:, t, col * BW + hp * P:col * BW + (hp + 1) * P]
                                               for hp in range(2) for t in range(T)], sem["b_in"])
                z_rest(1)
                z_first(2)
                z_rest(2)

                def decayed_level(j):
                    pe.wait_ge(sem["b_QK"], at("b_QK", l, j))
                    b_level(j, bQ, bK)

                def ad_transposes(n, q, k):
                    pe.wait_ge(sem["ad_n"], at("ad_n", l, n + 1))
                    if n:
                        pe.wait_ge(sem["ad_sb"], at("ad_sb", l, 2 * n))
                    for side, a in enumerate((q, k)):
                        transposes(wk[:, 2 + side, :], [a[:, t, c * P:(c + 1) * P] for c in range(2) for t in range(T)], sem["ad_T"])

                pe.wait_ge(sem["b_scan"], at("b_scan", l, 1))
                b_level(0, bq, bk)
                z_first(3)
                decayed_level(1)
                z_rest(3)
                decayed_level(2)
                z_first(4)
                decayed_level(3)
                z_rest(4)
                decayed_level(4)
                z_first(5)
                decayed_level(5)
                ad_transposes(0, z_dqk[:, :, 0:BW], z_dqk[:, :, BW:2 * BW])
                z_rest(5)
                decayed_level(6)

                def gate_first(g):
                    branch, half = g // 2, g % 2
                    if g < 2:
                        pe.wait_ge(sem["z"], at("z", l, 10 + 2 * g))
                    elif g < 4:
                        pe.wait_ge(sem["gate"], at("gate", l, 2 * (g - 1)))
                    else:
                        pe.wait_ge(sem["merge"], at("merge", l, GATE_AFTER[g - 4]))
                    half_block(GATE[branch][half][0], 512, half, 0)

                def gate_rest(g):
                    branch, half = g // 2, g % 2
                    half_block(GATE[branch][half][1], 512, half, 1)

                def project_half(n, second):
                    half, pair = PROJ_HALVES[n][second], PROJ_PAIR[n][second]
                    if second == 0:
                        pe.wait_ge(sem["yT_lo"], at("yT_lo", l, n + 1))
                        pe.wait_ge(sem["lo"], at("lo", l, 2 * (PROJ[n] + 1)))
                    if n == 0:
                        pe.wait_ge(sem["u"], at("u", l, T * (half + 1)))
                    elif n == 1 or n == 2 and second:
                        pe.wait_ge(sem["gate"], at("gate", l, 4 * n + 4 + T * (half + 1)))
                    elif n == 2:
                        pe.wait_ge(sem["merge"], at("merge", l, 8))
                    else:
                        pe.wait_ge(sem["merge"], at("merge", l, 12 + T * second))
                    return products(PROJ[n], [(acc[:, 2 * pair + t, :], 512,
                                               [(yT_hi[:, n % 2, k, t, :], yT_lo[:, n % 2, k, t, :], k * D + half * 512)
                                                for k in range(2)], True, True) for t in range(T)])

                def project(n):
                    project_half(n, 0).then_inc(sem["proj"], 1)
                    project_half(n, 1).then_inc(sem["mm"], 1)

                def b_cross():
                    pe.wait_ge(sem["b_QK"], at("b_QK", l, LEVELS + 1))
                    pe.wait_ge(sem["ad_sb"], at("ad_sb", l, 4))
                    for hp in range(2):
                        col = hp * SEQ
                        for odd in range(2):
                            r = slice(HD * odd, HD * odd + HD)
                            i = M.matmul(wk[:, 2 + odd, hp * P:(hp + 1) * P], bK[r, col:col + P], bQ[r, col + P:col + 2 * P],
                                         start=True, stop=True)
                            if hp:
                                i.then_inc(sem["b_cross"], 1)

                def b_out():
                    pe.wait_ge(sem["b_atx"], at("b_atx", l, 2))
                    pe.wait_ge(sem["b_at"], at("b_at", l, 2 * (LEVELS + 1)))
                    for t in range(T):
                        for h in range(H):
                            o = wk[:, 3, t * BW + h * HD:t * BW + (h + 1) * HD]
                            if t:
                                M.matmul(o, AT[2][:, 2 * (h % 2) + h // 2, :], z_ig[:, 0, h * HD:(h + 1) * HD], start=True, stop=False)
                            i = M.matmul(o, AT[h % 2][:, 2 * (h // 2) + t, :], z_ig[:, t, h * HD:(h + 1) * HD], start=t == 0, stop=True)
                    i.then_inc(sem["b_o"], 1)

                def c_latents():
                    pe.wait_ge(sem["c_n"], at("c_n", l, 1))
                    pe.wait_ge(sem["prob"], at("prob", l, 1))
                    transposes(wk[:, 1, :], [z_c[:, t, c * P:(c + 1) * P] for c in range(2) for t in range(T)], sem["c_T"])
                    transposes(wk[:, 2, :], [z_c[:, t, C_Q:C_Q + C_KV] for t in range(T)], sem["c_T"])

                def first_scores():
                    pe.wait_ge(sem["ad_sb"], at("ad_sb", l, 2))
                    pe.wait_ge(sem["d_x"], at("d_x", l, 1))
                    pe.wait_ge(sem["b_at"], at("b_at", l, 2 * (LEVELS + 1)))
                    scores(0, BR_D)

                def c_transposes():
                    pe.wait_ge(sem["c_n2"], at("c_n2", l, 1))
                    pe.wait_ge(sem["yT_lo"], at("yT_lo", l, 3))
                    for n, (a, h) in enumerate(((c_q, 0), (c_q, 2), (c_k, 0), (c_k, 2))):
                        transposes(wk[:, n, :], [a[:, 4 * t + hh, :] for hh in (h, h + 1) for t in range(T)],
                                   sem["c_T2"])

                gate_first(0)
                decayed_level(7)
                ad_transposes(1, z_a[:, :, 0:BW], kdup)
                gate_rest(0)
                b_cross()
                first_scores()
                gate_first(1)
                b_out()
                c_latents()
                gate_rest(1)
                pe.wait_ge(sem["c_lo"], at("c_lo", l, 1))
                p_transposes(0)
                pe.wait_ge(sem["prob"], at("prob", l, 1))
                scores(1, BR_D)

                gate_first(2)
                pe.wait_ge(sem["b_y"], at("b_y", l, 1))
                weighted(0, dv)
                gate_rest(2)
                p_transposes(1)
                pe.wait_ge(sem["prob"], at("prob", l, 2))
                scores(2, BR_A)

                gate_first(3)
                weighted(1, dv)
                y_transposes(0)
                gate_rest(3)
                pe.wait_ge(sem["yT_lo"], at("yT_lo", l, 1))
                p_transposes(2)
                pe.wait_ge(sem["prob"], at("prob", l, 3))
                scores(3, BR_A)
                pe.wait_ge(sem["y"], at("y", l, 2))
                pe.wait_ge(sem["pT_sb"], at("pT_sb", l, PT_DONE[2]))
                y_transposes(1)
                pe.wait_ge(sem["gate"], at("gate", l, 6))
                chunk(UQ, [(acc[:, t, :], H * C_DQ,
                            [(cT_hi[:, k, t, :], cT_lo[:, k, t, :], k * H * C_DQ) for k in range(2)], True, True)
                           for t in range(T)])
                weighted(2, av)
                pe.wait_ge(sem["gate"], at("gate", l, 8))
                chunk(UKV, [(acc[:, 2 + t, :], 512, [(cT_hi[:, 2, t, :], cT_lo[:, 2, t, :], 0)], True, True)
                            for t in range(T)])
                pe.wait_ge(sem["yT_lo"], at("yT_lo", l, 2))
                p_transposes(3)
                project(0)
                weighted(3, av)
                gate_first(4)
                gate_rest(4)
                pe.wait_ge(sem["y"], at("y", l, 4))
                y_transposes(2)
                gate_first(5)
                c_transposes()
                gate_rest(5)
                pe.wait_ge(sem["c_sb2"], at("c_sb2", l, 4))
                scores(4, BR_C)
                project(1)
                p_transposes(4)
                scores(5, BR_C)
                gate_first(6)
                weighted(4, cv)
                gate_rest(6)
                p_transposes(5)
                project(2)
                weighted(5, cv)
                pe.wait_ge(sem["merge"], at("merge", l, GATE_AFTER[3]))
                pe.wait_ge(sem["lo"], at("lo", l, 2 * (GATE[3][1][0] + 1)))
                products(GATE[3][1][0], x_parts(512, 1, 0)[:1])
                pe.wait_ge(sem["y"], at("y", l, 6))
                y_transposes(3)
                products(GATE[3][1][0], x_parts(512, 1, 0)[1:]).then_inc(sem["mm"], 1)
                project_half(3, 0).then_inc(sem["proj"], 1)
                pe.wait_ge(sem["lo"], at("lo", l, 2 * (GATE[3][1][1] + 1)))
                products(GATE[3][1][1], x_parts(512, 1, 1)).then_inc(sem["last_gate"], 1)
                pe.wait_ge(sem["merge"], at("merge", l, 14))
                half_transposes(merged, 0, 0)
                project_half(3, 1).then_inc(sem["mm"], 2)

                def out_parts(n):
                    h, half = OUT[n]
                    return [(acc[:, 2 * half + t, :], 512,
                             [(mT_hi[:, t, 4 * h + k, :], mT_lo[:, t, 4 * h + k, :], k * 512) for k in range(4)],
                             h == 0, h == 1) for t in range(T)]

                pe.wait_ge(sem["xT_lo"], at("xT_lo", l, 2 * T))
                pe.wait_ge(sem["gate"], at("gate", l, 16))
                chunk(OUT0, out_parts(0))
                pe.wait_ge(sem["merge"], at("merge", l, 16))
                half_transposes(merged, 1, 2)
                chunk(OUT0 + 1, out_parts(1))
                pe.wait_ge(sem["xT_lo"], at("xT_lo", l, 3 * T))
                chunk(OUT0 + 2, out_parts(2))
                pe.wait_ge(sem["lo"], at("lo", l, 2 * (OUT0 + 4)))
                products(OUT0 + 3, out_parts(3)[:1])
                pe.wait_ge(sem["xmid"], at("xmid", l, T))
                half_transposes(x, 0, 0)
                products(OUT0 + 3, out_parts(3)[1:]).then_inc(sem["mm"], 1)

                opening_block(FFN0, 512, 3, (sem["xmid"], at("xmid", l, 2 * T)), 2)

                def act_transposes(b, i):
                    pe.wait_ge(sem["act"], at("act", l, i * 4 + (2 * b + 2)))
                    transposes(wk[:, b % 2, :], [act[:, b % 2, t, c * P:(c + 1) * P] for c in range(2) for t in range(T)], sem["aT"])

                with pe.Fori(0, FFN_BLOCKS // 2) as i:
                    for b in (1, 2):
                        if b == 2:
                            pe.wait_ge(sem["act"], at("act", l, i * 4 + 2))
                        else:
                            pe.wait_ge(sem["act"], at("act", l, i * 4))
                        half_block(FFN0 + 2 * b, 512, b % 2, 0, off=i * 4)
                        half_block(FFN0 + 2 * b + 1, 512, b % 2, 1, off=i * 4)
                        pe.wait_ge(sem["aT_lo"], at("aT_lo", l, i * 2 + (b - 2) if b == 2 else i * 2))
                        act_transposes(b - 1, i)
                for c, (half, n) in enumerate(DOWN, DOWN0):
                    tiles = range(4 * n, min(4 * n + 4, FF_TILES))
                    if c < DOWN_HALF:
                        pe.wait_ge(sem["aT_lo"], at("aT_lo", l, min(2 * n + 2, FFN_BLOCKS)))
                    chunk(c, [(acc[:, 2 * half + t, :], 512,
                               [(aT_hi[:, k * SEQ + t * P:k * SEQ + (t + 1) * P],
                                 aT_lo[:, k * SEQ + t * P:k * SEQ + (t + 1) * P], (k - 4 * n) * 512) for k in tiles],
                               n == 0, n == DOWN_CHUNKS - 1) for t in range(T)])
                    if c == DOWN_HALF + 1:
                        pe.wait_ge(sem["xout"], at("xout", l, T))
                        half_transposes(x, 0, 2)
                    if c == DOWN0:
                        pe.wait_ge(sem["aT_lo"], at("aT_lo", l, FFN_BLOCKS - 2))
                        act_transposes(FFN_BLOCKS - 1, 0)


def stream_layout(w_in, w_branch, w_out, w_ffn_in, w_ffn_out, c_w_uq, c_w_ukv, np):
    out = np.zeros((DEPTH, CHUNKS, P, CW), np.float32)

    def rows(w, first, n):
        return w[first * P:(first + n) * P].reshape(n, P, -1).transpose(1, 0, 2).reshape(P, -1)

    for l in range(DEPTH):
        def put(c, a):
            out[l, c, :, :a.shape[1]] = a

        def halves(first, second, w):
            put(first, rows(w, 0, 4))
            put(second, rows(w, 4, 4))

        for b, (col, n) in enumerate(Z_BLOCKS):
            halves(2 * b, 2 * b + 1, w_in[l][:, col:col + n])
        for n, br in enumerate(MERGE_ORDER):
            for h in range(2):
                col = OFF_G + br * D + h * 512
                halves(*GATE[n][h], w_in[l][:, col:col + 512])
            put(PROJ[n], rows(w_branch[l, br], 0, 2))
        put(UQ, rows(c_w_uq[l], 0, 2))
        put(UKV, rows(c_w_ukv[l], 0, 1))
        for c, (h, half) in enumerate(OUT, OUT0):
            put(c, rows(w_out[l][:, half * 512:half * 512 + 512], 4 * h, 4))
        for b in range(FFN_BLOCKS):
            g = w_ffn_in[l][:, b * 256:b * 256 + 256]
            u = w_ffn_in[l][:, D_FF + b * 256:D_FF + b * 256 + 256]
            halves(FFN0 + 2 * b, FFN0 + 2 * b + 1, np.concatenate([g, u], axis=1))
        for c, (h, n) in enumerate(DOWN, DOWN0):
            put(c, rows(w_ffn_out[l][:, h * 512:h * 512 + 512], 4 * n, min(4, FF_TILES - 4 * n)))
    return out.reshape(DEPTH * CHUNKS, P, CW)


def constants(np):
    i = np.arange(P)
    row, col = i[:, None], i[None, :]
    const = np.zeros((P, CONST_N), np.float32)

    def put(name, a):
        col, n = CONST[name]
        const[:, col:col + n] = a

    put("ident", row == col)
    put("tri", row <= col)
    put("stri", col < row)
    put("ones", 1.0)
    put("half", -0.5)
    half = C_ROPE // 2
    inv = np.exp(np.float32(-np.log(10000.0)) * np.arange(half, dtype=np.float32) / np.float32(half))
    ang = (np.arange(T)[None, :, None] * P + i[:, None, None]).astype(np.float32) * inv.astype(np.float32)
    put("cos", np.concatenate([np.cos(ang), np.cos(ang)], axis=-1).reshape(P, -1))
    put("sin", np.concatenate([-np.sin(ang), np.sin(ang)], axis=-1).reshape(P, -1))
    mask = np.zeros((P, MASK_N), np.float32)
    masks = {"ident": row == col, "causal": np.where(col <= row, 0.0, NEG),
             "chunk": np.where(col // CHUNK <= row // CHUNK, 0.0, NEG),
             "window": np.where((row < CHUNK) & (col >= CHUNK), 0.0, NEG)}
    for name, a in masks.items():
        first, n = MASKS[name]
        mask[:, first:first + n] = a
    level = np.zeros((P, LEVELS * P), np.float32)
    for j in range(LEVELS):
        m = 2 ** j
        level[:, j * P:(j + 1) * P] = (row // (2 * m) == col // (2 * m)) & (row % (2 * m) < m) & (col % (2 * m) >= m)
    return const, mask, level


def parameters(v, np):
    par = np.zeros((P, DEPTH, PAR_IN), np.float32)

    def put(name, l, a):
        col, n = PAR[name]
        par[:, l, col:col + n] = a

    for l in range(DEPTH):
        put("mix", l, v["norm_mix_g"][l].reshape(DK, P).T)
        put("ffn", l, v["norm_ffn_g"][l].reshape(DK, P).T)
        put("cq", l, v["c_cq_norm_g"][l].reshape(2, P).T)
        put("ckv", l, v["c_ckv_norm_g"][l].reshape(1, P).T)
        for name, key in (("aq", "a_q_norm_g"), ("ak", "a_k_norm_g"), ("dq", "d_q_norm_g"), ("dk", "d_k_norm_g")):
            put(name, l, np.concatenate([v[key][l]] * 2)[:, None])
        put("lb", l, v["hgrn_lb_logits"][l].reshape(2, P).T)
        for name, key in (("bo", "b_o_norm_g"), ("cqn", "c_q_norm_g"), ("ckn", "c_k_norm_g"), ("sink", "a_sinks"),
                          ("fb", "d_f_bias")):
            put(name, l, v[key][l][None, :])
    return par


def kernel(**inputs):
    import numpy as np
    import concourse.bacc as bacc
    from concourse.bass_utils import run_bass_kernel_spmd

    v = {k: np.asarray(a) for k, a in inputs.items()}
    const, mask, level = constants(np)
    arrays = {
        "in_x": np.ascontiguousarray(v["x"].reshape(T, P, D).transpose(1, 0, 2)),
        "in_stream": stream_layout(v["w_in"], v["w_branch"], v["w_out"], v["w_ffn_in"], v["w_ffn_out"], v["c_w_uq"],
                                   v["c_w_ukv"], np),
        "in_par": parameters(v, np), "in_const": const, "in_mask": mask, "in_level": level,
    }
    nc = bacc.Bacc("TRN2", target_bir_lowering=False, num_devices=1)
    args = [nc.dram_tensor(n, a.shape, mybir.dt.from_np(a.dtype), kind="ExternalInput").ap() for n, a in arrays.items()]
    out = nc.dram_tensor("out_x", (P, T, D), F32, kind="ExternalOutput").ap()
    trunk(nc, *args, out)
    r = run_bass_kernel_spmd(nc, [arrays], core_ids=[0])
    return r.results[0]["out_x"].transpose(1, 0, 2).reshape(1, SEQ, D)
```
